# Optimizing a Trainium2 kernel written in Bass

```python
import jax, jax.numpy as jnp
from jax import lax
import numpy as np

D_MODEL = 1024
BATCH = 1
SEQ = 1024
DEPTH = 2

CHUNK = 64
QBLOCK = 128
ROPE_THETA = 10000.0
EPS = 1e-6

MLA_HEADS = 8
MLA_Q_LORA = 384
MLA_KV_LORA = 256
MLA_NOPE = 64
MLA_ROPE = 32
MLA_V = 64

DSA_HEADS = 8
DSA_HEAD_DIM = 64
DSA_IDX_HEADS = 4
DSA_IDX_DIM = 64
DSA_TOPK_MAX = 256

SWA_HEADS = 8
SWA_KV_HEADS = 2
SWA_HEAD_DIM = 64
SWA_WINDOW = 128
SWA_WINDOW_CHUNKS = SWA_WINDOW // CHUNK

N_BRANCHES = 3
D_FF = 2048
CONV_WIDTH = 3

IN_SPLITS = (
    MLA_Q_LORA, MLA_KV_LORA, MLA_ROPE,
    DSA_HEADS * DSA_HEAD_DIM, DSA_HEAD_DIM, DSA_HEAD_DIM,
    DSA_IDX_HEADS * DSA_IDX_DIM, DSA_IDX_DIM, DSA_IDX_HEADS,
    SWA_HEADS * SWA_HEAD_DIM, SWA_KV_HEADS * SWA_HEAD_DIM, SWA_KV_HEADS * SWA_HEAD_DIM,
    N_BRANCHES * D_MODEL,
)
IN_WIDTH = sum(IN_SPLITS)

kernel_name = "hybrid_mla_dsa_swa_convffn_encoder"

def rms_norm(x, g):
    xf = x.astype(jnp.float32)
    y = xf * lax.rsqrt(jnp.mean(xf * xf, axis=-1, keepdims=True) + EPS)
    return (y * g.astype(jnp.float32)).astype(x.dtype)

def rope_tables(seq, dim):
    inv = 1.0 / (ROPE_THETA ** (jnp.arange(0, dim, 2, dtype=jnp.float32) / dim))
    ang = jnp.arange(seq, dtype=jnp.float32)[:, None] * inv[None, :]
    return jnp.cos(ang), jnp.sin(ang)

def apply_rope(x, cos, sin):
    d2 = x.shape[-1] // 2
    x1, x2 = x[..., :d2], x[..., d2:]
    c = cos[:, None, :].astype(x.dtype)
    s = sin[:, None, :].astype(x.dtype)
    return jnp.concatenate([x1 * c - x2 * s, x2 * c + x1 * s], axis=-1)

def split_columns(a):
    out, start = [], 0
    for w in IN_SPLITS:
        out.append(a[..., start:start + w])
        start += w
    return out

def to_blocks(a, nb):
    a = a.reshape((a.shape[0], nb, QBLOCK) + a.shape[2:])
    return jnp.moveaxis(a, 1, 0)

def from_blocks(a):
    a = jnp.moveaxis(a, 0, 1)
    return a.reshape((a.shape[0], a.shape[1] * a.shape[2]) + a.shape[3:])

def mla_branch(c_q, c_kv, k_rope, q_norm, w_uq, kv_norm, w_ukv, cos, sin):
    b, s, _ = c_q.shape
    q = (rms_norm(c_q, q_norm) @ w_uq).reshape(b, s, MLA_HEADS, MLA_NOPE + MLA_ROPE)
    q = jnp.concatenate([q[..., :MLA_NOPE], apply_rope(q[..., MLA_NOPE:], cos, sin)], axis=-1)
    kv = (rms_norm(c_kv, kv_norm) @ w_ukv).reshape(b, s, MLA_HEADS, MLA_NOPE + MLA_V)
    k_r = apply_rope(k_rope[:, :, None, :], cos, sin)
    k = jnp.concatenate(
        [kv[..., :MLA_NOPE], jnp.broadcast_to(k_r, (b, s, MLA_HEADS, MLA_ROPE))], axis=-1)
    v = kv[..., MLA_NOPE:]
    scale = (MLA_NOPE + MLA_ROPE) ** -0.5
    nb = s // QBLOCK
    key_chunk = jnp.arange(s) // CHUNK
    q_chunk = key_chunk.reshape(nb, QBLOCK)

    def block(args):
        qb, qc = args
        logits = jnp.einsum('bqhd,bshd->bhqs', qb, k).astype(jnp.float32) * scale
        logits = jnp.where(key_chunk[None, :] <= qc[:, None], logits, -jnp.inf)
        p = jax.nn.softmax(logits, axis=-1).astype(v.dtype)
        return jnp.einsum('bhqs,bshd->bqhd', p, v)

    out = lax.map(block, (to_blocks(q, nb), q_chunk))
    return from_blocks(out).reshape(b, s, MLA_HEADS * MLA_V)

def dsa_branch(q, k, v, qi, ki, wi, cos, sin):
    b, s, _ = q.shape
    q = apply_rope(q.reshape(b, s, DSA_HEADS, DSA_HEAD_DIM), cos, sin)
    k = apply_rope(k[:, :, None, :], cos, sin)[:, :, 0]
    qi = apply_rope(qi.reshape(b, s, DSA_IDX_HEADS, DSA_IDX_DIM), cos, sin)
    ki = apply_rope(ki[:, :, None, :], cos, sin)[:, :, 0]
    wi = wi.astype(jnp.float32) * (DSA_IDX_HEADS ** -0.5 * DSA_IDX_DIM ** -0.5)
    topk = min(DSA_TOPK_MAX, s // 4)
    scale = DSA_HEAD_DIM ** -0.5
    nb = s // QBLOCK
    key_chunk = jnp.arange(s) // CHUNK
    q_chunk = key_chunk.reshape(nb, QBLOCK)
    gather = jax.vmap(lambda a, i: a[i])

    def block(args):
        qb, qib, wib, qc = args
        idx = jnp.einsum('bqhd,bsd->bqhs', qib, ki).astype(jnp.float32)
        idx = jnp.einsum('bqhs,bqh->bqs', jax.nn.relu(idx), wib)
        idx = jnp.where(key_chunk[None, None, :] <= qc[None, :, None], idx, -jnp.inf)
        top_v, top_i = lax.top_k(idx, topk)
        k_sel = gather(k, top_i)
        v_sel = gather(v, top_i)
        logits = jnp.einsum('bqhd,bqkd->bhqk', qb, k_sel).astype(jnp.float32) * scale
        logits = jnp.where(jnp.isfinite(top_v)[:, None], logits, -jnp.inf)
        p = jax.nn.softmax(logits, axis=-1).astype(v_sel.dtype)
        return jnp.einsum('bhqk,bqkd->bqhd', p, v_sel)

    out = lax.map(block, (to_blocks(q, nb), to_blocks(qi, nb), to_blocks(wi, nb), q_chunk))
    return from_blocks(out).reshape(b, s, DSA_HEADS * DSA_HEAD_DIM)

def swa_branch(q, k, v, sinks, cos, sin):
    b, s, _ = q.shape
    nc = s // CHUNK
    g, r, d = SWA_KV_HEADS, SWA_HEADS // SWA_KV_HEADS, SWA_HEAD_DIM
    q = apply_rope(q.reshape(b, s, SWA_HEADS, d), cos, sin).reshape(b, nc, CHUNK, g, r, d)
    k = apply_rope(k.reshape(b, s, g, d), cos, sin).reshape(b, nc, CHUNK, g, d)
    v = v.reshape(b, nc, CHUNK, g, d)

    def band(a):
        pad = jnp.pad(a, ((0, 0), (SWA_WINDOW_CHUNKS - 1, 0), (0, 0), (0, 0), (0, 0)))
        return jnp.concatenate([pad[:, j:j + nc] for j in range(SWA_WINDOW_CHUNKS)], axis=2)

    kw, vw = band(k), band(v)
    logits = jnp.einsum('bncgrd,bnkgd->bngrck', q, kw).astype(jnp.float32) * (d ** -0.5)
    key_pos = (jnp.arange(nc)[:, None] * CHUNK + jnp.arange(SWA_WINDOW_CHUNKS * CHUNK)[None, :]
               - (SWA_WINDOW_CHUNKS - 1) * CHUNK)
    logits = jnp.where((key_pos >= 0)[None, :, None, None, None, :], logits, -jnp.inf)
    sink = sinks.astype(jnp.float32).reshape(1, 1, g, r, 1, 1)
    m = jnp.maximum(jnp.max(logits, axis=-1, keepdims=True), sink)
    p = jnp.exp(logits - m)
    p = p / (jnp.sum(p, axis=-1, keepdims=True) + jnp.exp(sink - m))
    out = jnp.einsum('bngrck,bnkgd->bncgrd', p.astype(vw.dtype), vw)
    return out.reshape(b, s, SWA_HEADS * d)

def conv_ffn(h, w_up, w_gate, conv_w, conv_b, w_down):
    s = h.shape[1]
    u = h @ w_up
    gp = jnp.pad(h @ w_gate, ((0, 0), (CONV_WIDTH - 1, 0), (0, 0)))
    g = conv_b + gp[:, 0:s] * conv_w[0]
    for j in range(1, CONV_WIDTH):
        g = g + gp[:, j:j + s] * conv_w[j]
    return (jax.nn.gelu(g, approximate=False) * u) @ w_down

def setup_inputs(seed: int = 0) -> dict:
    key = jax.random.key(seed)
    ks = jax.random.split(key, 24)
    L, D = DEPTH, D_MODEL

    def w(k, shape, fan_in):
        return jax.random.normal(k, shape, jnp.float32) * (fan_in ** -0.5)

    def gain(k, shape):
        return 1.0 + 0.05 * jax.random.normal(k, shape, jnp.float32)

    return {
        "x": jax.random.normal(ks[0], (BATCH, SEQ, D), jnp.float32),
        "attn_norm": gain(ks[1], (L, D)),
        "w_in": w(ks[2], (L, D, IN_WIDTH), D),
        "b_gate": 0.1 * jax.random.normal(ks[3], (L, N_BRANCHES * D), jnp.float32),
        "mla_q_norm": gain(ks[4], (L, MLA_Q_LORA)),
        "mla_w_uq": w(ks[5], (L, MLA_Q_LORA, MLA_HEADS * (MLA_NOPE + MLA_ROPE)), MLA_Q_LORA),
        "mla_kv_norm": gain(ks[6], (L, MLA_KV_LORA)),
        "mla_w_ukv": w(ks[7], (L, MLA_KV_LORA, MLA_HEADS * (MLA_NOPE + MLA_V)), MLA_KV_LORA),
        "swa_sinks": 0.5 * jax.random.normal(ks[8], (L, SWA_HEADS), jnp.float32),
        "w_branch_mla": w(ks[9], (L, MLA_HEADS * MLA_V, D), MLA_HEADS * MLA_V),
        "w_branch_dsa": w(ks[10], (L, DSA_HEADS * DSA_HEAD_DIM, D), DSA_HEADS * DSA_HEAD_DIM),
        "w_branch_swa": w(ks[11], (L, SWA_HEADS * SWA_HEAD_DIM, D), SWA_HEADS * SWA_HEAD_DIM),
        "w_out": w(ks[12], (L, D, D), D),
        "ffn_norm": gain(ks[13], (L, D)),
        "w_up": w(ks[14], (L, D, D_FF), D),
        "w_gate": w(ks[15], (L, D, D_FF), D),
        "conv_w": w(ks[16], (L, CONV_WIDTH, D_FF), CONV_WIDTH),
        "conv_b": 0.1 * jax.random.normal(ks[17], (L, D_FF), jnp.float32),
        "w_down": w(ks[18], (L, D_FF, D), D_FF),
        "final_norm": gain(ks[19], (D,)),
    }

def reference(x, attn_norm, w_in, b_gate, mla_q_norm, mla_w_uq, mla_kv_norm, mla_w_ukv,
              swa_sinks, w_branch_mla, w_branch_dsa, w_branch_swa, w_out, ffn_norm,
              w_up, w_gate, conv_w, conv_b, w_down, final_norm):
    b, s, _ = x.shape
    cos_r, sin_r = rope_tables(s, MLA_ROPE)
    cos_h, sin_h = rope_tables(s, DSA_HEAD_DIM)
    for l in range(DEPTH):
        h = rms_norm(x, attn_norm[l])
        (c_q, c_kv, k_rope, dq, dk, dv, iq, ik, iw,
         sq, sk, sv, gate_logits) = split_columns(h @ w_in[l])
        y_a = mla_branch(c_q, c_kv, k_rope, mla_q_norm[l], mla_w_uq[l], mla_kv_norm[l],
                         mla_w_ukv[l], cos_r, sin_r) @ w_branch_mla[l]
        y_b = dsa_branch(dq, dk, dv, iq, ik, iw, cos_h, sin_h) @ w_branch_dsa[l]
        y_c = swa_branch(sq, sk, sv, swa_sinks[l], cos_h, sin_h) @ w_branch_swa[l]
        gates = jax.nn.sigmoid((gate_logits + b_gate[l]).astype(jnp.float32))
        gates = gates.astype(x.dtype).reshape(b, s, N_BRANCHES, D_MODEL)
        merged = gates[:, :, 0] * y_a + gates[:, :, 1] * y_b + gates[:, :, 2] * y_c
        x = x + merged @ w_out[l]
        x = x + conv_ffn(rms_norm(x, ffn_norm[l]), w_up[l], w_gate[l], conv_w[l],
                         conv_b[l], w_down[l])
    return rms_norm(x, final_norm)


_drawn_inputs = setup_inputs


def setup_inputs(seed=0):
    import zlib

    import numpy as np

    out = dict(_drawn_inputs(seed))
    spreads = {}
    factors = {'b_gate': 6.681, 'mla_q_norm': 8.0, 'mla_kv_norm': 7.002, 'swa_sinks': 8.0}
    for name, (base, spread) in spreads.items():
        noise = np.random.default_rng([zlib.crc32(name.encode()), seed]).standard_normal(out[name].shape)
        drawn = base * np.exp(spread * noise) if base else spread * noise
        out[name] = __import__('jax').numpy.asarray(drawn.astype(out[name].dtype))
    for name, factor in factors.items():
        out[name] = (out[name] * factor).astype(out[name].dtype)
    return out
```

```python
from contextlib import ExitStack

import concourse.bass as bass
from concourse import mybir
import numpy as np

F32 = mybir.dt.float32
F32R = mybir.dt.float32r
BF16 = mybir.dt.bfloat16
ALU = mybir.AluOpType
ACT = mybir.ActivationFunctionType
AX = mybir.AxisListType

P = 128
D = 1024
T = 1024
HALF = 512
DEPTH = 2
KD = D // P
NB = T // P
CHUNK = 64
FF = 2048
NF = FF // P
FG = 8
GROUPS = NF // FG
HEADS = 8
PAIRS = HEADS // 2
TOPK = 256
ROUNDS = TOPK // 8
CQ, CKV = 3, 2
EPS = 1e-6
MLA_SCALE = 96.0 ** -0.5
HEAD_SCALE = 64.0 ** -0.5
IDX_SCALE = 4.0 ** -0.5 * 64.0 ** -0.5
HIDDEN = -1e30
FUTURE = -2e38
TAKEN = -3e38

IQ, IK, MISC, SQ_, SK, SV, LQ, LKV, DK, DQ, GATE = 0, 2, 3, 4, 8, 9, 10, 13, 15, 16, 20
NPROJ = GATE + 3 * KD
MISC_ROPE, MISC_IW, MISC_V = 0, 32, 64

W_PROJ = 0
W_SWA = W_PROJ + NPROJ
W_MLAP = W_SWA + KD // 2
W_MLA = W_MLAP + 2 * PAIRS
W_DSA = W_MLA + KD // 2
W_OUT = W_DSA + KD // 2
W_FFN = W_OUT + KD
NW = W_FFN + GROUPS * (2 * FG + KD)

D_PROJ = 0
D_SWA = D_PROJ + NPROJ
D_MLAP = D_SWA + KD
D_MLA = D_MLAP + 4 * PAIRS
D_DSA = D_MLA + KD
D_OUT = D_DSA + KD
D_FFN = D_OUT + KD
ND = D_FFN + GROUPS * (2 * FG + KD)
assert NW % 2 == 0 and ND % 2 == 0

S_AN, S_FN, S_BG, S_QN, S_KVN, S_CW, S_CB = 0, 8, 16, 40, 43, 45, 93
NS = S_CB + NF

IDX_BLOCKS = range(TOPK // P, NB)
NIDX = len(IDX_BLOCKS)
SWA, MLA, DSA = 0, 1, 2
GATE_OF = (2, 0, 1)
UNITS = 2 * NB


def boff(b):
    return P * b * (b + 1) // 2


def encoder_kernel(nc, x, wall, smalls, fnorm, sinks, tables, ident_h, masks_h, out):
    proj = nc.dram_tensor("proj_scratch", (NPROJ, P, T), F32).ap()
    xs = nc.dram_tensor("x_scratch", (P, KD, T), F32).ap()

    with ExitStack() as ctx:
        def sem(name):
            return ctx.enter_context(nc.semaphore(name))

        def small(name, shape, dt=F32):
            return ctx.enter_context(nc.sbuf_tensor(name, shape, dt))

        ident = small("ident", [P, P])
        ones = small("ones", [P, P])
        masks_all = small("masks_all", [2, P + 2 * 256 + P], BF16)
        selr, masks = masks_all[:, 0:P], masks_all[:, P:]
        sm = small("sm", [P, NS])
        fn = small("fn", [P, KD])
        sk = small("sk", [1, 2 * HEADS])
        eps = small("eps", [P, 1])
        nmax = small("nmax", [P, 4])
        iw = small("iw", [P, NB, 4])
        m8 = small("m8", [P, NIDX, 8])

        base = (nc.sbuf_base + 63) // 64 * 64

        def put(name, shape, dt, off):
            assert base + off + 4 * int(np.prod(shape[1:])) <= nc.sbuf_usable_end, name
            return nc.alloc_sbuf_tensor_at(name, shape, dt, offset=base + off)

        K = 1024
        TB = 0
        RING = TB + 16448
        RX = RING + 24 * K
        RH = RX + 32 * K
        RG = RH + 64 * K
        RR = RG + 64 * K

        cosT = put("cosT", [P, T], F32, TB)
        sinT = put("sinT", [P, T], F32, TB + 4 * K)
        ropeM = put("ropeM", [P, T], F32, TB + 8 * K)
        mask32 = put("mask32", [2, P + 2 * 256 + P], F32, TB + 12 * K)
        km1 = put("km1", [P, T], F32, TB + 12 * K)
        tt = put("tt", [P, 2, T], F32, TB)
        rt = put("rt", [P, T], F32, TB + 8 * K)
        gpad = put("gpad", [P, T + 2], F32, TB)
        conv = put("conv", [P, T], F32, TB + 4128)
        act = put("act", [P, T], F32, TB + 4128 + 4 * K)
        sqx = put("sqx", [P, 2, T], F32, TB)

        wraw = put("wraw", [P, 2, 1024], F32, RING)
        whi = put("whi", [P, 2, 1024], F32R, RING + 8 * K)
        wlo = put("wlo", [P, 2, 1024], F32R, RING + 16 * K)

        xt = put("xt", [P, KD, T], F32, RX)
        bias = put("bias", [P, boff(NB)], F32, RX)
        qb = put("qb", [P, T], F32, RX + 18 * K)
        kb = put("kb", [P, T], F32, RX + 22 * K)
        tmpo = put("tmpo", [P, T], F32, RX + 26 * K)
        rec = put("rec", [P, HALF], F32, RX + 30 * K)

        hhi = put("hhi", [P, KD, T], F32R, RH)
        hlo = put("hlo", [P, KD, T], F32R, RH + 32 * K)
        mhi = put("mhi", [P, KD, T], F32R, RH)
        mlo = put("mlo", [P, KD, T], F32R, RH + 32 * K)
        chi = put("chi", [P, CQ, T], F32R, RH)
        craw = put("craw", [P, CQ, T], F32, RH + 12 * K)
        clo = put("clo", [P, CQ, T], F32R, RH + 12 * K)
        khi = put("khi", [P, CKV, T], F32R, RH + 24 * K)
        kraw = put("kraw", [P, CKV, T], F32, RH + 32 * K)
        klo = put("klo", [P, CKV, T], F32R, RH + 32 * K)
        qs = put("qs", [P, 2, T], F32, RH)
        msc = put("msc", [P, 2, T], F32, RH + 24 * K)
        v = put("v", [P, NB, 192], F32, RH + 40 * K)
        pr = put("pr", [P, 2, T], F32, RH + 46 * K)
        pw = put("pw", [P, 2, 256], F32, RH + 46 * K)
        vprev = put("vprev", [P, NB, 192], F32, RH + 48 * K)
        gs = put("gs", [P, 2, T], F32, RH + 46 * K)
        pt = put("pt", [P, 2, T], F32, RH + 54 * K)
        rope_t = put("rope_t", [P, T], F32, RH + 54 * K)
        vraw = put("vraw", [P, T], F32, RH + 54 * K)
        csq = put("csq", [P, T], F32, RH + 54 * K)
        csum = put("csum", [P, T], F32, RH + 58 * K)

        stage = put("stage", [P, 2, T], F32, RG)
        iq = put("iq", [P, 3, T], F32, RG + 8 * K)
        iqr = put("iqr", [P, 3, T], F32, RG + 20 * K)
        rel = put("rel", [P, 2, T], F32, RG + 32 * K)
        miscs = put("miscs", [P, T], F32, RG + 40 * K)
        acc = put("acc", [P, KD, T], F32, RG)
        ohi = put("ohi", [P, PAIRS, T], F32R, RG + 32 * K)
        olo = put("olo", [P, PAIRS, T], F32R, RG + 48 * K)
        ahi = put("ahi", [P, FG, T], F32R, RG)
        alo = put("alo", [P, FG, T], F32R, RG + 32 * K)

        xsum = put("xsum", [P, T], F32, RR)
        qm1 = put("qm1", [P, T], F32, RR)
        kr = tmpo

        dps = ctx.enter_context(nc.psum_tensor("dps", [P, 2, T], F32))
        tps = ctx.enter_context(nc.psum_tensor("tps", [P, T], F32))
        ops = ctx.enter_context(nc.psum_tensor("ops", [P, T], F32))
        ips = [tps, ops]

        const_in = sem("const_in")
        const_set = sem("const_set")
        x_in = sem("x_in")
        small_in = sem("small_in")
        x_saved = sem("x_saved")
        table_in = sem("table_in")
        w_in = [sem("w_in0"), sem("w_in1")]
        w_high = sem("w_high")
        w_low = sem("w_low")
        w_used = sem("w_used")
        tile_done = sem("tile_done")
        tile_free = sem("tile_free")
        sum_zero = sem("sum_zero")
        squared = sem("squared")
        summed = sem("summed")
        stat_done = sem("stat_done")
        root_done = sem("root_done")
        rstd_done = sem("rstd_done")
        scaled = sem("scaled")
        norm_high = sem("norm_high")
        norm_low = sem("norm_low")
        stored = [sem("stored0"), sem("stored1")]
        idx_in = sem("idx_in")
        misc_in = sem("misc_in")
        rope_mul = sem("rope_mul")
        idx_rope = sem("idx_rope")
        v_turned = sem("v_turned")
        iw_done = sem("iw_done")
        idx_done = sem("idx_done")
        idx_relu = sem("idx_relu")
        idx_added = sem("idx_added")
        future_set = sem("future_set")
        top_found = sem("top_found")
        top_taken = sem("top_taken")
        bias_done = sem("bias_done")
        k_in = sem("k_in")
        v_in = sem("v_in")
        q_in = sem("q_in")
        k_roped = sem("k_roped")
        v_set = sem("v_set")
        v_done = sem("v_done")
        q_roped = sem("q_roped")
        logits = sem("logits")
        max_done = sem("max_done")
        exp_done = sem("exp_done")
        turned = sem("turned")
        turned_a = sem("turned_a")
        turned_b = sem("turned_b")
        out_half = sem("out_half")
        recip = sem("recip")
        out_norm = sem("out_norm")
        out_high = sem("out_high")
        out_low = sem("out_low")
        gate_in = [sem("gate_in0"), sem("gate_in1")]
        merged = sem("merged")
        sum_high = sem("sum_high")
        sum_low = sem("sum_low")
        lat_in = sem("lat_in")
        lat_zero = sem("lat_zero")
        lat_sq = sem("lat_sq")
        lat_sum = sem("lat_sum")
        lat_stat = sem("lat_stat")
        lat_root = sem("lat_root")
        lat_rstd = sem("lat_rstd")
        lat_scaled = sem("lat_scaled")
        lat_high = sem("lat_high")
        lat_low = sem("lat_low")
        mq_nope = sem("mq_nope")
        mq_mul = sem("mq_mul")
        mq_rope = sem("mq_rope")
        mk_nope = sem("mk_nope")
        kr_mul = sem("kr_mul")
        pad_set = sem("pad_set")
        ffn_gate = sem("ffn_gate")
        ffn_tap = sem("ffn_tap")
        ffn_conv = sem("ffn_conv")
        ffn_gelu = sem("ffn_gelu")
        ffn_high = sem("ffn_high")
        ffn_low = sem("ffn_low")
        out_scaled = sem("out_scaled")
        out_saved = [sem("out_saved0"), sem("out_saved1")]

        def unit_at(L, br, j=0):
            return L * (3 * PAIRS * UNITS) + br * PAIRS * UNITS + j * UNITS

        def pair_at(L, br, j=0):
            return L * (3 * PAIRS) + br * PAIRS + j

        def sink_col(L, j, hd):
            h = j + 4 * hd
            return sk[0:1, bass.ds(2 * h, 2)]

        def half_at(L, br, j=0):
            return L * (3 * PAIRS * 4) + br * PAIRS * 4 + j * 4

        def turned_b_at(L, br, j=0):
            return L * (2 * PAIRS * 8) + (br - 1) * PAIRS * 8 + j * 8

        passed = sem("passed")

        def wait_apart(eng, s, value):
            eng.wait_ge(s, value)
            eng.sem_inc(passed, 1)

        block = ctx.enter_context(nc.Block())

        @block.gpsimd
        def _(pool):
            total = DEPTH * NW

            def split(n, u):
                pool.wait_ge(w_in[u], n * 8 + 16 - 8 * u)
                wait_apart(pool, w_used, n + 1)
                pool.tensor_copy(whi[:, u, :], wraw[:, u, :]).then_inc(w_high, 1)
                pool.wait_ge(w_high, n + 1)
                pool.tensor_tensor(wlo[:, u, :], wraw[:, u, :], whi[:, u, :].bitcast(F32),
                                   ALU.subtract).then_inc(w_low, 1)

            for u in range(2):
                pool.dma_start(wraw[:, u, :], wall[u]).then_inc(w_in[u], 16)
            with pool.Fori(0, total // 2 - 1) as i:
                for u in range(2):
                    split(2 * i + u, u)
                    pool.wait_ge(w_low, 2 * i + u + 1)
                    pool.dma_start(wraw[:, u, :], wall[2 * i + u + 2]).then_inc(w_in[u], 16)
            for u in range(2):
                split(total - 2 + u, u)

        @block.sync
        def _(sp):
            sp.sem_inc(stored[0], 16)
            sp.sem_inc(stored[1], 16)
            for dst, src in ((ident, ident_h), (mask32, masks_h), (fn, fnorm)):
                sp.dma_start(dst[:], src).then_inc(const_in, 16)
            sp.dma_start(xt[:], x).then_inc(x_in, 16)

            def store(L, i, u):
                sp.wait_ge(tile_free, 2 + L * ND + i + 1)
                sp.dma_start(proj[i], stage[:, u, :]).then_inc(stored[u], 16)

            def rotated(dst, src, s):
                for r in range(4):
                    o = r ^ 1
                    sp.dma_start(dst[32 * r:32 * r + 32], src[32 * o:32 * o + 32]).then_inc(s, 16)

            def queries(L, br, j, tile):
                sp.dma_start(qs[:, 0, :], proj[tile + j]).then_inc(q_in, 16)
                rotated(qs[:, 1, :], proj[tile + j], q_in)

            def gates(L, br):
                wait_apart(sp, out_half, half_at(L, br) + 4 * PAIRS)
                with sp.Fori(0, KD // 2) as b:
                    for u in range(2):
                        n = 2 * b + u
                        if br == SWA:
                            sp.wait_ge(tile_free, L * ND + D_SWA + n + 1)
                        else:
                            sp.wait_ge(merged, (2 * L + br - 1) * KD + n + 1)
                        sp.dma_start(gs[:, u, :], proj[GATE + KD * GATE_OF[br] + n]).then_inc(gate_in[u], 16)

            with sp.Fori(0, DEPTH) as L:
                sp.wait_ge(summed, KD + 3 * KD * L)
                sp.dma_start(sm[:], smalls[L]).then_inc(small_in, 16)
                sp.dma_start(sk[:], sinks[L]).then_inc(small_in, 16)
                sp.dma_start(xs, xt[:]).then_inc(x_saved, 16)
                sp.wait_ge(norm_low, 2 * KD * L + KD)
                for n, dst in enumerate((cosT, sinT, ropeM)):
                    sp.dma_start(dst[:], tables[n]).then_inc(table_in, 16)
                for i in range(4):
                    store(L, i, i % 2)
                sp.wait_ge(stored[0], 16 * (NPROJ // 2) * L + 48)
                sp.wait_ge(stored[1], 16 * (NPROJ // 2) * L + 48)
                sp.dma_start(iq[:], proj[0:3].rearrange("t p n -> p t n")).then_inc(idx_in, 16)
                for r in range(4):
                    o = r ^ 1
                    sp.dma_start(iqr[32 * r:32 * r + 32],
                                 proj[0:3, 32 * o:32 * o + 32].rearrange("t p n -> p t n")).then_inc(idx_in, 16)
                sp.dma_start(miscs[:], proj[MISC]).then_inc(misc_in, 16)
                with sp.Fori(2, NPROJ // 2) as b:
                    for u in range(2):
                        store(L, 2 * b + u, u)
                wait_apart(sp, stored[0], 16 * (NPROJ // 2) * (L + 1) + 16)
                wait_apart(sp, stored[1], 16 * (NPROJ // 2) * (L + 1) + 16)
                sp.wait_ge(x_saved, 16 * (L + 1))
                sp.dma_start(kb[:], proj[SK]).then_inc(k_in, 16)
                rotated(tmpo, proj[SK], k_in)
                sp.wait_ge(tile_done, L * ND + NPROJ)
                sp.dma_start(vraw[:], proj[SV]).then_inc(v_in, 16)
                queries(L, SWA, 0, SQ_)
                with sp.Fori(1, PAIRS) as j:
                    sp.wait_ge(q_roped, 2 * PAIRS * L + j)
                    queries(L, SWA, j, SQ_)
                gates(L, SWA)
                sp.wait_ge(out_low, pair_at(L, SWA) + PAIRS + 1)
                sp.dma_start(craw[:], proj[LQ:LQ + CQ].rearrange("t p n -> p t n")).then_inc(lat_in, 16)
                sp.dma_start(kraw[:], proj[LKV:LKV + CKV].rearrange("t p n -> p t n")).then_inc(lat_in, 16)
                sp.dma_start(kr[0:32], proj[MISC, 0:32]).then_inc(lat_in, 16)
                sp.dma_start(kr[32:48], proj[MISC, 16:32]).then_inc(lat_in, 16)
                sp.dma_start(kr[48:64], proj[MISC, 0:16]).then_inc(lat_in, 16)
                gates(L, MLA)
                sp.wait_ge(out_low, pair_at(L, MLA) + PAIRS + 1)
                sp.dma_start(kb[:], proj[DK]).then_inc(k_in, 16)
                rotated(tmpo, proj[DK], k_in)
                sp.dma_start(vraw[:], proj[MISC]).then_inc(v_in, 16)
                queries(L, DSA, 0, DQ)
                with sp.Fori(1, PAIRS) as j:
                    sp.wait_ge(q_roped, 2 * PAIRS * L + PAIRS + j)
                    queries(L, DSA, j, DQ)
                gates(L, DSA)
                sp.wait_ge(out_low, pair_at(L, DSA) + PAIRS + 1)
                sp.dma_start(xt[:], xs).then_inc(x_in, 16)
            with sp.Fori(0, KD // 2) as b:
                for u in range(2):
                    k = 2 * b + u
                    sp.wait_ge(out_scaled, k + 1)
                    sp.dma_start(out[k], stage[:, u, :]).then_inc(out_saved[u], 16)
            sp.wait_ge(out_saved[0], 16 * (KD // 2))
            sp.wait_ge(out_saved[1], 16 * (KD // 2))
            sp.wait_ge(x_saved, 16 * DEPTH)

        @block.tensor
        def _(pe):
            pe.sem_inc(w_used, 1)

            def dense(w, u, wcol, kt, hi, lo, free, slot, ready=None, landed=True):
                if landed:
                    pe.wait_ge(w_low, w + 1)
                pe.wait_ge(tile_free, free)
                first = True
                for k in range(kt):
                    if ready is not None:
                        pe.wait_ge(ready[0], ready[1] + k + 1)
                    wh, wl = whi[:, u, wcol(k)], wlo[:, u, wcol(k)]
                    for a, b in ((wh, hi), (wh, lo), (wl, hi)):
                        for h in range(2):
                            mm = pe.matmul(dps[:, slot, h * HALF:(h + 1) * HALF], a,
                                           b[:, k, h * HALF:(h + 1) * HALF],
                                           start=(k == 0 and a is wh and b is hi),
                                           stop=(k == kt - 1 and a is wl))
                            if landed and first:
                                mm.then_inc(w_used, 1)
                            first = False
                mm.then_inc(tile_done, 1)

            def eighth(k):
                return slice(k * P, (k + 1) * P)

            def statistics(count, src, ps, waited):
                pe.wait_ge(waited[0], waited[1])
                for h in range(2):
                    mm = pe.matmul(ps[:, h * HALF:(h + 1) * HALF], ones[:], src[:, h * HALF:(h + 1) * HALF],
                                   start=True, stop=True)
                mm.then_inc(count, 1)

            def turn_values(src):
                for t in range(NB):
                    mm = pe.transpose(ops[:, t * P:(t + 1) * P], src[:, t * P:(t + 1) * P], ident[:])
                mm.then_inc(v_turned, 1)

            def attention(L, br, j, q_of, k_of):
                u0 = unit_at(L, br, j)

                def qk(n):
                    hd, b = n // NB, n % NB
                    s = dps[:, n % 2, :]
                    q, k = q_of(hd), k_of(hd)
                    qcols = q[:, b * P:(b + 1) * P]
                    if n >= 2:
                        if br == DSA:
                            pe.wait_ge(max_done, u0 + n - 1)
                        else:
                            pe.wait_ge(exp_done, u0 + n - 1)
                    if br == SWA:
                        first = 256 if b == 0 else 0
                        pe.matmul(s[:, 0:256], selr, masks[:, first:first + 256], start=True, stop=False,
                                  skip_group_check=True)
                        col = sink_col(L, j, hd)
                        pe.matmul(s[:, 64:66], ones[0:1, :], col, start=False, stop=False, skip_group_check=True)
                        if b:
                            pe.matmul(s[:, 0:64], qcols, k[:, b * P - 64:b * P], start=False, stop=False,
                                      skip_group_check=True)
                        mm = pe.matmul(s[:, 128:256], qcols, k[:, b * P:(b + 1) * P], start=False, stop=True,
                                       skip_group_check=True)
                    else:
                        nk = (b + 1) * P
                        for c in range(0, nk, HALF):
                            e = min(c + HALF, nk)
                            mm = pe.matmul(s[:, c:e], qcols, k[:, c:e], start=True,
                                           stop=True)
                        if br == MLA:
                            mm = pe.matmul(s[:, nk - P:nk], selr, masks[:, 512:512 + P], start=False, stop=True,
                                           skip_group_check=True)
                    mm.then_inc(logits, 1)

                def turn(n):
                    b = n % NB
                    pe.wait_ge(exp_done, u0 + n + 1)
                    tiles = 2 if br == SWA else b + 1
                    src = pw[:, n % 2, :] if br == SWA else pr[:, n % 2, :]
                    for t in range(tiles):
                        mm = pe.transpose(tps[:, t * P:(t + 1) * P], src[:, t * P:(t + 1) * P], ident[:])
                    mm.then_inc(turned, 1)

                def pv(n):
                    hd, b = n // NB, n % NB
                    pe.wait_ge(turned_a, u0 + n + 1)
                    if br != SWA and b >= 4:
                        pe.wait_ge(turned_b, turned_b_at(L, br, j) + hd * 4 + b - 4 + 1)
                    if b % 4 == 0:
                        pe.wait_ge(out_norm, half_at(L, br, j) + 2 * hd + b // 4 + 1)
                    w = slice(0, P) if hd == 0 else slice(64, 192)
                    o = ops[:, b * P:(b + 1) * P]
                    if br == SWA:
                        pe.matmul(o, vprev[:, b, w], pt[:, n % 2, 0:P], start=True, stop=False)
                        mm = pe.matmul(o, v[:, b, w], pt[:, n % 2, P:2 * P], start=False, stop=True)
                    else:
                        for t in range(b + 1):
                            mm = pe.matmul(o, v[:, t, w], pt[:, n % 2, t * P:(t + 1) * P],
                                           start=(t == 0), stop=(t == b))
                    if b % 4 == 3:
                        mm.then_inc(out_half, 1)

                qk(0)
                qk(1)
                for n in range(UNITS):
                    turn(n)
                    if n + 2 < UNITS:
                        qk(n + 2)
                    pv(n)

            def merge(L, br, w0, d0):
                with pe.Fori(0, KD // 4) as i:
                    for u in range(2):
                        for e in range(2):
                            n = 2 * u + e
                            dense(L * NW + w0 + 2 * i + u, u, lambda k, e=e: slice((e * PAIRS + k) * P, (e * PAIRS + k + 1) * P),
                                  PAIRS, ohi, olo, L * ND + d0 + 4 * i + n + 1, n % 2, landed=(e == 0))

            pe.wait_ge(const_in, 48)
            pe.wait_ge(const_set, 3)
            with pe.Fori(0, DEPTH) as L:
                wb, db = L * NW, L * ND
                statistics(stat_done, xsum, tps, (summed, KD + 3 * KD * L))
                dense(wb, 0, eighth, KD, hhi, hlo, db + 1, 0, ready=(norm_low, 2 * KD * L))
                dense(wb + 1, 1, eighth, KD, hhi, hlo, db + 2, 1)

                def project(lo_, hi_):
                    with pe.Fori(lo_ // 2, hi_ // 2) as i:
                        for u in range(2):
                            dense(wb + 2 * i + u, u, eighth, KD, hhi, hlo, db + 2 * i + u + 1, u)

                project(2, 10)
                pe.wait_ge(misc_in, 16 * (L + 1))
                turn_values(miscs)
                pe.wait_ge(iw_done, L + 1)
                pe.wait_ge(idx_rope, 3 * (L + 1))
                s = 0
                for b in IDX_BLOCKS:
                    for h in range(4):
                        if s >= 2:
                            pe.wait_ge(idx_relu, 4 * NIDX * L + s - 1)
                        r = slice(64 * (h % 2), 64 * (h % 2) + 64)
                        nk = (b + 1) * P
                        for c in range(0, nk, HALF):
                            e = min(c + HALF, nk)
                            mm = pe.matmul(ips[s % 2][:, c:e], iq[r, h // 2, b * P:(b + 1) * P], iq[r, 2, c:e],
                                           start=True, stop=True)
                        mm.then_inc(idx_done, 1)
                        s += 1
                wait_apart(pe, idx_relu, 4 * NIDX * (L + 1))
                project(10, NPROJ)

                pe.wait_ge(tile_free, db + NPROJ + 2)
                pe.wait_ge(v_in, 32 * L + 16)
                turn_values(vraw)
                pe.wait_ge(v_done, 6 * L + 1)
                wait_apart(pe, k_roped, 2 * L + 1)
                halves = (slice(0, 64), slice(64, P))
                with pe.Fori(0, PAIRS) as j:
                    pe.wait_ge(q_roped, 2 * PAIRS * L + j + 1)
                    attention(L, SWA, j, lambda h: qb[halves[h], :], lambda h: kb[halves[h], :])
                wait_apart(pe, out_low, pair_at(L, SWA) + PAIRS + 1)
                merge(L, SWA, W_SWA, D_SWA)

                for i, (src, kt) in enumerate(((csum, CQ), (csum, CKV))):
                    statistics(lat_stat, src, tps, (lat_sum, 5 * L + (CQ if i == 0 else CQ + CKV)))
                wait_apart(pe, lat_low, 5 * (L + 1))
                with pe.Fori(0, PAIRS) as j:
                    w, d = wb + W_MLAP + 2 * j, db + D_MLAP + 4 * j
                    dense(w, 0, lambda k: slice(k * 256, k * 256 + P), CQ, chi, clo, d + 1, 0)
                    dense(w, 0, lambda k: slice(k * 256 + P, k * 256 + 2 * P), CQ, chi, clo, d + 2, 1, landed=False)
                    dense(w + 1, 1, lambda k: slice(k * 256, k * 256 + P), CKV, khi, klo, d + 3, 0)
                    dense(w + 1, 1, lambda k: slice(k * 256 + P, k * 256 + 2 * P), CKV, khi, klo, d + 4, 1, landed=False)
                    pe.wait_ge(tile_free, d + 4 + 2)
                    pe.wait_ge(out_norm, half_at(L, MLA, j) + 2)
                    turn_values(tmpo)
                    pe.wait_ge(v_done, 6 * L + 2 + j)
                    pe.wait_ge(mq_rope, 8 * L + 2 * j + 2)
                    attention(L, MLA, j, lambda h: (qb, qm1)[h][0:96, :], lambda h: (kb, km1)[h][0:96, :])
                wait_apart(pe, out_low, pair_at(L, MLA) + PAIRS + 1)
                merge(L, MLA, W_MLA, D_MLA)

                pe.wait_ge(tile_free, db + D_DSA + 2)
                pe.wait_ge(v_in, 32 * L + 32)
                pe.wait_ge(out_norm, half_at(L, DSA) + 2)
                turn_values(vraw)
                pe.wait_ge(v_done, 6 * L + 6)
                wait_apart(pe, k_roped, 2 * L + 2)
                with pe.Fori(0, PAIRS) as j:
                    pe.wait_ge(q_roped, 2 * PAIRS * L + PAIRS + j + 1)
                    attention(L, DSA, j, lambda h: qb[halves[h], :], lambda h: kb[halves[h], :])
                wait_apart(pe, out_low, pair_at(L, DSA) + PAIRS + 1)
                merge(L, DSA, W_DSA, D_DSA)

                dense(wb + W_OUT, 0, eighth, KD, mhi, mlo, db + D_OUT + 1, 0, ready=(sum_low, KD * L))
                dense(wb + W_OUT + 1, 1, eighth, KD, mhi, mlo, db + D_OUT + 2, 1)
                with pe.Fori(1, KD // 2) as i:
                    for u in range(2):
                        dense(wb + W_OUT + 2 * i + u, u, eighth, KD, mhi, mlo, db + D_OUT + 2 * i + u + 1, u)

                statistics(stat_done, xsum, tps, (summed, KD + 3 * KD * L + KD))
                wait_apart(pe, norm_low, 2 * KD * (L + 1))
                with pe.Fori(0, GROUPS) as g:
                    wg, dg = wb + W_FFN + g * (2 * FG + KD), db + D_FFN + g * (2 * FG + KD)
                    with pe.Fori(0, FG) as f:
                        for u in range(2):
                            dense(wg + 2 * f + u, u, eighth, KD, hhi, hlo, dg + 2 * f + u + 1, u)
                    wg2, dg2 = wg + 2 * FG, dg + 2 * FG
                    wait_apart(pe, ffn_low, NF * L + FG * g + FG + 1)
                    with pe.Fori(0, KD // 2) as i:
                        for u in range(2):
                            dense(wg2 + 2 * i + u, u, eighth, FG, ahi, alo, dg2 + 2 * i + u + 1, u)
            statistics(stat_done, xsum, tps, (summed, KD + 3 * KD * DEPTH))

        @block.scalar
        def _(act_):
            def norm_scale(q, gains):
                act_.wait_ge(stat_done, q + 1)
                act_.activation(rt[:], tps[:], ACT.Sqrt, bias=eps[:, 0:1], scale=1.0 / D).then_inc(root_done, 1)

            def norm(L, q, g0):
                norm_scale(q, None)
                act_.wait_ge(small_in, 32 * (L + 1))
                for k in range(KD):
                    act_.wait_ge(scaled, KD * q + k + 1)
                    act_.activation(hhi[:, k, :], tt[:, k % 2, :], ACT.Copy, scale=sm[:, g0 + k:g0 + k + 1]).then_inc(norm_high, 1)

            def squares(first, k, slot, n):
                act_.activation(sqx[:, slot, :], xt[:, k, :], ACT.Square).then_inc(squared, 1)

            def attention(L, br, j):
                u0 = unit_at(L, br, j)

                def expo(n):
                    b = n % NB
                    act_.wait_ge(max_done, u0 + n + 1)
                    nk = 256 if br == SWA else (b + 1) * P
                    if br == DSA:
                        act_.activation(pr[:, n % 2, 0:nk], msc[:, n % 2, 0:nk], ACT.Exp, bias=nmax[:, n % 4:n % 4 + 1],
                                        scale=-1.0).then_inc(exp_done, 1)
                    else:
                        dst = pw if br == SWA else pr
                        act_.activation(dst[:, n % 2, 0:nk], dps[:, n % 2, 0:nk], ACT.Exp,
                                        bias=nmax[:, n % 4:n % 4 + 1]).then_inc(exp_done, 1)

                expo(0)
                for n in range(UNITS):
                    if n + 1 < UNITS:
                        expo(n + 1)
                    act_.wait_ge(turned, u0 + n + 1)
                    nk = 256 if br == SWA else min((n % NB + 1) * P, HALF)
                    act_.activation(pt[:, n % 2, 0:nk], tps[:, 0:nk], ACT.Copy).then_inc(turned_a, 1)
                act_.wait_ge(out_norm, half_at(L, br, j) + 4 + 2)
                act_.activation(ohi[:, bass.ds(j, 1), :].rearrange("p a n -> p (a n)"), tmpo[:], ACT.Copy).then_inc(out_high, 1)

            act_.wait_ge(const_set, 3)
            act_.wait_ge(x_in, 16)
            for k in range(KD):
                if k >= 2:
                    act_.wait_ge(summed, k - 1)
                squares(None, k, k % 2, k)
            with act_.Fori(0, DEPTH) as L:
                db = L * ND
                norm(L, 2 * L, S_AN)

                def features(lo_, hi_):
                    with act_.Fori(lo_ // 2, hi_ // 2) as i:
                        for u in range(2):
                            act_.wait_ge(tile_done, db + 2 * i + u + 1)
                            act_.wait_ge(stored[u], 16 * (NPROJ // 2) * L + 16 * i + 16)
                            act_.activation(stage[:, u, :], dps[:, u, :], ACT.Copy).then_inc(tile_free, 1)

                features(0, 10)
                for s in range(4 * NIDX):
                    nk = (IDX_BLOCKS[s // 4] + 1) * P
                    act_.wait_ge(idx_done, 4 * NIDX * L + s + 1)
                    if s >= 2:
                        act_.wait_ge(idx_added, 4 * NIDX * L + s - 1)
                    act_.activation(rel[:, s % 2, 0:nk], ips[s % 2][:, 0:nk], ACT.Relu).then_inc(idx_relu, 1)
                features(10, GATE)
                with act_.Fori(0, 3 * KD // 2) as i:
                    for u in range(2):
                        act_.wait_ge(tile_done, db + GATE + 2 * i + u + 1)
                        act_.wait_ge(stored[u], 16 * (NPROJ // 2) * L + 16 * (GATE // 2) + 16 * i + 16)
                        act_.activation(stage[:, u, :], dps[:, u, :], ACT.Sigmoid,
                                        bias=sm[:, bass.ds(S_BG + 2 * i + u, 1)]).then_inc(tile_free, 1)
                with act_.Fori(0, PAIRS) as j:
                    attention(L, SWA, j)
                for c, (raw, hi, kt, g0, k0) in enumerate(((craw, chi, CQ, S_QN, 0), (kraw, khi, CKV, S_KVN, CQ))):
                    if c == 0:
                        act_.wait_ge(lat_in, 80 * (L + 1))
                        act_.wait_ge(tile_done, db + D_MLAP)
                    for k in range(kt):
                        if c or k:
                            act_.wait_ge(lat_sum, 5 * L + k0 + k)
                        act_.activation(csq[:], raw[:, k, :], ACT.Square).then_inc(lat_sq, 1)
                    act_.wait_ge(lat_stat, 2 * L + c + 1)
                    act_.activation(qb[:], tps[:], ACT.Sqrt, bias=eps[:, 0:1], scale=1.0 / (kt * P)).then_inc(lat_root, 1)
                    for k in range(kt):
                        act_.wait_ge(lat_scaled, 5 * L + k0 + k + 1)
                        act_.activation(hi[:, k, :], raw[:, k, :], ACT.Copy, scale=sm[:, g0 + k:g0 + k + 1]).then_inc(lat_high, 1)
                with act_.Fori(0, PAIRS) as j:
                    d = db + D_MLAP + 4 * j
                    for h, q in enumerate((qb, qm1)):
                        act_.wait_ge(tile_done, d + h + 1)
                        act_.activation(q[0:64, :], dps[0:64, h, :], ACT.Copy, scale=MLA_SCALE).then_inc(mq_nope, 1)
                    act_.wait_ge(tile_done, d + 3)
                    act_.activation(kb[0:64, :], dps[0:64, 0, :], ACT.Copy).then_inc(mk_nope, 1)
                    act_.wait_ge(mq_rope, 8 * L + 2 * j + 2)
                    act_.activation(km1[0:64, :], dps[64:128, 0, :], ACT.Copy).then_inc(tile_free, 1)
                    act_.wait_ge(tile_done, d + 4)
                    act_.wait_ge(out_low, pair_at(L, MLA, j) + 1)
                    act_.activation(tmpo[:], dps[:, 1, :], ACT.Copy).then_inc(tile_free, 1)
                    attention(L, MLA, j)
                with act_.Fori(0, PAIRS) as j:
                    attention(L, DSA, j)
                for k in range(KD):
                    act_.wait_ge(merged, 2 + 2 * KD * (L + 1))
                    act_.activation(mhi[:, k, :], acc[:, k, :], ACT.Copy).then_inc(sum_high, 1)

                def residual(free0, sum0):
                    with act_.Fori(0, KD // 2) as i:
                        for u in range(2):
                            n = 2 * i + u
                            act_.wait_ge(tile_free, free0 + n + 1)
                            act_.wait_ge(summed, sum0 + n - 1)
                            act_.activation(sqx[:, u, :], xt[:, bass.ds(n, 1), :].rearrange("p a n -> p (a n)"),
                                            ACT.Square).then_inc(squared, 1)

                residual(db + D_OUT + 2, KD + 3 * KD * L)
                norm(L, 2 * L + 1, S_FN)
                with act_.Fori(0, GROUPS) as g:
                    dg = db + D_FFN + g * (2 * FG + KD)
                    wait_apart(act_, summed, KD + 3 * KD * L + KD + KD * g)
                    with act_.Fori(0, FG) as f:
                        n = NF * L + FG * g + f
                        act_.wait_ge(tile_done, dg + 2 * f + 1)
                        act_.wait_ge(ffn_low, n + 1)
                        act_.activation(gpad[:, 2:T + 2], dps[:, 0, :], ACT.Copy).then_inc(ffn_gate, 1)
                        act_.activation(conv[:], dps[:, 0, :], ACT.Identity,
                                        bias=sm[:, bass.ds(S_CB + FG * g + f, 1)],
                                        scale=sm[:, bass.ds(S_CW + 2 * NF + FG * g + f, 1)]).then_inc(tile_free, 1)
                        act_.wait_ge(ffn_conv, n + 1)
                        act_.activation(act[:], conv[:], ACT.Gelu).then_inc(ffn_gelu, 1)
                        act_.wait_ge(tile_free, 2 + dg + 2 * f + 2)
                        act_.activation(ahi[:, bass.ds(f, 1), :].rearrange("p a n -> p (a n)"), act[:],
                                        ACT.Copy).then_inc(ffn_high, 1)
                    residual(dg + 2 * FG + 2, KD + 3 * KD * L + KD + KD * g)
            norm_scale(2 * DEPTH, None)
            act_.wait_ge(const_in, 48)
            for k in range(KD):
                act_.wait_ge(scaled, KD * 2 * DEPTH + k + 1)
                if k >= 2:
                    act_.wait_ge(out_saved[k % 2], 16 * (k // 2))
                act_.activation(stage[:, k % 2, :], tt[:, k % 2, :], ACT.Copy, scale=fn[:, k:k + 1]).then_inc(out_scaled, 1)

        @block.vector
        def _(dve):
            dve.sem_inc(tile_free, 2)
            dve.sem_inc(out_norm, 2)
            dve.sem_inc(ffn_low, 1)
            dve.sem_inc(merged, 2)
            dve.sem_inc(out_low, 1)
            dve.memset(ones[:], 1.0).then_inc(const_set, 1)
            dve.memset(eps[:], EPS).then_inc(const_set, 1)
            dve.wait_ge(const_in, 48)
            dve.tensor_copy(masks_all[:], mask32[:]).then_inc(const_set, 1)

            def rstd(q):
                dve.wait_ge(root_done, q + 1)
                dve.reciprocal(rt[:], rt[:]).then_inc(rstd_done, 1)
                dve.wait_ge(rstd_done, q + 1)

            def norm(L, q, g0):
                rstd(q)

                def low(k):
                    dve.wait_ge(norm_high, KD * q + k + 1)
                    dve.scalar_tensor_tensor(hlo[:, k, :], tt[:, k % 2, :], sm[:, g0 + k:g0 + k + 1],
                                             hhi[:, k, :].bitcast(F32), ALU.mult, ALU.subtract).then_inc(norm_low, 1)

                dve.wait_ge(small_in, 32 * (L + 1))
                for k in range(KD):
                    if k >= 2:
                        dve.wait_ge(norm_low, KD * q + k - 1)
                    dve.tensor_tensor(tt[:, k % 2, :], xt[:, k, :], rt[:], ALU.mult).then_inc(scaled, 1)
                    if k >= 1:
                        low(k - 1)
                dve.wait_ge(scaled, KD * (q + 1))
                low(KD - 1)

            def add_square(n, slot):
                dve.wait_ge(squared, n + 1)
                if not (isinstance(n, int) and n == 0):
                    dve.wait_ge(summed, n)
                dve.tensor_tensor(xsum[:], xsum[:], sqx[:, slot, :], ALU.add).then_inc(summed, 1)

            def attention(L, br, j):
                u0, h0, t0 = unit_at(L, br, j), half_at(L, br, j), None

                def top(n):
                    b = n % NB
                    (wait_apart(dve, logits, u0 + n + 1) if br == DSA else dve.wait_ge(logits, u0 + n + 1))
                    nk = 256 if br == SWA else (b + 1) * P
                    if br == DSA:
                        if n >= 2:
                            wait_apart(dve, exp_done, u0 + n - 1)
                        dve.tensor_tensor_reduce(out=msc[:, n % 2, 0:nk], in0=dps[:, n % 2, 0:nk],
                                                 in1=bias[:, boff(b):boff(b) + nk], scale=-1.0, scalar=3e38,
                                                 op0=ALU.add, op1=ALU.min,
                                                 accum_out=nmax[:, n % 4:n % 4 + 1]).then_inc(max_done, 1)
                    else:
                        dve.tensor_reduce(nmax[:, n % 4:n % 4 + 1], dps[:, n % 2, 0:nk], AX.X, ALU.max,
                                          negate=True).then_inc(max_done, 1)

                def evacuate(n):
                    b = n % NB
                    if br == SWA or b < 4:
                        return
                    dve.wait_ge(turned, u0 + n + 1)
                    dve.tensor_copy(pt[:, n % 2, HALF:(b + 1) * P], tps[:, HALF:(b + 1) * P]).then_inc(turned_b, 1)

                def normalise(n):
                    hd, b = n // NB, n % NB
                    if b % 4 != 3:
                        return
                    if n == 3:
                        dve.wait_ge(out_low, pair_at(L, br, j) + 1)
                    i = 2 * hd + b // 4
                    c = slice(HALF * (b // 4), HALF * (b // 4) + HALF)
                    o, s = (slice(0, 64), slice(64, P)) if hd == 0 else (slice(64, P), slice(0, 64))
                    dve.wait_ge(out_half, h0 + i + 1)
                    dve.wait_ge(out_norm, h0 + i + 2)
                    dve.reciprocal(rec[o, :], ops[s, c]).then_inc(recip, 1)
                    dve.wait_ge(recip, h0 + i + 1)
                    dve.tensor_tensor(tmpo[o, c], ops[o, c], rec[o, :], ALU.mult).then_inc(out_norm, 1)

                top(0)
                top(1)
                for n in range(UNITS):
                    evacuate(n)
                    if n + 2 < UNITS:
                        top(n + 2)
                    if n >= 1:
                        normalise(n - 1)
                normalise(UNITS - 1)
                pj = pair_at(L, br, j)
                dve.wait_ge(out_high, pj + 1)
                dve.tensor_tensor(olo[:, bass.ds(j, 1), :].rearrange("p a n -> p (a n)"), tmpo[:],
                                  ohi[:, bass.ds(j, 1), :].rearrange("p a n -> p (a n)").bitcast(F32),
                                  ALU.subtract).then_inc(out_low, 1)

            def rope_queries(L, br, j, n):
                dve.wait_ge(q_in, 80 * (n + 1))
                m = rope_at(L, br) + 2 * j
                for t, tab in ((1, sinT), (0, cosT)):
                    dve.scalar_tensor_tensor(qs[:, t, :], qs[:, t, :], HEAD_SCALE, tab[:], ALU.mult,
                                             ALU.mult).then_inc(rope_mul, 1)
                dve.wait_ge(rope_mul, m + 2)
                dve.tensor_tensor(qb[:], qs[:, 0, :], qs[:, 1, :], ALU.add).then_inc(q_roped, 1)

            def rope_at(L, br):
                return L * 26 + 6 + (0 if br == SWA else 10) + 2

            def rope_keys(L, br, n):
                dve.wait_ge(k_in, 80 * (n + 1))
                dve.tensor_tensor(tmpo[:], tmpo[:], sinT[:], ALU.mult).then_inc(rope_mul, 1)
                dve.tensor_tensor(kb[:], kb[:], cosT[:], ALU.mult).then_inc(rope_mul, 1)
                dve.wait_ge(rope_mul, rope_at(L, br))
                dve.tensor_tensor(kb[:], kb[:], tmpo[:], ALU.add).then_inc(k_roped, 1)

            def place_values(ps, a, b, last, n):
                dve.wait_ge(v_turned, last)
                ps8 = ps[:].rearrange("p (t c) -> p t c", c=P)
                dve.tensor_copy(v[:, :, 0:64], ps8[:, :, a:a + 64]).then_inc(v_set, 1)
                dve.wait_ge(v_set, n)
                dve.tensor_copy(v[:, :, 128:192], ps8[:, :, b:b + 64]).then_inc(v_done, 1)

            def merge(L, br, d0):
                with dve.Fori(0, KD // 2) as i:
                    for u in range(2):
                        n = 2 * i + u
                        dve.wait_ge(gate_in[u], 16 * (KD // 2) * (3 * L + br) + 16 * i + 16)
                        dve.wait_ge(tile_done, L * ND + d0 + n + 1)
                        a = acc[:, bass.ds(n, 1), :].rearrange("p a n -> p (a n)")
                        if br == SWA:
                            dve.tensor_tensor(a, dps[:, u, :], gs[:, u, :], ALU.mult).then_inc(tile_free, 1)
                        else:
                            dve.tensor_tensor(gs[:, u, :], dps[:, u, :], gs[:, u, :], ALU.mult).then_inc(tile_free, 1)
                            dve.wait_ge(tile_free, 2 + L * ND + d0 + n + 1)
                            dve.tensor_tensor(a, a, gs[:, u, :], ALU.add).then_inc(merged, 1)

            dve.memset(xsum[:], 0.0).then_inc(sum_zero, 1)
            dve.wait_ge(sum_zero, 1)
            dve.wait_ge(const_set, 3)
            for k in range(KD):
                add_square(k, k % 2)
            with dve.Fori(0, DEPTH) as L:
                db = L * ND
                norm(L, 2 * L, S_AN)
                dve.wait_ge(table_in, 48 * (L + 1))
                dve.wait_ge(idx_in, 80 * (L + 1))
                for t in range(3):
                    dve.tensor_tensor(iqr[:, t, :], iqr[:, t, :], sinT[:], ALU.mult).then_inc(rope_mul, 1)
                    dve.tensor_tensor(iq[:, t, :], iq[:, t, :], cosT[:], ALU.mult).then_inc(rope_mul, 1)
                    dve.wait_ge(rope_mul, L * 26 + 2 * t + 2)
                    dve.tensor_tensor(iq[:, t, :], iq[:, t, :], iqr[:, t, :], ALU.add).then_inc(idx_rope, 1)
                dve.wait_ge(v_turned, 7 * L + 1)
                dve.tensor_scalar(iw[:], ops[:].rearrange("p (t c) -> p t c", c=P)[:, :, MISC_IW:MISC_IW + 4],
                                  IDX_SCALE, None, ALU.mult).then_inc(iw_done, 1)
                dve.wait_ge(iw_done, L + 1)
                dve.wait_ge(x_saved, 16 * (L + 1))
                s = 0
                for n, b in enumerate(IDX_BLOCKS):
                    nk = (b + 1) * P
                    c = bias[:, boff(b):boff(b) + nk]
                    for h in range(4):
                        dve.wait_ge(idx_relu, 4 * NIDX * L + s + 1)
                        if h == 0:
                            dve.tensor_scalar(c, rel[:, s % 2, 0:nk], iw[:, b, h:h + 1], None,
                                              ALU.mult).then_inc(idx_added, 1)
                        else:
                            dve.wait_ge(idx_added, 4 * NIDX * L + s)
                            dve.scalar_tensor_tensor(c, rel[:, s % 2, 0:nk], iw[:, b, h:h + 1], c, ALU.mult,
                                                     ALU.add).then_inc(idx_added, 1)
                        s += 1
                    dve.wait_ge(idx_added, 4 * NIDX * L + s)
                    dve.memset(bias[0:64, boff(b) + nk - CHUNK:boff(b) + nk], FUTURE).then_inc(future_set, 1)
                wait_apart(dve, future_set, NIDX * (L + 1))
                with dve.Fori(0, ROUNDS) as r:
                    for n, b in enumerate(IDX_BLOCKS):
                        dve.max(m8[:, n, :], bias[:, boff(b):boff(b + 1)]).then_inc(top_found, 1)
                    wait_apart(dve, top_found, (ROUNDS * L + r) * NIDX + NIDX)
                    for n, b in enumerate(IDX_BLOCKS):
                        dve.match_replace(bias[:, boff(b):boff(b + 1)], m8[:, n, :], bias[:, boff(b):boff(b + 1)],
                                          TAKEN).then_inc(top_taken, 1)
                    dve.wait_ge(top_taken, (ROUNDS * L + r) * NIDX + NIDX)
                first = boff(IDX_BLOCKS[0])
                dve.tensor_scalar(bias[:, first:boff(NB)], bias[:, first:boff(NB)], TAKEN, HIDDEN, ALU.not_equal,
                                  ALU.mult).then_inc(bias_done, 1)
                dve.memset(bias[:, 0:first], 0.0).then_inc(bias_done, 1)
                dve.wait_ge(bias_done, 4 * L + 2)
                for b in range(IDX_BLOCKS[0]):
                    dve.memset(bias[0:64, boff(b + 1) - CHUNK:boff(b + 1)], HIDDEN).then_inc(bias_done, 1)
                dve.wait_ge(bias_done, 4 * L + 4)

                rope_keys(L, SWA, 2 * L)
                dve.wait_ge(tile_done, db + NPROJ)
                dve.memset(v[:, :, 64:128], 1.0).then_inc(v_set, 1)
                dve.memset(vprev[:], 0.0).then_inc(v_set, 1)
                dve.wait_ge(v_set, 11 * L + 2)
                dve.memset(vprev[:, :, 64:128], 1.0).then_inc(v_set, 1)
                dve.wait_ge(v_turned, 7 * L + 2)
                ps8 = ops[:].rearrange("p (t c) -> p t c", c=P)
                for c0, c1 in ((0, 0), (128, 64)):
                    dve.tensor_copy(vprev[0:64, 1:NB, c0:c0 + 64], ps8[64:128, 0:NB - 1, c1:c1 + 64]).then_inc(v_set, 1)
                dve.wait_ge(v_set, 11 * L + 5)
                place_values(ops, 0, 64, 7 * L + 2, 11 * L + 6)
                with dve.Fori(0, PAIRS) as j:
                    rope_queries(L, SWA, j, 2 * PAIRS * L + j)
                    attention(L, SWA, j)
                merge(L, SWA, D_SWA)

                dve.wait_ge(tile_done, db + D_MLAP)
                for c, (raw, hi, lo, kt, g0, k0) in enumerate(((craw, chi, clo, CQ, S_QN, 0),
                                                               (kraw, khi, klo, CKV, S_KVN, CQ))):
                    if c == 0:
                        dve.wait_ge(tile_free, 2 + db + D_MLAP)
                    dve.memset(csum[:], 0.0).then_inc(lat_zero, 1)
                    dve.wait_ge(lat_zero, 2 * L + c + 1)
                    for k in range(kt):
                        dve.wait_ge(lat_sq, 5 * L + k0 + k + 1)
                        if k0 + k:
                            dve.wait_ge(lat_sum, 5 * L + k0 + k)
                        dve.tensor_tensor(csum[:], csum[:], csq[:], ALU.add).then_inc(lat_sum, 1)
                    dve.wait_ge(lat_root, 2 * L + c + 1)
                    dve.reciprocal(qb[:], qb[:]).then_inc(lat_rstd, 1)
                    dve.wait_ge(lat_rstd, 2 * L + c + 1)
                    for k in range(kt):
                        dve.tensor_tensor(raw[:, k, :], raw[:, k, :], qb[:], ALU.mult).then_inc(lat_scaled, 1)
                    dve.wait_ge(lat_scaled, 5 * L + k0 + kt)
                    for k in range(kt):
                        dve.wait_ge(lat_high, 5 * L + k0 + k + 1)
                        dve.scalar_tensor_tensor(lo[:, k, :], raw[:, k, :], sm[:, g0 + k:g0 + k + 1],
                                                 hi[:, k, :].bitcast(F32), ALU.mult, ALU.subtract).then_inc(lat_low, 1)
                dve.wait_ge(lat_in, 80 * (L + 1))
                dve.tensor_tensor(rope_t[0:32, :], kr[32:64, :], ropeM[32:64, :], ALU.mult).then_inc(kr_mul, 1)
                dve.tensor_tensor(kr[0:32, :], kr[0:32, :], ropeM[0:32, :], ALU.mult).then_inc(kr_mul, 1)
                dve.wait_ge(kr_mul, 4 * L + 2)
                dve.tensor_tensor(kb[64:96, :], kr[0:32, :], rope_t[0:32, :], ALU.add).then_inc(kr_mul, 1)
                dve.tensor_tensor(km1[64:96, :], kr[0:32, :], rope_t[0:32, :], ALU.add).then_inc(kr_mul, 1)
                wait_apart(dve, kr_mul, 4 * L + 4)
                with dve.Fori(0, PAIRS) as j:
                    d = db + D_MLAP + 4 * j
                    for h, q in enumerate((qb, qm1)):
                        n = 8 * L + 2 * j + h
                        dve.wait_ge(tile_done, d + h + 1)
                        dve.wait_ge(mq_nope, n + 1)
                        dve.scalar_tensor_tensor(q[64:96, :], dps[64:96, h, :], MLA_SCALE, ropeM[64:96, :], ALU.mult,
                                                 ALU.mult).then_inc(mq_mul, 1)
                        dve.wait_ge(mq_mul, n + 1)
                        dve.scalar_tensor_tensor(rope_t[64:96, :], dps[96:128, h, :], MLA_SCALE, ropeM[96:128, :],
                                                 ALU.mult, ALU.mult).then_inc(tile_free, 1)
                        dve.wait_ge(tile_free, 2 + d + h + 1)
                        dve.tensor_tensor(q[64:96, :], q[64:96, :], rope_t[64:96, :], ALU.add).then_inc(mq_rope, 1)
                        dve.wait_ge(mq_rope, n + 1)
                    place_values(ops, 0, 64, 7 * L + 3 + j, 11 * L + 7 + j)
                    attention(L, MLA, j)
                merge(L, MLA, D_MLA)

                rope_keys(L, DSA, 2 * L + 1)
                place_values(ops, MISC_V, MISC_V, 7 * L + 7, 11 * L + 11)
                with dve.Fori(0, PAIRS) as j:
                    rope_queries(L, DSA, j, 2 * PAIRS * L + PAIRS + j)
                    attention(L, DSA, j)
                merge(L, DSA, D_DSA)

                for k in range(KD):
                    dve.wait_ge(sum_high, KD * L + k + 1)
                    dve.tensor_tensor(mlo[:, k, :], acc[:, k, :], mhi[:, k, :].bitcast(F32),
                                      ALU.subtract).then_inc(sum_low, 1)

                def residual(d0, n0, z):
                    dve.wait_ge(summed, n0)
                    dve.memset(xsum[:], 0.0).then_inc(sum_zero, 1)
                    wait_apart(dve, sum_zero, z)
                    with dve.Fori(0, KD // 2) as i:
                        for u in range(2):
                            n = 2 * i + u
                            xn = xt[:, bass.ds(n, 1), :].rearrange("p a n -> p (a n)")
                            dve.wait_ge(tile_done, d0 + n + 1)
                            dve.tensor_tensor(xn, xn, dps[:, u, :], ALU.add).then_inc(tile_free, 1)
                            add_square(n0 + n, u)

                dve.wait_ge(x_in, 16 * (L + 2))
                residual(db + D_OUT, KD + 3 * KD * L, 3 * L + 2)
                norm(L, 2 * L + 1, S_FN)
                wait_apart(dve, norm_low, 2 * KD * (L + 1))
                with dve.Fori(0, GROUPS) as g:
                    dg = db + D_FFN + g * (2 * FG + KD)
                    dve.wait_ge(summed, KD + 3 * KD * L + KD + KD * g)
                    dve.memset(gpad[:, 0:2], 0.0).then_inc(pad_set, 1)
                    wait_apart(dve, pad_set, GROUPS * L + g + 1)
                    with dve.Fori(0, FG) as f:
                        n = NF * L + FG * g + f
                        w = S_CW + FG * g + f
                        dve.wait_ge(ffn_gate, n + 1)
                        dve.wait_ge(tile_free, 2 + dg + 2 * f + 1)
                        dve.scalar_tensor_tensor(conv[:], gpad[:, 1:T + 1], sm[:, bass.ds(w + NF, 1)], conv[:], ALU.mult,
                                                 ALU.add).then_inc(ffn_tap, 1)
                        dve.wait_ge(ffn_tap, n + 1)
                        dve.scalar_tensor_tensor(conv[:], gpad[:, 0:T], sm[:, bass.ds(w, 1)], conv[:], ALU.mult,
                                                 ALU.add).then_inc(ffn_conv, 1)
                        dve.wait_ge(ffn_gelu, n + 1)
                        dve.wait_ge(tile_done, dg + 2 * f + 2)
                        dve.tensor_tensor(act[:], act[:], dps[:, 1, :], ALU.mult).then_inc(tile_free, 1)
                        dve.wait_ge(ffn_high, n + 1)
                        dve.tensor_tensor(alo[:, bass.ds(f, 1), :].rearrange("p a n -> p (a n)"), act[:],
                                          ahi[:, bass.ds(f, 1), :].rearrange("p a n -> p (a n)").bitcast(F32),
                                          ALU.subtract).then_inc(ffn_low, 1)
                    residual(dg + 2 * FG, KD + 3 * KD * L + KD + KD * g, 3 * L + 3 + g)
            rstd(2 * DEPTH)
            for k in range(KD):
                if k >= 2:
                    dve.wait_ge(out_scaled, k - 1)
                dve.tensor_tensor(tt[:, k % 2, :], xt[:, k, :], rt[:], ALU.mult).then_inc(scaled, 1)


def _layout(inp):
    f = {k: np.ascontiguousarray(np.asarray(v, dtype=np.float32)) for k, v in inp.items()}
    arange = np.arange
    seg, at = {}, 0
    for name, w in zip(("cq", "ckv", "kr", "dq", "dk", "dv", "iq", "ik", "iw", "sq", "sk", "sv", "g"),
                       (384, 256, 32, 512, 64, 64, 256, 64, 4, 512, 128, 128, 3072)):
        seg[name] = arange(at, at + w)
        at += w
    pad = lambda n: np.full(n, -1)
    twin = lambda c: [np.concatenate([c[j * 64:(j + 1) * 64], c[(j + 4) * 64:(j + 5) * 64]]) for j in range(4)]
    cols = [seg["iq"], seg["ik"], seg["ik"], seg["kr"], seg["iw"], pad(28), seg["dv"], *twin(seg["sq"]), seg["sk"],
            seg["sv"], seg["cq"], seg["ckv"], seg["dk"], seg["dk"], *twin(seg["dq"]), seg["g"]]
    cols = np.concatenate(cols)
    assert cols.size == NPROJ * P
    swap = np.concatenate([arange(80, 96), arange(64, 80)])

    def tiles(w, kt, width):
        n = w.shape[1] // width
        return w.reshape(kt, P, n, width).transpose(2, 1, 0, 3).reshape(n, P, kt * width)

    def padded(t):
        return np.concatenate([t, np.zeros(t.shape[:2] + (1024 - t.shape[2],), np.float32)], axis=2)

    perm = np.concatenate([np.concatenate([arange(j * 64, (j + 1) * 64), arange((j + 4) * 64, (j + 5) * 64)])
                           for j in range(4)])
    wall = []
    for l in range(DEPTH):
        w = np.concatenate([f["w_in"][l], np.zeros((D, 1), np.float32)], axis=1)[:, cols]
        wall.append(tiles(w, KD, P))

        def branch(wb, order):
            t = tiles(wb[order], PAIRS, P)
            return t.reshape(KD // 2, 2, P, PAIRS * P).transpose(0, 2, 1, 3).reshape(KD // 2, P, 1024)

        uq, ukv = f["mla_w_uq"][l], f["mla_w_ukv"][l]
        qcols = np.concatenate([np.concatenate([h * 96 + arange(96), h * 96 + swap]) for h in range(HEADS)])
        tq = tiles(uq[:, qcols], CQ, 2 * P)
        kvcols = np.concatenate([np.concatenate([h * 128 + arange(64) for h in (2 * j, 2 * j + 1)] +
                                                [h * 128 + 64 + arange(64) for h in (2 * j, 2 * j + 1)])
                                 for j in range(PAIRS)])
        tkv = tiles(ukv[:, kvcols], CKV, 2 * P)
        wall.append(branch(f["w_branch_swa"][l], perm))
        wall.append(np.stack([padded(tq), padded(tkv)], axis=1).reshape(2 * PAIRS, P, 1024))
        wall.append(branch(f["w_branch_mla"][l], arange(512)))
        wall.append(branch(f["w_branch_dsa"][l], perm))
        wall.append(tiles(f["w_out"][l], KD, P))
        tg, tu = tiles(f["w_gate"][l], KD, P), tiles(f["w_up"][l], KD, P)
        for g in range(GROUPS):
            s = slice(g * FG, (g + 1) * FG)
            wall.append(np.stack([tg[s], tu[s]], axis=1).reshape(2 * FG, P, 1024))
            wall.append(tiles(f["w_down"][l][g * FG * P:(g + 1) * FG * P], FG, P))
    wall = np.ascontiguousarray(np.concatenate(wall))
    assert wall.shape == (DEPTH * NW, P, 1024)

    col = lambda a: a.reshape(-1, P).T
    smalls = np.stack([np.concatenate([col(f["attn_norm"][l]), col(f["ffn_norm"][l]), col(f["b_gate"][l]),
                                       col(f["mla_q_norm"][l]), col(f["mla_kv_norm"][l]),
                                       *(col(f["conv_w"][l, c]) for c in range(3)), col(f["conv_b"][l])], axis=1)
                       for l in range(DEPTH)])
    assert smalls.shape == (DEPTH, P, NS)
    sinks = np.zeros((DEPTH, 1, HEADS, 2), np.float32)
    sinks[:, 0, :, 0] = f["swa_sinks"][:DEPTH]

    def angles(dim):
        inv = (1.0 / (np.float32(10000.0) ** (arange(0, dim, 2, dtype=np.float32) / np.float32(dim)))).astype(np.float32)
        ang = (arange(T, dtype=np.float32)[:, None] * inv[None, :]).astype(np.float32)
        return np.cos(ang).T.astype(np.float32), np.sin(ang).T.astype(np.float32)

    c, s = angles(64)
    cr, sr = angles(32)
    cosm = np.concatenate([cr, cr])
    sinm = np.concatenate([-sr, sr])
    tables = np.stack([np.tile(c, (4, 1)), np.concatenate([-s, s, -s, s]), np.concatenate([cosm, sinm, cosm, sinm])])

    sel = np.zeros((2, P), np.float32)
    sel[0, :64] = 1
    sel[1, 64:] = 1
    masks = np.zeros((2, 2 * 256 + P), np.float32)
    for first in range(2):
        m = masks[:, 256 * first:256 * first + 256]
        m[:, 65:128] = HIDDEN
        m[0, 192:256] = HIDDEN
        m[1, 0:64] = HIDDEN
        if first:
            m[0, 0:64] = HIDDEN
    masks[0, 512 + 64:512 + 128] = HIDDEN
    return {
        "x": np.ascontiguousarray(f["x"][0].T.reshape(KD, P, T).transpose(1, 0, 2)),
        "wall": wall, "smalls": np.ascontiguousarray(smalls), "fnorm": np.ascontiguousarray(col(f["final_norm"])),
        "sinks": sinks.reshape(DEPTH, 1, 2 * HEADS), "tables": np.ascontiguousarray(tables),
        "ident": np.eye(P, dtype=np.float32), "masks": np.concatenate([sel, masks], axis=1),
    }


def kernel(**inputs):
    import concourse.bacc as bacc
    from concourse.bass_utils import run_bass_kernel_spmd as run

    nc = bacc.Bacc("TRN2", target_bir_lowering=False, num_devices=1)
    arrays, args = {}, []
    for name, a in _layout(inputs).items():
        arrays[f"in_{name}"] = a
        args.append(nc.dram_tensor(f"in_{name}", a.shape, mybir.dt.from_np(a.dtype), kind="ExternalInput").ap())
    args.append(nc.dram_tensor("out_t", (KD, P, T), F32, kind="ExternalOutput").ap())
    encoder_kernel(nc, *args)
    r = run(nc, [arrays], core_ids=[0])
    got = r.results[0]["out_t"]
    return np.ascontiguousarray(np.asarray(got).reshape(D, T).T)[None]
```

```python
from contextlib import ExitStack

import concourse.bass as bass
from concourse import mybir
import numpy as np

F32 = mybir.dt.float32
F32R = mybir.dt.float32r
BF16 = mybir.dt.bfloat16
ALU = mybir.AluOpType
ACT = mybir.ActivationFunctionType
AX = mybir.AxisListType

P = 128
D = 1024
T = 1024
HALF = 512
DEPTH = 2
KD = D // P
NB = T // P
CHUNK = 64
FF = 2048
NF = FF // P
FG = 8
GROUPS = NF // FG
HEADS = 8
PAIRS = HEADS // 2
TOPK = 256
ROUNDS = TOPK // 8
CQ, CKV = 3, 2
EPS = 1e-6
MLA_SCALE = 96.0 ** -0.5
HEAD_SCALE = 64.0 ** -0.5
IDX_SCALE = 4.0 ** -0.5 * 64.0 ** -0.5
HIDDEN = -1e30
FUTURE = -2e38
TAKEN = -3e38

IQ, IK, MISC, SQ_, SK, SV, LQ, LKV, DK, DQ, GATE = 0, 2, 3, 4, 8, 9, 10, 13, 15, 16, 20
NPROJ = GATE + 3 * KD
MISC_ROPE, MISC_IW, MISC_V = 0, 32, 64

W_PROJ = 0
W_SWA = W_PROJ + NPROJ
W_MLAP = W_SWA + KD // 2
W_MLA = W_MLAP + 2 * PAIRS
W_DSA = W_MLA + KD // 2
W_OUT = W_DSA + KD // 2
W_FFN = W_OUT + KD
NW = W_FFN + GROUPS * (2 * FG + KD)

D_PROJ = 0
D_SWA = D_PROJ + NPROJ
D_MLAP = D_SWA + KD
D_MLA = D_MLAP + 4 * PAIRS
D_DSA = D_MLA + KD
D_OUT = D_DSA + KD
D_FFN = D_OUT + KD
ND = D_FFN + GROUPS * (2 * FG + KD)
assert NW % 2 == 0 and ND % 2 == 0

S_AN, S_FN, S_BG, S_QN, S_KVN, S_CW, S_CB = 0, 8, 16, 40, 43, 45, 93
NS = S_CB + NF

IDX_BLOCKS = range(TOPK // P, NB)
NIDX = len(IDX_BLOCKS)
SWA, MLA, DSA = 0, 1, 2
GATE_OF = (2, 0, 1)
PIECES = 2 * NB
TOGETHER = {SWA: ((0, 1, 2, 3), (4, 5, 6, 7)), MLA: ((7,), (6, 0), (5, 1), (4, 2), (3,))}
TOGETHER[DSA] = TOGETHER[MLA]
WINDOW = 256


def boff(b):
    return P * b * (b + 1) // 2


def width(br, blocks):
    return sum(WINDOW if br == SWA else (b + 1) * P for b in blocks)


def encoder_kernel(nc, x, wall, smalls, fnorm, sinks, tables, ident_h, masks_h, out):
    proj = nc.dram_tensor("proj_scratch", (NPROJ, P, T), F32).ap()
    xs = nc.dram_tensor("x_scratch", (P, KD, T), F32).ap()

    with ExitStack() as ctx:
        def sem(name):
            return ctx.enter_context(nc.semaphore(name))

        def small(name, shape, dt=F32):
            return ctx.enter_context(nc.sbuf_tensor(name, shape, dt))

        ident = small("ident", [P, P])
        ones = small("ones", [P, P])
        masks_all = small("masks_all", [2, P + 2 * 256 + P], BF16)
        selr, masks = masks_all[:, 0:P], masks_all[:, P:]
        sm = small("sm", [P, NS])
        fn = small("fn", [P, KD])
        sk = small("sk", [1, 2 * HEADS])
        eps = small("eps", [P, 1])
        nmax = small("nmax", [P, 16])
        psum_row = small("psum_row", [P, 16])
        pinv = small("pinv", [P, 16])
        root = small("root", [P, 2, 2 * NB])
        iw = small("iw", [P, NB, 4])
        m8 = small("m8", [P, NIDX, 8])

        base = (nc.sbuf_base + 63) // 64 * 64

        def put(name, shape, dt, off):
            assert base + off + 4 * int(np.prod(shape[1:])) <= nc.sbuf_usable_end, name
            return nc.alloc_sbuf_tensor_at(name, shape, dt, offset=base + off)

        K = 1024
        TB = 0
        RING = TB + 16448
        RX = RING + 24 * K
        RH = RX + 32 * K
        RG = RH + 64 * K
        RR = RG + 64 * K

        cosT = put("cosT", [P, T], F32, TB)
        sinT = put("sinT", [P, T], F32, TB + 4 * K)
        ropeM = put("ropeM", [P, T], F32, TB + 8 * K)
        mask32 = put("mask32", [2, P + 2 * 256 + P], F32, TB + 12 * K)
        km1 = put("km1", [P, T], F32, TB + 12 * K)
        tt = put("tt", [P, 2, T], F32, TB)
        diag = put("diag", [P, NB, P], F32, TB + 8 * K)
        gpad = put("gpad", [P, T + 2], F32, TB)
        conv = put("conv", [P, T], F32, TB + 4128)
        act = put("act", [P, T], F32, TB + 4128 + 4 * K)
        sqx = put("sqx", [P, 2, T], F32, TB)

        wraw = put("wraw", [P, 2, 1024], F32, RING)
        whi = put("whi", [P, 2, 1024], F32R, RING + 8 * K)
        wlo = put("wlo", [P, 2, 1024], F32R, RING + 16 * K)

        xt = put("xt", [P, KD, T], F32, RX)
        bias = put("bias", [P, boff(NB)], F32, RX)
        qb = put("qb", [P, T], F32, RX + 18 * K)
        kb = put("kb", [P, T], F32, RX + 22 * K)
        tmpo = put("tmpo", [P, T], F32, RX + 26 * K)

        hhi = put("hhi", [P, KD, T], F32R, RH)
        hlo = put("hlo", [P, KD, T], F32R, RH + 32 * K)
        mhi = put("mhi", [P, KD, T], F32R, RH)
        mlo = put("mlo", [P, KD, T], F32R, RH + 32 * K)
        chi = put("chi", [P, CQ, T], F32R, RH)
        craw = put("craw", [P, CQ, T], F32, RH + 12 * K)
        clo = put("clo", [P, CQ, T], F32R, RH + 12 * K)
        khi = put("khi", [P, CKV, T], F32R, RH + 24 * K)
        kraw = put("kraw", [P, CKV, T], F32, RH + 32 * K)
        klo = put("klo", [P, CKV, T], F32R, RH + 32 * K)
        qs = put("qs", [P, 2, T], F32, RH)
        msc = put("msc", [P, 2, T], F32, RH + 24 * K)
        v = put("v", [P, NB, P], F32, RH + 40 * K)
        pr = put("pr", [P, 2, T], F32, RH + 48 * K)
        vprev = put("vprev", [P, NB, P], F32, RH + 24 * K)
        gs = put("gs", [P, 2, T], F32, RH + 48 * K)
        pt = put("pt", [P, 2, T], F32, RH + 56 * K)
        rope_t = put("rope_t", [P, T], F32, RH + 44 * K)
        vraw = put("vraw", [P, T], F32, RH + 56 * K)
        csq = put("csq", [P, T], F32, RH + 28 * K)
        csum = put("csum", [P, T], F32, RH + 8 * K)
        csum2 = put("csum2", [P, T], F32, RH + 24 * K)

        stage = put("stage", [P, 2, T], F32, RG)
        iq = put("iq", [P, 3, T], F32, RG + 8 * K)
        iqr = put("iqr", [P, 3, T], F32, RG + 20 * K)
        rel = put("rel", [P, 2, T], F32, RG + 32 * K)
        miscs = put("miscs", [P, T], F32, RG + 40 * K)
        acc = put("acc", [P, KD, T], F32, RG)
        ohi = put("ohi", [P, PAIRS, T], F32R, RG + 32 * K)
        olo = put("olo", [P, PAIRS, T], F32R, RG + 48 * K)
        ahi = put("ahi", [P, FG, T], F32R, RG)
        alo = put("alo", [P, FG, T], F32R, RG + 32 * K)

        xsum = put("xsum", [P, T], F32, RR)
        qm1 = put("qm1", [P, T], F32, RR)
        lat_diag = (qb, qm1)
        kr = tmpo

        dps = ctx.enter_context(nc.psum_tensor("dps", [P, 2, T], F32))
        tps = ctx.enter_context(nc.psum_tensor("tps", [P, T], F32))
        ops = ctx.enter_context(nc.psum_tensor("ops", [P, T], F32))
        ips = [tps, ops]

        const_in = sem("const_in")
        const_set = sem("const_set")
        x_in = sem("x_in")
        small_in = sem("small_in")
        x_saved = sem("x_saved")
        table_in = sem("table_in")
        w_in = [sem("w_in0"), sem("w_in1")]
        w_high = sem("w_high")
        w_low = sem("w_low")
        w_used = sem("w_used")
        tile_done = sem("tile_done")
        tile_free = sem("tile_free")
        sum_zero = sem("sum_zero")
        squared = sem("squared")
        summed = sem("summed")
        stat_done = sem("stat_done")
        root_done = sem("root_done")
        rstd_done = sem("rstd_done")
        diag_done = sem("diag_done")
        spread = sem("spread")
        scaled = sem("scaled")
        norm_high = sem("norm_high")
        norm_low = sem("norm_low")
        stored = [sem("stored0"), sem("stored1")]
        idx_in = sem("idx_in")
        misc_in = sem("misc_in")
        rope_mul = sem("rope_mul")
        idx_rope = sem("idx_rope")
        v_turned = sem("v_turned")
        iw_done = sem("iw_done")
        idx_done = sem("idx_done")
        idx_relu = sem("idx_relu")
        idx_added = sem("idx_added")
        future_set = sem("future_set")
        top_found = sem("top_found")
        top_taken = sem("top_taken")
        bias_done = sem("bias_done")
        k_in = sem("k_in")
        v_in = sem("v_in")
        q_in = sem("q_in")
        k_roped = sem("k_roped")
        v_set = sem("v_set")
        v_done = sem("v_done")
        q_roped = sem("q_roped")
        logits = sem("logits")
        max_done = sem("max_done")
        exp_done = sem("exp_done")
        turned = sem("turned")
        turned_a = sem("turned_a")
        turned_b = sem("turned_b")
        row_recip = sem("row_recip")
        prob_scaled = sem("prob_scaled")
        out_half = sem("out_half")
        out_high = sem("out_high")
        out_low = sem("out_low")
        gate_in = [sem("gate_in0"), sem("gate_in1")]
        merged = sem("merged")
        sum_high = sem("sum_high")
        sum_low = sem("sum_low")
        lat_in = sem("lat_in")
        lat_first = sem("lat_first")
        lat_sq = sem("lat_sq")
        lat_sum = sem("lat_sum")
        lat_stat = sem("lat_stat")
        lat_root = sem("lat_root")
        lat_rstd = sem("lat_rstd")
        lat_diagonal = sem("lat_diagonal")
        lat_spread = sem("lat_spread")
        lat_scaled = sem("lat_scaled")
        lat_high = sem("lat_high")
        lat_low = sem("lat_low")
        mq_nope = sem("mq_nope")
        mq_mul = sem("mq_mul")
        mq_rope = sem("mq_rope")
        mk_nope = sem("mk_nope")
        kr_mul = sem("kr_mul")
        pad_set = sem("pad_set")
        ffn_gate = sem("ffn_gate")
        ffn_tap = sem("ffn_tap")
        ffn_conv = sem("ffn_conv")
        ffn_gelu = sem("ffn_gelu")
        ffn_high = sem("ffn_high")
        ffn_low = sem("ffn_low")
        out_scaled = sem("out_scaled")
        out_saved = [sem("out_saved0"), sem("out_saved1")]

        def counted(per_pair):
            total = PAIRS * sum(per_pair)

            def at(L, br, j=0):
                return L * total + PAIRS * sum(per_pair[:br]) + j * per_pair[br]
            return at

        unit_at = counted([2 * len(TOGETHER[br]) for br in (SWA, MLA, DSA)])
        wide_at = counted([2 * sum(width(br, u) > HALF for u in TOGETHER[br]) for br in (SWA, MLA, DSA)])
        max_at = counted([2 * len(TOGETHER[SWA]), PIECES, PIECES])
        piece_at = counted([PIECES] * 3)
        half_at = counted([2] * 3)

        def units(br):
            n, piece, out = 0, 0, []
            for hd in range(2):
                for blocks in TOGETHER[br]:
                    col, placed = 0, []
                    for b in blocks:
                        placed.append((b, col))
                        col += WINDOW if br == SWA else (b + 1) * P
                    out.append((n, hd, placed, piece))
                    n, piece = n + 1, piece + len(blocks)
            return out

        def half_order(br):
            return (0, 1) if br == SWA else (1, 0)

        def sink_col(L, j, hd):
            h = j + 4 * hd
            return sk[0:1, bass.ds(2 * h, 2)]

        passed = sem("passed")

        def wait_apart(eng, s, value):
            eng.wait_ge(s, value)
            eng.sem_inc(passed, 1)

        block = ctx.enter_context(nc.Block())

        @block.gpsimd
        def _(pool):
            total = DEPTH * NW

            def split(n, u):
                pool.wait_ge(w_in[u], n * 8 + 16 - 8 * u)
                wait_apart(pool, w_used, n + 1)
                pool.tensor_copy(whi[:, u, :], wraw[:, u, :]).then_inc(w_high, 1)
                pool.wait_ge(w_high, n + 1)
                pool.tensor_tensor(wlo[:, u, :], wraw[:, u, :], whi[:, u, :].bitcast(F32),
                                   ALU.subtract).then_inc(w_low, 1)

            for u in range(2):
                pool.dma_start(wraw[:, u, :], wall[u]).then_inc(w_in[u], 16)
            with pool.Fori(0, total // 2 - 1) as i:
                for u in range(2):
                    split(2 * i + u, u)
                    pool.wait_ge(w_low, 2 * i + u + 1)
                    pool.dma_start(wraw[:, u, :], wall[2 * i + u + 2]).then_inc(w_in[u], 16)
            for u in range(2):
                split(total - 2 + u, u)

        @block.sync
        def _(sp):
            sp.sem_inc(stored[0], 16)
            sp.sem_inc(stored[1], 16)
            for dst, src in ((ident, ident_h), (mask32, masks_h), (fn, fnorm)):
                sp.dma_start(dst[:], src).then_inc(const_in, 16)
            sp.dma_start(xt[:], x).then_inc(x_in, 16)

            def store(L, i, u):
                sp.wait_ge(tile_free, 2 + L * ND + i + 1)
                sp.dma_start(proj[i], stage[:, u, :]).then_inc(stored[u], 16)

            def rotated(dst, src, s):
                for r in range(4):
                    o = r ^ 1
                    sp.dma_start(dst[32 * r:32 * r + 32], src[32 * o:32 * o + 32]).then_inc(s, 16)

            def queries(L, br, j, tile):
                sp.dma_start(qs[:, 0, :], proj[tile + j]).then_inc(q_in, 16)
                rotated(qs[:, 1, :], proj[tile + j], q_in)

            def gates(L, br):
                wait_apart(sp, turned, unit_at(L, br, PAIRS))
                with sp.Fori(0, KD // 2) as b:
                    for u in range(2):
                        n = 2 * b + u
                        if br == SWA:
                            sp.wait_ge(tile_free, L * ND + D_SWA + n + 1)
                        else:
                            sp.wait_ge(merged, (2 * L + br - 1) * KD + n + 1)
                        sp.dma_start(gs[:, u, :], proj[GATE + KD * GATE_OF[br] + n]).then_inc(gate_in[u], 16)

            with sp.Fori(0, DEPTH) as L:
                sp.wait_ge(summed, KD + 3 * KD * L)
                sp.dma_start(sm[:], smalls[L]).then_inc(small_in, 16)
                sp.dma_start(sk[:], sinks[L]).then_inc(small_in, 16)
                sp.dma_start(xs, xt[:]).then_inc(x_saved, 16)
                sp.wait_ge(norm_low, 2 * KD * L + KD)
                for n, dst in enumerate((cosT, sinT, ropeM)):
                    sp.dma_start(dst[:], tables[n]).then_inc(table_in, 16)
                for i in range(4):
                    store(L, i, i % 2)
                sp.wait_ge(stored[0], 16 * (NPROJ // 2) * L + 48)
                sp.wait_ge(stored[1], 16 * (NPROJ // 2) * L + 48)
                sp.dma_start(iq[:], proj[0:3].rearrange("t p n -> p t n")).then_inc(idx_in, 16)
                for r in range(4):
                    o = r ^ 1
                    sp.dma_start(iqr[32 * r:32 * r + 32],
                                 proj[0:3, 32 * o:32 * o + 32].rearrange("t p n -> p t n")).then_inc(idx_in, 16)
                sp.dma_start(miscs[:], proj[MISC]).then_inc(misc_in, 16)
                with sp.Fori(2, NPROJ // 2) as b:
                    for u in range(2):
                        store(L, 2 * b + u, u)
                wait_apart(sp, stored[0], 16 * (NPROJ // 2) * (L + 1) + 16)
                wait_apart(sp, stored[1], 16 * (NPROJ // 2) * (L + 1) + 16)
                sp.wait_ge(x_saved, 16 * (L + 1))
                sp.dma_start(kb[:], proj[SK]).then_inc(k_in, 16)
                rotated(tmpo, proj[SK], k_in)
                sp.wait_ge(tile_done, L * ND + NPROJ)
                sp.dma_start(vraw[:], proj[SV]).then_inc(v_in, 16)
                queries(L, SWA, 0, SQ_)
                sp.dma_start(craw[:], proj[LQ:LQ + CQ].rearrange("t p n -> p t n")).then_inc(lat_in, 16)
                sp.dma_start(kraw[:], proj[LKV:LKV + CKV].rearrange("t p n -> p t n")).then_inc(lat_in, 16)
                sp.wait_ge(k_roped, 2 * L + 1)
                sp.dma_start(kr[0:32], proj[MISC, 0:32]).then_inc(lat_in, 16)
                sp.dma_start(kr[32:48], proj[MISC, 16:32]).then_inc(lat_in, 16)
                sp.dma_start(kr[48:64], proj[MISC, 0:16]).then_inc(lat_in, 16)
                with sp.Fori(1, PAIRS) as j:
                    sp.wait_ge(q_roped, 2 * PAIRS * L + j)
                    queries(L, SWA, j, SQ_)
                gates(L, SWA)
                gates(L, MLA)
                sp.wait_ge(out_low, half_at(L, MLA, PAIRS) + 2)
                sp.dma_start(kb[:], proj[DK]).then_inc(k_in, 16)
                rotated(tmpo, proj[DK], k_in)
                sp.dma_start(vraw[:], proj[MISC]).then_inc(v_in, 16)
                queries(L, DSA, 0, DQ)
                with sp.Fori(1, PAIRS) as j:
                    sp.wait_ge(q_roped, 2 * PAIRS * L + PAIRS + j)
                    queries(L, DSA, j, DQ)
                gates(L, DSA)
                sp.wait_ge(out_low, half_at(L, DSA, PAIRS) + 2)
                sp.dma_start(xt[:], xs).then_inc(x_in, 16)
            with sp.Fori(0, KD // 2) as b:
                for u in range(2):
                    k = 2 * b + u
                    sp.wait_ge(out_scaled, k + 1)
                    sp.dma_start(out[k], stage[:, u, :]).then_inc(out_saved[u], 16)
            sp.wait_ge(out_saved[0], 16 * (KD // 2))
            sp.wait_ge(out_saved[1], 16 * (KD // 2))
            sp.wait_ge(x_saved, 16 * DEPTH)

        @block.tensor
        def _(pe):
            pe.sem_inc(w_used, 1)

            def dense(w, u, wcol, kt, hi, lo, free, slot, ready=None, landed=True):
                if landed:
                    pe.wait_ge(w_low, w + 1)
                pe.wait_ge(tile_free, free)
                first = True
                for k in range(kt):
                    if ready is not None:
                        pe.wait_ge(ready[0], ready[1] + k + 1)
                    wh, wl = whi[:, u, wcol(k)], wlo[:, u, wcol(k)]
                    for a, b in ((wh, hi), (wh, lo), (wl, hi)):
                        for h in range(2):
                            mm = pe.matmul(dps[:, slot, h * HALF:(h + 1) * HALF], a,
                                           b[:, k, h * HALF:(h + 1) * HALF],
                                           start=(k == 0 and a is wh and b is hi),
                                           stop=(k == kt - 1 and a is wl))
                            if landed and first:
                                mm.then_inc(w_used, 1)
                            first = False
                mm.then_inc(tile_done, 1)

            def eighth(k):
                return slice(k * P, (k + 1) * P)

            def dense_pair(w, kt, hi, lo, free, ready):
                pe.wait_ge(tile_free, free + 1)
                for k in range(kt):
                    pe.wait_ge(ready[0], ready[1] + k + 1)
                    for u in range(2):
                        if k == 0:
                            pe.wait_ge(w_low, w + u + 1)
                        wh, wl = whi[:, u, eighth(k)], wlo[:, u, eighth(k)]
                        for a, b in ((wh, hi), (wh, lo), (wl, hi)):
                            for h in range(2):
                                mm = pe.matmul(dps[:, u, h * HALF:(h + 1) * HALF], a, b[:, k, h * HALF:(h + 1) * HALF],
                                               start=(k == 0 and a is wh and b is hi), stop=(k == kt - 1 and a is wl))
                                if k == kt - 1 and u == 1 and h == 0 and a is wh and b is hi:
                                    mm.then_inc(w_used, 1)
                        if k == kt - 1:
                            mm.then_inc(tile_done, 1)

            def statistics(count, src, ps, past_weights=False):
                for t in range(NB):
                    mm = pe.matmul(ps[:, 2 * t:2 * t + 2], src[:, t * P:(t + 1) * P], ones[:, 0:2], start=True, stop=True)
                    if past_weights and t == 0:
                        mm.then_inc(w_used, 1)
                mm.then_inc(count, 1)

            def spread_over_rows(count, src, ps):
                for h in range(2):
                    mm = pe.matmul(ps[:, h * HALF:(h + 1) * HALF], ones[:], src[:, h * HALF:(h + 1) * HALF],
                                   start=True, stop=True)
                mm.then_inc(count, 1)

            def norm(q, sums, past_weights):
                pe.wait_ge(summed, sums)
                statistics(stat_done, xsum, tps, past_weights)
                pe.wait_ge(diag_done, NB * (q + 1))
                spread_over_rows(spread, diag.rearrange("p t c -> p (t c)"), tps)

            def turn_values(src):
                for t in range(NB):
                    mm = pe.transpose(tps[:, t * P:(t + 1) * P], src[:, t * P:(t + 1) * P], ident[:])
                mm.then_inc(v_turned, 1)

            def qk(L, br, j, unit, before=None):
                n, hd, placed, piece = unit
                s = dps[:, n % 2, :]
                halves = (slice(0, 64), slice(64, P))
                q, k = ((qb, qm1)[hd][0:96, :], (kb, km1)[hd][0:96, :]) if br == MLA else (qb[halves[hd], :], kb[halves[hd], :])
                if before is not None:
                    jb, (_, _, placed_b, piece_b) = before
                    if br == DSA:
                        pe.wait_ge(max_done, max_at(L, br, jb) + piece_b + len(placed_b))
                    else:
                        pe.wait_ge(exp_done, piece_at(L, br, jb) + piece_b + len(placed_b))
                for b, o in placed:
                    qcols = q[:, b * P:(b + 1) * P]
                    if br == SWA:
                        first = WINDOW if b == 0 else 0
                        pe.matmul(s[:, o:o + WINDOW], selr, masks[:, first:first + WINDOW], start=True,
                                  stop=False, skip_group_check=True)
                        pe.matmul(s[:, o + 64:o + 66], ones[0:1, :], sink_col(L, j, hd), start=False, stop=False,
                                  skip_group_check=True)
                        if b:
                            pe.matmul(s[:, o:o + 64], qcols, k[:, b * P - 64:b * P], start=False, stop=False,
                                      skip_group_check=True)
                        mm = pe.matmul(s[:, o + P:o + WINDOW], qcols, k[:, b * P:(b + 1) * P], start=False,
                                       stop=True, skip_group_check=True)
                    else:
                        end = o + (b + 1) * P
                        c = o
                        while c < end:
                            e = min((c // HALF + 1) * HALF, end)
                            mm = pe.matmul(s[:, c:e], qcols, k[:, c - o:e - o], start=True, stop=True)
                            c = e
                        if br == MLA:
                            mm = pe.matmul(s[:, end - P:end], selr, masks[:, 512:512 + P], start=False,
                                           stop=True, skip_group_check=True)
                mm.then_inc(logits, 1)

            def mla_tile(L, j, i):
                w, d = L * NW + W_MLAP + 2 * j, L * ND + D_MLAP + 4 * j
                part = lambda k: slice(k * 256 + i % 2 * P, k * 256 + i % 2 * P + P)
                if i < 2:
                    dense(w, 0, part, CQ, chi, clo, d + i + 1, i, landed=(i == 0))
                else:
                    dense(w + 1, 1, part, CKV, khi, klo, d + i + 1, i % 2, landed=(i == 2))

            def mla_start(L, j):
                pe.wait_ge(tile_free, L * ND + D_MLAP + 4 * j + 4 + 2)
                turn_values(tmpo)
                pe.wait_ge(mq_rope, 8 * L + 2 * j + 2)
                for unit in units(MLA)[:2]:
                    qk(L, MLA, j, unit)

            def attention(L, br, j, last):
                work = units(br)
                n0, p0 = unit_at(L, br, j), piece_at(L, br, j)

                def turn(unit):
                    n, hd, placed, piece = unit
                    pe.wait_ge(prob_scaled, p0 + piece + len(placed))
                    for t in range(width(br, [b for b, _ in placed]) // P):
                        mm = pe.transpose(tps[:, t * P:(t + 1) * P], pr[:, n % 2, t * P:(t + 1) * P], ident[:])
                    mm.then_inc(turned, 1)

                def pv(unit):
                    n, hd, placed, piece = unit
                    pe.wait_ge(turned_a, n0 + n + 1)
                    wide = sum(width(br, [b for b, _ in w[2]]) > HALF for w in work[:n + 1])
                    if width(br, [b for b, _ in placed]) > HALF:
                        pe.wait_ge(turned_b, wide_at(L, br, j) + wide)
                    for b, o in placed:
                        half = b // 4
                        if first_use[half] == (n, b):
                            pe.wait_ge(out_low, half_at(L, br, j) + 1 + half_order(br).index(half))
                        vcol = slice(0, 64) if br == DSA else slice(64 * hd, 64 * hd + 64)
                        out_ = ops[64 * hd:64 * hd + 64, b * P:(b + 1) * P]
                        if br == SWA:
                            pe.matmul(out_, vprev[:, b, vcol], pt[:, n % 2, o:o + P], start=True, stop=False)
                            mm = pe.matmul(out_, v[:, b, vcol], pt[:, n % 2, o + P:o + 2 * P], start=False, stop=True)
                        else:
                            for t in range(b + 1):
                                mm = pe.matmul(out_, v[:, t, vcol], pt[:, n % 2, o + t * P:o + (t + 1) * P],
                                               start=(t == 0), stop=(t == b))
                        if last_use[half] == (n, b):
                            mm.then_inc(out_half, 1)

                first_use, last_use = {}, {}
                for n, hd, placed, piece in work:
                    for b, o in placed:
                        first_use.setdefault(b // 4, (n, b))
                        last_use[b // 4] = (n, b)
                assert all(first_use[h][0] < len(work) // 2 for h in first_use)

                if br == MLA:
                    pe.wait_ge(v_done, 6 * L + 2 + j)
                for n, unit in enumerate(work):
                    turn(unit)
                    ahead = n + 2 - len(work)
                    if ahead < 0:
                        qk(L, br, j, work[n + 2], (j, unit))
                    elif not last and br == MLA:
                        mla_tile(L, j + 1, ahead)
                    elif not last:
                        if ahead == 0:
                            pe.wait_ge(q_roped, 2 * PAIRS * L + (PAIRS if br == DSA else 0) + j + 2)
                        qk(L, br, j + 1, work[ahead], (j, unit))
                    pv(unit)
                if not last and br == MLA:
                    mla_tile(L, j + 1, 2)
                    mla_tile(L, j + 1, 3)
                    mla_start(L, j + 1)

            def attentions(L, br):
                with pe.Fori(0, PAIRS - 1) as j:
                    attention(L, br, j, False)
                attention(L, br, PAIRS - 1, True)

            def merge_part(L, br, w0, d0, i):
                for e in range(2):
                    dense(L * NW + w0 + i, i % 2, lambda k, e=e: slice((e * PAIRS + k) * P, (e * PAIRS + k + 1) * P),
                          PAIRS, ohi, olo, L * ND + d0 + 2 * i + e + 1, e, landed=(e == 0))

            def merge(L, br, w0, d0):
                with pe.Fori(0, KD // 4) as i:
                    for u in range(2):
                        for e in range(2):
                            n = 2 * u + e
                            dense(L * NW + w0 + 2 * i + u, u, lambda k, e=e: slice((e * PAIRS + k) * P, (e * PAIRS + k + 1) * P),
                                  PAIRS, ohi, olo, L * ND + d0 + 4 * i + n + 1, n % 2, landed=(e == 0))

            pe.wait_ge(const_in, 48)
            pe.wait_ge(const_set, 3)
            with pe.Fori(0, DEPTH) as L:
                wb, db = L * NW, L * ND
                norm(2 * L, KD + 3 * KD * L, True)
                dense_pair(wb, KD, hhi, hlo, db + 1, (norm_low, 2 * KD * L))

                def project(lo_, hi_):
                    with pe.Fori(lo_ // 2, hi_ // 2) as i:
                        for u in range(2):
                            dense(wb + 2 * i + u, u, eighth, KD, hhi, hlo, db + 2 * i + u + 1, u)

                project(2, 10)
                pe.wait_ge(misc_in, 16 * (L + 1))
                turn_values(miscs)
                pe.wait_ge(iw_done, L + 1)
                pe.wait_ge(idx_rope, 3 * (L + 1))
                s = 0
                for b in IDX_BLOCKS:
                    for h in range(4):
                        if s >= 2:
                            pe.wait_ge(idx_relu, 4 * NIDX * L + s - 1)
                        r = slice(64 * (h % 2), 64 * (h % 2) + 64)
                        nk = (b + 1) * P
                        for c in range(0, nk, HALF):
                            e = min(c + HALF, nk)
                            mm = pe.matmul(ips[s % 2][:, c:e], iq[r, h // 2, b * P:(b + 1) * P], iq[r, 2, c:e],
                                           start=True, stop=True)
                        mm.then_inc(idx_done, 1)
                        s += 1
                wait_apart(pe, idx_relu, 4 * NIDX * (L + 1))
                project(10, NPROJ)

                pe.wait_ge(tile_free, db + NPROJ + 2)
                pe.wait_ge(v_in, 32 * L + 16)
                turn_values(vraw)
                pe.wait_ge(v_done, 6 * L + 1)
                wait_apart(pe, k_roped, 2 * L + 1)
                pe.wait_ge(q_roped, 2 * PAIRS * L + 1)
                for unit in units(SWA)[:2]:
                    qk(L, SWA, 0, unit)
                attentions(L, SWA)
                wait_apart(pe, out_low, half_at(L, SWA, PAIRS) + 2)
                merge_part(L, SWA, W_SWA, D_SWA, 0)
                for c, src in enumerate((csum, csum2)):
                    pe.wait_ge(lat_sum, 3 * L + 2 + c)
                    statistics(lat_stat, src, (tps, ops)[c])
                merge_part(L, SWA, W_SWA, D_SWA, 1)
                for c, src in enumerate(lat_diag):
                    pe.wait_ge(lat_diagonal, 2 * NB * L + NB * (c + 1))
                    spread_over_rows(lat_spread, src, (tps, ops)[c])
                for i in range(2, KD // 2):
                    merge_part(L, SWA, W_SWA, D_SWA, i)
                wait_apart(pe, lat_low, 5 * (L + 1))
                for i in range(4):
                    mla_tile(L, 0, i)
                mla_start(L, 0)
                attentions(L, MLA)
                wait_apart(pe, out_low, half_at(L, MLA, PAIRS) + 2)
                merge(L, MLA, W_MLA, D_MLA)

                pe.wait_ge(tile_free, db + D_DSA + 2)
                pe.wait_ge(v_in, 32 * L + 32)
                turn_values(vraw)
                pe.wait_ge(v_done, 6 * L + 6)
                wait_apart(pe, k_roped, 2 * L + 2)
                pe.wait_ge(q_roped, 2 * PAIRS * L + PAIRS + 1)
                for unit in units(DSA)[:2]:
                    qk(L, DSA, 0, unit)
                attentions(L, DSA)
                wait_apart(pe, out_low, half_at(L, DSA, PAIRS) + 2)
                merge(L, DSA, W_DSA, D_DSA)

                dense(wb + W_OUT, 0, eighth, KD, mhi, mlo, db + D_OUT + 1, 0, ready=(sum_low, KD * L))
                dense(wb + W_OUT + 1, 1, eighth, KD, mhi, mlo, db + D_OUT + 2, 1)
                with pe.Fori(1, KD // 2) as i:
                    for u in range(2):
                        dense(wb + W_OUT + 2 * i + u, u, eighth, KD, mhi, mlo, db + D_OUT + 2 * i + u + 1, u)

                norm(2 * L + 1, KD + 3 * KD * L + KD, True)
                for g in range(GROUPS):
                    wg, dg = wb + W_FFN + g * (2 * FG + KD), db + D_FFN + g * (2 * FG + KD)
                    if g == 0:
                        dense_pair(wg, KD, hhi, hlo, dg + 1, (norm_low, 2 * KD * L + KD))
                    with pe.Fori(1 if g == 0 else 0, FG) as f:
                        for u in range(2):
                            dense(wg + 2 * f + u, u, eighth, KD, hhi, hlo, dg + 2 * f + u + 1, u)
                    wg2, dg2 = wg + 2 * FG, dg + 2 * FG
                    wait_apart(pe, ffn_low, NF * L + FG * g + FG + 1)
                    with pe.Fori(0, KD // 2) as i:
                        for u in range(2):
                            dense(wg2 + 2 * i + u, u, eighth, FG, ahi, alo, dg2 + 2 * i + u + 1, u)
            norm(2 * DEPTH, KD + 3 * KD * DEPTH, False)

        @block.scalar
        def _(act_):
            def norm_root(q):
                act_.wait_ge(stat_done, q + 1)
                act_.activation(root[:, 0, :], tps[:, 0:2 * NB], ACT.Sqrt, bias=eps[:, 0:1], scale=1.0 / D).then_inc(root_done, 1)

            def norm(L, q, g0):
                norm_root(q)
                act_.wait_ge(small_in, 32 * (L + 1))
                for k in range(KD):
                    act_.wait_ge(scaled, KD * q + k + 1)
                    act_.activation(hhi[:, k, :], tt[:, k % 2, :], ACT.Copy, scale=sm[:, g0 + k:g0 + k + 1]).then_inc(norm_high, 1)

            def squares(first, k, slot, n):
                act_.activation(sqx[:, slot, :], xt[:, k, :], ACT.Square).then_inc(squared, 1)

            def expo(L, br, j, unit):
                n, hd, placed, piece = unit
                m0 = max_at(L, br, j)
                for i, (b, o) in enumerate(placed):
                    nk = WINDOW if br == SWA else (b + 1) * P
                    c = 4 * (n % 4) + i
                    if br == DSA:
                        act_.wait_ge(max_done, m0 + piece + i + 1)
                    elif i == 0:
                        act_.wait_ge(max_done, m0 + (n + 1 if br == SWA else piece + len(placed)))
                    src, scale = (msc, -1.0) if br == DSA else (dps, 1.0)
                    act_.activation(pr[:, n % 2, o:o + nk], src[:, n % 2, o:o + nk], ACT.Exp,
                                    bias=nmax[:, c:c + 1], scale=scale,
                                    accum_out=psum_row[:, c:c + 1]).then_inc(exp_done, 1)

            def mla_queries(L, j):
                d = L * ND + D_MLAP + 4 * j
                for h, q in enumerate((qb, qm1)):
                    act_.wait_ge(tile_done, d + h + 1)
                    act_.activation(q[0:64, :], dps[0:64, h, :], ACT.Copy, scale=MLA_SCALE).then_inc(mq_nope, 1)

            def mla_keys(L, j):
                d = L * ND + D_MLAP + 4 * j
                act_.wait_ge(tile_done, d + 3)
                act_.activation(kb[0:64, :], dps[0:64, 0, :], ACT.Copy).then_inc(mk_nope, 1)
                act_.wait_ge(mq_rope, 8 * L + 2 * j + 2)
                act_.activation(km1[0:64, :], dps[64:128, 0, :], ACT.Copy).then_inc(tile_free, 1)
                act_.wait_ge(tile_done, d + 4)
                act_.activation(tmpo[:], dps[:, 1, :], ACT.Copy).then_inc(tile_free, 1)

            def attention(L, br, j, last):
                work = units(br)
                n0 = unit_at(L, br, j)
                for n, unit in enumerate(work):
                    if n + 1 < len(work):
                        expo(L, br, j, work[n + 1])
                    elif not last and br != MLA:
                        expo(L, br, j + 1, work[0])
                    act_.wait_ge(turned, n0 + n + 1)
                    w = min(width(br, [b for b, _ in unit[2]]), HALF)
                    act_.activation(pt[:, n % 2, 0:w], tps[:, 0:w], ACT.Copy).then_inc(turned_a, 1)
                if not last and br == MLA:
                    mla_queries(L, j + 1)
                for i, half in enumerate(half_order(br)):
                    act_.wait_ge(out_half, half_at(L, br, j) + i + 1)
                    c = slice(half * HALF, (half + 1) * HALF)
                    act_.activation(ohi[:, bass.ds(j, 1), c].rearrange("p a n -> p (a n)"), ops[:, c],
                                    ACT.Copy).then_inc(out_high, 1)
                if not last and br == MLA:
                    mla_keys(L, j + 1)
                    expo(L, br, j + 1, work[0])

            def attentions(L, br):
                expo(L, br, 0, units(br)[0])
                with act_.Fori(0, PAIRS - 1) as j:
                    attention(L, br, j, False)
                attention(L, br, PAIRS - 1, True)

            act_.wait_ge(const_set, 3)
            act_.wait_ge(x_in, 16)
            for k in range(KD):
                if k >= 2:
                    act_.wait_ge(summed, k - 1)
                squares(None, k, k % 2, k)
            with act_.Fori(0, DEPTH) as L:
                db = L * ND
                norm(L, 2 * L, S_AN)

                def features(lo_, hi_):
                    with act_.Fori(lo_ // 2, hi_ // 2) as i:
                        for u in range(2):
                            act_.wait_ge(tile_done, db + 2 * i + u + 1)
                            act_.wait_ge(stored[u], 16 * (NPROJ // 2) * L + 16 * i + 16)
                            act_.activation(stage[:, u, :], dps[:, u, :], ACT.Copy).then_inc(tile_free, 1)

                features(0, 10)
                for s in range(4 * NIDX):
                    nk = (IDX_BLOCKS[s // 4] + 1) * P
                    act_.wait_ge(idx_done, 4 * NIDX * L + s + 1)
                    if s >= 2:
                        act_.wait_ge(idx_added, 4 * NIDX * L + s - 1)
                    act_.activation(rel[:, s % 2, 0:nk], ips[s % 2][:, 0:nk], ACT.Relu).then_inc(idx_relu, 1)
                features(10, GATE)
                with act_.Fori(0, 3 * KD // 2) as i:
                    for u in range(2):
                        act_.wait_ge(tile_done, db + GATE + 2 * i + u + 1)
                        act_.wait_ge(stored[u], 16 * (NPROJ // 2) * L + 16 * (GATE // 2) + 16 * i + 16)
                        act_.activation(stage[:, u, :], dps[:, u, :], ACT.Sigmoid,
                                        bias=sm[:, bass.ds(S_BG + 2 * i + u, 1)]).then_inc(tile_free, 1)
                attentions(L, SWA)
                wait_apart(act_, lat_in, 80 * (L + 1))
                wait_apart(act_, out_half, half_at(L, SWA, PAIRS))
                for c, (raw, total, kt, k0) in enumerate(((craw, csum, CQ, 0), (kraw, csum2, CKV, 2))):
                    act_.activation(total[:], raw[:, 0, :], ACT.Square).then_inc(lat_first, 1)
                    for k in range(1, kt):
                        if c or k > 1:
                            act_.wait_ge(lat_sum, 3 * L + c + k - 1 + (1 if c else 0))
                        act_.activation(csq[:], raw[:, k, :], ACT.Square).then_inc(lat_sq, 1)
                for c, kt in enumerate((CQ, CKV)):
                    act_.wait_ge(lat_stat, 2 * L + c + 1)
                    act_.activation(root[:, c, :], (tps, ops)[c][:, 0:2 * NB], ACT.Sqrt, bias=eps[:, 0:1],
                                    scale=1.0 / (kt * P)).then_inc(lat_root, 1)
                for raw, hi, kt, g0, k0 in ((craw, chi, CQ, S_QN, 0), (kraw, khi, CKV, S_KVN, CQ)):
                    for k in range(kt):
                        act_.wait_ge(lat_scaled, 5 * L + k0 + k + 1)
                        act_.activation(hi[:, k, :], raw[:, k, :], ACT.Copy, scale=sm[:, g0 + k:g0 + k + 1]).then_inc(lat_high, 1)
                mla_queries(L, 0)
                mla_keys(L, 0)
                attentions(L, MLA)
                attentions(L, DSA)
                for k in range(KD):
                    act_.wait_ge(merged, 2 + 2 * KD * (L + 1))
                    act_.activation(mhi[:, k, :], acc[:, k, :], ACT.Copy).then_inc(sum_high, 1)

                def residual(free0, sum0):
                    with act_.Fori(0, KD // 2) as i:
                        for u in range(2):
                            n = 2 * i + u
                            act_.wait_ge(tile_free, free0 + n + 1)
                            act_.wait_ge(summed, sum0 + n - 1)
                            act_.activation(sqx[:, u, :], xt[:, bass.ds(n, 1), :].rearrange("p a n -> p (a n)"),
                                            ACT.Square).then_inc(squared, 1)

                residual(db + D_OUT + 2, KD + 3 * KD * L)
                norm(L, 2 * L + 1, S_FN)
                with act_.Fori(0, GROUPS) as g:
                    dg = db + D_FFN + g * (2 * FG + KD)
                    wait_apart(act_, summed, KD + 3 * KD * L + KD + KD * g)
                    with act_.Fori(0, FG) as f:
                        n = NF * L + FG * g + f
                        act_.wait_ge(tile_done, dg + 2 * f + 1)
                        act_.wait_ge(ffn_low, n + 1)
                        act_.activation(gpad[:, 2:T + 2], dps[:, 0, :], ACT.Copy).then_inc(ffn_gate, 1)
                        act_.activation(conv[:], dps[:, 0, :], ACT.Identity,
                                        bias=sm[:, bass.ds(S_CB + FG * g + f, 1)],
                                        scale=sm[:, bass.ds(S_CW + 2 * NF + FG * g + f, 1)]).then_inc(tile_free, 1)
                        act_.wait_ge(ffn_conv, n + 1)
                        act_.activation(act[:], conv[:], ACT.Gelu).then_inc(ffn_gelu, 1)
                        act_.wait_ge(tile_free, 2 + dg + 2 * f + 2)
                        act_.activation(ahi[:, bass.ds(f, 1), :].rearrange("p a n -> p (a n)"), act[:],
                                        ACT.Copy).then_inc(ffn_high, 1)
                    residual(dg + 2 * FG + 2, KD + 3 * KD * L + KD + KD * g)
            norm_root(2 * DEPTH)
            act_.wait_ge(const_in, 48)
            for k in range(KD):
                act_.wait_ge(scaled, KD * 2 * DEPTH + k + 1)
                if k >= 2:
                    act_.wait_ge(out_saved[k % 2], 16 * (k // 2))
                act_.activation(stage[:, k % 2, :], tt[:, k % 2, :], ACT.Copy, scale=fn[:, k:k + 1]).then_inc(out_scaled, 1)

        @block.vector
        def _(dve):
            dve.sem_inc(tile_free, 2)
            dve.sem_inc(ffn_low, 1)
            dve.sem_inc(merged, 2)
            dve.sem_inc(out_low, 2)
            dve.memset(ones[:], 1.0).then_inc(const_set, 1)
            dve.memset(eps[:], EPS).then_inc(const_set, 1)
            dve.wait_ge(const_in, 48)
            dve.tensor_copy(masks_all[:], mask32[:]).then_inc(const_set, 1)

            def diagonal(c, dst, count, ready, done, n):
                dve.wait_ge(ready[0], ready[1])
                dve.reciprocal(root[:, c, :], root[:, c, :]).then_inc(done, 1)
                dve.wait_ge(done, n)
                for t in range(NB):
                    dve.tensor_scalar(dst[:, t * P:(t + 1) * P], ident[:], root[:, c, 2 * t:2 * t + 1], None,
                                      ALU.mult).then_inc(count, 1)

            def rstd(q):
                diagonal(0, diag.rearrange("p t c -> p (t c)"), diag_done, (root_done, q + 1), rstd_done, q + 1)
                dve.wait_ge(spread, q + 1)

            def norm(L, q, g0):
                rstd(q)

                def low(k):
                    dve.wait_ge(norm_high, KD * q + k + 1)
                    dve.scalar_tensor_tensor(hlo[:, k, :], tt[:, k % 2, :], sm[:, g0 + k:g0 + k + 1],
                                             hhi[:, k, :].bitcast(F32), ALU.mult, ALU.subtract).then_inc(norm_low, 1)

                dve.wait_ge(small_in, 32 * (L + 1))
                for k in range(KD):
                    if k >= 2:
                        dve.wait_ge(norm_low, KD * q + k - 1)
                    dve.tensor_tensor(tt[:, k % 2, :], xt[:, k, :], tps[:], ALU.mult).then_inc(scaled, 1)
                    if k >= 1:
                        low(k - 1)
                dve.wait_ge(scaled, KD * (q + 1))
                low(KD - 1)

            def add_square(n, slot):
                dve.wait_ge(squared, n + 1)
                if not (isinstance(n, int) and n == 0):
                    dve.wait_ge(summed, n)
                dve.tensor_tensor(xsum[:], xsum[:], sqx[:, slot, :], ALU.add).then_inc(summed, 1)

            def top(L, br, j, unit, before=None):
                n, hd, placed, piece = unit
                n0 = unit_at(L, br, j)
                c = 4 * (n % 4)
                if br == SWA:
                    dve.wait_ge(logits, n0 + n + 1)
                    dve.tensor_reduce(nmax[:, c:c + 4], dps[:, n % 2, :].rearrange("p (b k) -> p b k", k=WINDOW),
                                      AX.X, ALU.max, negate=True).then_inc(max_done, 1)
                    return
                if br == DSA:
                    wait_apart(dve, logits, n0 + n + 1)
                    if before is not None:
                        wait_apart(dve, exp_done, piece_at(L, br, before[0]) + before[1][3] + len(before[1][2]))
                else:
                    dve.wait_ge(logits, n0 + n + 1)
                for i, (b, o) in enumerate(placed):
                    nk = (b + 1) * P
                    if br == DSA:
                        dve.tensor_tensor_reduce(out=msc[:, n % 2, o:o + nk], in0=dps[:, n % 2, o:o + nk],
                                                 in1=bias[:, boff(b):boff(b) + nk], scale=-1.0, scalar=3e38,
                                                 op0=ALU.add, op1=ALU.min,
                                                 accum_out=nmax[:, c + i:c + i + 1]).then_inc(max_done, 1)
                    else:
                        dve.tensor_reduce(nmax[:, c + i:c + i + 1], dps[:, n % 2, o:o + nk], AX.X, ALU.max,
                                          negate=True).then_inc(max_done, 1)

            def mla_queries(L, j):
                d = L * ND + D_MLAP + 4 * j
                for h, q in enumerate((qb, qm1)):
                    n = 8 * L + 2 * j + h
                    dve.wait_ge(tile_done, d + h + 1)
                    dve.wait_ge(mq_nope, n + 1)
                    dve.scalar_tensor_tensor(q[64:96, :], dps[64:96, h, :], MLA_SCALE, ropeM[64:96, :], ALU.mult,
                                             ALU.mult).then_inc(mq_mul, 1)
                    dve.wait_ge(mq_mul, n + 1)
                    dve.scalar_tensor_tensor(rope_t[64:96, :], dps[96:128, h, :], MLA_SCALE, ropeM[96:128, :],
                                             ALU.mult, ALU.mult).then_inc(tile_free, 1)
                    dve.wait_ge(tile_free, 2 + d + h + 1)
                    dve.tensor_tensor(q[64:96, :], q[64:96, :], rope_t[64:96, :], ALU.add).then_inc(mq_rope, 1)
                    dve.wait_ge(mq_rope, n + 1)

            def divide(L, br, j, unit):
                n, hd, placed, piece = unit
                c = 4 * (n % 4)
                dve.wait_ge(exp_done, piece_at(L, br, j) + piece + len(placed))
                dve.reciprocal(pinv[:, c:c + len(placed)], psum_row[:, c:c + len(placed)]).then_inc(row_recip, 1)
                dve.wait_ge(row_recip, unit_at(L, br, j) + n + 1)
                for i, (b, o) in enumerate(placed):
                    nk = WINDOW if br == SWA else (b + 1) * P
                    dve.tensor_scalar(pr[:, n % 2, o:o + nk], pr[:, n % 2, o:o + nk], pinv[:, c + i:c + i + 1],
                                      None, ALU.mult).then_inc(prob_scaled, 1)

            def attention(L, br, j, last):
                work = units(br)
                n0 = unit_at(L, br, j)
                number = 2 * PAIRS * L + (PAIRS if br == DSA else 0) + j + 1

                def evacuate(unit):
                    n, hd, placed, piece = unit
                    w = width(br, [b for b, _ in placed])
                    if w > HALF:
                        dve.wait_ge(turned, n0 + n + 1)
                        dve.tensor_copy(pt[:, n % 2, HALF:w], tps[:, HALF:w]).then_inc(turned_b, 1)

                def low(i):
                    half = half_order(br)[i]
                    dve.wait_ge(out_high, half_at(L, br, j) + i + 1)
                    c = slice(half * HALF, (half + 1) * HALF)
                    hi = ohi[:, bass.ds(j, 1), c].rearrange("p a n -> p (a n)").bitcast(F32)
                    dve.tensor_tensor(olo[:, bass.ds(j, 1), c].rearrange("p a n -> p (a n)"), ops[:, c], hi,
                                      ALU.subtract).then_inc(out_low, 1)

                end = len(work)
                for n, unit in enumerate(work):
                    if n:
                        divide(L, br, j, unit)
                    if n + 1 < end:
                        top(L, br, j, work[n + 1], (j, work[n - 1]) if n else None)
                    elif not last and br != MLA:
                        top(L, br, j + 1, work[0], (j, work[n - 1]))
                    if not last and br != MLA and n == end - 2:
                        add_rotated()
                    evacuate(unit)
                    if not last and br != MLA and n == end - 3:
                        rotate_queries(L, br, j + 1, number)
                if not last and br == MLA:
                    mla_queries(L, j + 1)
                low(0)
                if not last and br != MLA:
                    divide(L, br, j + 1, work[0])
                low(1)
                if not last and br == MLA:
                    place_values(0, P, 7 * L + 3 + j + 1)
                    top(L, br, j + 1, work[0])
                    divide(L, br, j + 1, work[0])

            def attentions(L, br):
                top(L, br, 0, units(br)[0])
                divide(L, br, 0, units(br)[0])
                with dve.Fori(0, PAIRS - 1) as j:
                    attention(L, br, j, False)
                attention(L, br, PAIRS - 1, True)

            def rotate_queries(L, br, j, n):
                dve.wait_ge(q_in, 80 * (n + 1))
                for t, tab in ((1, sinT), (0, cosT)):
                    dve.scalar_tensor_tensor(qs[:, t, :], qs[:, t, :], HEAD_SCALE, tab[:], ALU.mult,
                                             ALU.mult).then_inc(rope_mul, 1)
                dve.wait_ge(rope_mul, rope_at(L, br) + 2 * j + 2)

            def add_rotated():
                dve.tensor_tensor(qb[:], qs[:, 0, :], qs[:, 1, :], ALU.add).then_inc(q_roped, 1)

            def rope_at(L, br):
                return L * 26 + 6 + (0 if br == SWA else 10) + 2

            def rope_keys(L, br, n):
                dve.wait_ge(k_in, 80 * (n + 1))
                dve.tensor_tensor(tmpo[:], tmpo[:], sinT[:], ALU.mult).then_inc(rope_mul, 1)
                dve.tensor_tensor(kb[:], kb[:], cosT[:], ALU.mult).then_inc(rope_mul, 1)
                dve.wait_ge(rope_mul, rope_at(L, br))
                dve.tensor_tensor(kb[:], kb[:], tmpo[:], ALU.add).then_inc(k_roped, 1)

            def place_values(col, cols, turned_):
                dve.wait_ge(v_turned, turned_)
                ps8 = tps[:].rearrange("p (t c) -> p t c", c=P)
                dve.tensor_copy(v[:, :, 0:cols], ps8[:, :, col:col + cols]).then_inc(v_done, 1)

            def merge_swa(L, n):
                u = n % 2
                dve.wait_ge(gate_in[u], 16 * (KD // 2) * (3 * L + SWA) + 16 * (n // 2) + 16)
                dve.wait_ge(tile_done, L * ND + D_SWA + n + 1)
                dve.tensor_tensor(acc[:, n, :], dps[:, u, :], gs[:, u, :], ALU.mult).then_inc(tile_free, 1)

            def merge(L, br, d0):
                with dve.Fori(0, KD // 2) as i:
                    for u in range(2):
                        n = 2 * i + u
                        dve.wait_ge(gate_in[u], 16 * (KD // 2) * (3 * L + br) + 16 * i + 16)
                        dve.wait_ge(tile_done, L * ND + d0 + n + 1)
                        a = acc[:, bass.ds(n, 1), :].rearrange("p a n -> p (a n)")
                        dve.tensor_tensor(gs[:, u, :], dps[:, u, :], gs[:, u, :], ALU.mult).then_inc(tile_free, 1)
                        dve.wait_ge(tile_free, 2 + L * ND + d0 + n + 1)
                        dve.tensor_tensor(a, a, gs[:, u, :], ALU.add).then_inc(merged, 1)

            dve.memset(xsum[:], 0.0).then_inc(sum_zero, 1)
            dve.wait_ge(sum_zero, 1)
            dve.wait_ge(const_set, 3)
            for k in range(KD):
                add_square(k, k % 2)
            with dve.Fori(0, DEPTH) as L:
                db = L * ND
                norm(L, 2 * L, S_AN)
                dve.wait_ge(table_in, 48 * (L + 1))
                dve.wait_ge(idx_in, 80 * (L + 1))
                for t in range(3):
                    dve.tensor_tensor(iqr[:, t, :], iqr[:, t, :], sinT[:], ALU.mult).then_inc(rope_mul, 1)
                    dve.tensor_tensor(iq[:, t, :], iq[:, t, :], cosT[:], ALU.mult).then_inc(rope_mul, 1)
                    dve.wait_ge(rope_mul, L * 26 + 2 * t + 2)
                    dve.tensor_tensor(iq[:, t, :], iq[:, t, :], iqr[:, t, :], ALU.add).then_inc(idx_rope, 1)
                dve.wait_ge(v_turned, 7 * L + 1)
                dve.tensor_scalar(iw[:], tps[:].rearrange("p (t c) -> p t c", c=P)[:, :, MISC_IW:MISC_IW + 4],
                                  IDX_SCALE, None, ALU.mult).then_inc(iw_done, 1)
                dve.wait_ge(iw_done, L + 1)
                dve.wait_ge(x_saved, 16 * (L + 1))
                s = 0
                for n, b in enumerate(IDX_BLOCKS):
                    nk = (b + 1) * P
                    c = bias[:, boff(b):boff(b) + nk]
                    for h in range(4):
                        dve.wait_ge(idx_relu, 4 * NIDX * L + s + 1)
                        if h == 0:
                            dve.tensor_scalar(c, rel[:, s % 2, 0:nk], iw[:, b, h:h + 1], None,
                                              ALU.mult).then_inc(idx_added, 1)
                        else:
                            dve.wait_ge(idx_added, 4 * NIDX * L + s)
                            dve.scalar_tensor_tensor(c, rel[:, s % 2, 0:nk], iw[:, b, h:h + 1], c, ALU.mult,
                                                     ALU.add).then_inc(idx_added, 1)
                        s += 1
                    dve.wait_ge(idx_added, 4 * NIDX * L + s)
                    dve.memset(bias[0:64, boff(b) + nk - CHUNK:boff(b) + nk], FUTURE).then_inc(future_set, 1)
                wait_apart(dve, future_set, NIDX * (L + 1))
                with dve.Fori(0, ROUNDS) as r:
                    for n, b in enumerate(IDX_BLOCKS):
                        dve.max(m8[:, n, :], bias[:, boff(b):boff(b + 1)]).then_inc(top_found, 1)
                    wait_apart(dve, top_found, (ROUNDS * L + r) * NIDX + NIDX)
                    for n, b in enumerate(IDX_BLOCKS):
                        dve.match_replace(bias[:, boff(b):boff(b + 1)], m8[:, n, :], bias[:, boff(b):boff(b + 1)],
                                          TAKEN).then_inc(top_taken, 1)
                    dve.wait_ge(top_taken, (ROUNDS * L + r) * NIDX + NIDX)
                first = boff(IDX_BLOCKS[0])
                dve.tensor_scalar(bias[:, first:boff(NB)], bias[:, first:boff(NB)], TAKEN, HIDDEN, ALU.not_equal,
                                  ALU.mult).then_inc(bias_done, 1)
                dve.memset(bias[:, 0:first], 0.0).then_inc(bias_done, 1)
                dve.wait_ge(bias_done, 4 * L + 2)
                for b in range(IDX_BLOCKS[0]):
                    dve.memset(bias[0:64, boff(b + 1) - CHUNK:boff(b + 1)], HIDDEN).then_inc(bias_done, 1)
                dve.wait_ge(bias_done, 4 * L + 4)

                rope_keys(L, SWA, 2 * L)
                dve.wait_ge(tile_done, db + NPROJ)
                dve.memset(vprev[:], 0.0).then_inc(v_set, 1)
                dve.wait_ge(v_set, 2 * L + 1)
                dve.wait_ge(v_turned, 7 * L + 2)
                ps8 = tps[:].rearrange("p (t c) -> p t c", c=P)
                dve.tensor_copy(vprev[0:64, 1:NB, :], ps8[64:128, 0:NB - 1, :]).then_inc(v_set, 1)
                dve.wait_ge(v_set, 2 * L + 2)
                place_values(0, P, 7 * L + 2)
                rotate_queries(L, SWA, 0, 2 * PAIRS * L)
                add_rotated()
                attentions(L, SWA)
                latents = ((craw, csum, chi, clo, CQ, S_QN, 0, 0), (kraw, csum2, khi, klo, CKV, S_KVN, CQ, 2))
                merge_swa(L, 0)
                for c, (raw, total, hi, lo, kt, g0, k0, s0) in enumerate(latents):
                    dve.wait_ge(lat_first, 2 * L + c + 1)
                    for k in range(1, kt):
                        dve.wait_ge(lat_sq, 3 * L + s0 + k)
                        if c or k > 1:
                            dve.wait_ge(lat_sum, 3 * L + s0 + k - 1)
                        dve.tensor_tensor(total[:], total[:], csq[:], ALU.add).then_inc(lat_sum, 1)
                merge_swa(L, 1)
                merge_swa(L, 2)
                for c in range(2):
                    diagonal(c, lat_diag[c], lat_diagonal, (lat_root, 2 * L + c + 1), lat_rstd, 2 * L + c + 1)
                merge_swa(L, 3)
                merge_swa(L, 4)

                def lat_scale(c, k):
                    raw, total, hi, lo, kt, g0, k0, s0 = latents[c]
                    dve.wait_ge(lat_spread, 2 * L + c + 1)
                    dve.tensor_tensor(raw[:, k, :], raw[:, k, :], (tps, ops)[c][:], ALU.mult).then_inc(lat_scaled, 1)

                def lat_halve(c, k):
                    raw, total, hi, lo, kt, g0, k0, s0 = latents[c]
                    dve.wait_ge(lat_high, 5 * L + k0 + k + 1)
                    dve.scalar_tensor_tensor(lo[:, k, :], raw[:, k, :], sm[:, g0 + k:g0 + k + 1],
                                             hi[:, k, :].bitcast(F32), ALU.mult, ALU.subtract).then_inc(lat_low, 1)

                lat_scale(0, 0)
                lat_scale(0, 1)
                lat_halve(0, 0)
                merge_swa(L, 5)
                lat_scale(0, 2)
                lat_halve(0, 1)
                lat_scale(1, 0)
                merge_swa(L, 6)
                lat_halve(0, 2)
                lat_scale(1, 1)
                lat_halve(1, 0)
                merge_swa(L, 7)
                lat_halve(1, 1)
                dve.wait_ge(lat_in, 80 * (L + 1))
                dve.tensor_tensor(rope_t[0:32, :], kr[32:64, :], ropeM[32:64, :], ALU.mult).then_inc(kr_mul, 1)
                dve.tensor_tensor(kr[0:32, :], kr[0:32, :], ropeM[0:32, :], ALU.mult).then_inc(kr_mul, 1)
                dve.wait_ge(kr_mul, 4 * L + 2)
                dve.tensor_tensor(kb[64:96, :], kr[0:32, :], rope_t[0:32, :], ALU.add).then_inc(kr_mul, 1)
                dve.tensor_tensor(km1[64:96, :], kr[0:32, :], rope_t[0:32, :], ALU.add).then_inc(kr_mul, 1)
                wait_apart(dve, kr_mul, 4 * L + 4)
                mla_queries(L, 0)
                place_values(0, P, 7 * L + 3)
                attentions(L, MLA)
                merge(L, MLA, D_MLA)

                rope_keys(L, DSA, 2 * L + 1)
                place_values(MISC_V, 64, 7 * L + 7)
                rotate_queries(L, DSA, 0, 2 * PAIRS * L + PAIRS)
                add_rotated()
                attentions(L, DSA)
                merge(L, DSA, D_DSA)

                for k in range(KD):
                    dve.wait_ge(sum_high, KD * L + k + 1)
                    dve.tensor_tensor(mlo[:, k, :], acc[:, k, :], mhi[:, k, :].bitcast(F32),
                                      ALU.subtract).then_inc(sum_low, 1)

                def residual(d0, n0, z):
                    dve.wait_ge(summed, n0)
                    dve.memset(xsum[:], 0.0).then_inc(sum_zero, 1)
                    wait_apart(dve, sum_zero, z)
                    with dve.Fori(0, KD // 2) as i:
                        for u in range(2):
                            n = 2 * i + u
                            xn = xt[:, bass.ds(n, 1), :].rearrange("p a n -> p (a n)")
                            dve.wait_ge(tile_done, d0 + n + 1)
                            dve.tensor_tensor(xn, xn, dps[:, u, :], ALU.add).then_inc(tile_free, 1)
                            add_square(n0 + n, u)

                dve.wait_ge(x_in, 16 * (L + 2))
                residual(db + D_OUT, KD + 3 * KD * L, 3 * L + 2)
                norm(L, 2 * L + 1, S_FN)
                wait_apart(dve, norm_low, 2 * KD * (L + 1))
                with dve.Fori(0, GROUPS) as g:
                    dg = db + D_FFN + g * (2 * FG + KD)
                    dve.wait_ge(summed, KD + 3 * KD * L + KD + KD * g)
                    dve.memset(gpad[:, 0:2], 0.0).then_inc(pad_set, 1)
                    wait_apart(dve, pad_set, GROUPS * L + g + 1)
                    with dve.Fori(0, FG) as f:
                        n = NF * L + FG * g + f
                        w = S_CW + FG * g + f
                        dve.wait_ge(ffn_gate, n + 1)
                        dve.wait_ge(tile_free, 2 + dg + 2 * f + 1)
                        dve.scalar_tensor_tensor(conv[:], gpad[:, 1:T + 1], sm[:, bass.ds(w + NF, 1)], conv[:], ALU.mult,
                                                 ALU.add).then_inc(ffn_tap, 1)
                        dve.wait_ge(ffn_tap, n + 1)
                        dve.scalar_tensor_tensor(conv[:], gpad[:, 0:T], sm[:, bass.ds(w, 1)], conv[:], ALU.mult,
                                                 ALU.add).then_inc(ffn_conv, 1)
                        dve.wait_ge(ffn_gelu, n + 1)
                        dve.wait_ge(tile_done, dg + 2 * f + 2)
                        dve.tensor_tensor(act[:], act[:], dps[:, 1, :], ALU.mult).then_inc(tile_free, 1)
                        dve.wait_ge(ffn_high, n + 1)
                        dve.tensor_tensor(alo[:, bass.ds(f, 1), :].rearrange("p a n -> p (a n)"), act[:],
                                          ahi[:, bass.ds(f, 1), :].rearrange("p a n -> p (a n)").bitcast(F32),
                                          ALU.subtract).then_inc(ffn_low, 1)
                    residual(dg + 2 * FG, KD + 3 * KD * L + KD + KD * g, 3 * L + 3 + g)
            rstd(2 * DEPTH)
            for k in range(KD):
                if k >= 2:
                    dve.wait_ge(out_scaled, k - 1)
                dve.tensor_tensor(tt[:, k % 2, :], xt[:, k, :], tps[:], ALU.mult).then_inc(scaled, 1)


def _layout(inp):
    f = {k: np.ascontiguousarray(np.asarray(v, dtype=np.float32)) for k, v in inp.items()}
    arange = np.arange
    seg, at = {}, 0
    for name, w in zip(("cq", "ckv", "kr", "dq", "dk", "dv", "iq", "ik", "iw", "sq", "sk", "sv", "g"),
                       (384, 256, 32, 512, 64, 64, 256, 64, 4, 512, 128, 128, 3072)):
        seg[name] = arange(at, at + w)
        at += w
    pad = lambda n: np.full(n, -1)
    twin = lambda c: [np.concatenate([c[j * 64:(j + 1) * 64], c[(j + 4) * 64:(j + 5) * 64]]) for j in range(4)]
    cols = [seg["iq"], seg["ik"], seg["ik"], seg["kr"], seg["iw"], pad(28), seg["dv"], *twin(seg["sq"]), seg["sk"],
            seg["sv"], seg["cq"], seg["ckv"], seg["dk"], seg["dk"], *twin(seg["dq"]), seg["g"]]
    cols = np.concatenate(cols)
    assert cols.size == NPROJ * P
    swap = np.concatenate([arange(80, 96), arange(64, 80)])

    def tiles(w, kt, width):
        n = w.shape[1] // width
        return w.reshape(kt, P, n, width).transpose(2, 1, 0, 3).reshape(n, P, kt * width)

    def padded(t):
        return np.concatenate([t, np.zeros(t.shape[:2] + (1024 - t.shape[2],), np.float32)], axis=2)

    perm = np.concatenate([np.concatenate([arange(j * 64, (j + 1) * 64), arange((j + 4) * 64, (j + 5) * 64)])
                           for j in range(4)])
    wall = []
    for l in range(DEPTH):
        w = np.concatenate([f["w_in"][l], np.zeros((D, 1), np.float32)], axis=1)[:, cols]
        wall.append(tiles(w, KD, P))

        def branch(wb, order):
            t = tiles(wb[order], PAIRS, P)
            return t.reshape(KD // 2, 2, P, PAIRS * P).transpose(0, 2, 1, 3).reshape(KD // 2, P, 1024)

        uq, ukv = f["mla_w_uq"][l], f["mla_w_ukv"][l]
        qcols = np.concatenate([np.concatenate([h * 96 + arange(96), h * 96 + swap]) for h in range(HEADS)])
        tq = tiles(uq[:, qcols], CQ, 2 * P)
        kvcols = np.concatenate([np.concatenate([h * 128 + arange(64) for h in (2 * j, 2 * j + 1)] +
                                                [h * 128 + 64 + arange(64) for h in (2 * j, 2 * j + 1)])
                                 for j in range(PAIRS)])
        tkv = tiles(ukv[:, kvcols], CKV, 2 * P)
        wall.append(branch(f["w_branch_swa"][l], perm))
        wall.append(np.stack([padded(tq), padded(tkv)], axis=1).reshape(2 * PAIRS, P, 1024))
        wall.append(branch(f["w_branch_mla"][l], arange(512)))
        wall.append(branch(f["w_branch_dsa"][l], perm))
        wall.append(tiles(f["w_out"][l], KD, P))
        tg, tu = tiles(f["w_gate"][l], KD, P), tiles(f["w_up"][l], KD, P)
        for g in range(GROUPS):
            s = slice(g * FG, (g + 1) * FG)
            wall.append(np.stack([tg[s], tu[s]], axis=1).reshape(2 * FG, P, 1024))
            wall.append(tiles(f["w_down"][l][g * FG * P:(g + 1) * FG * P], FG, P))
    wall = np.ascontiguousarray(np.concatenate(wall))
    assert wall.shape == (DEPTH * NW, P, 1024)

    col = lambda a: a.reshape(-1, P).T
    smalls = np.stack([np.concatenate([col(f["attn_norm"][l]), col(f["ffn_norm"][l]), col(f["b_gate"][l]),
                                       col(f["mla_q_norm"][l]), col(f["mla_kv_norm"][l]),
                                       *(col(f["conv_w"][l, c]) for c in range(3)), col(f["conv_b"][l])], axis=1)
                       for l in range(DEPTH)])
    assert smalls.shape == (DEPTH, P, NS)
    sinks = np.zeros((DEPTH, 1, HEADS, 2), np.float32)
    sinks[:, 0, :, 0] = f["swa_sinks"][:DEPTH]

    def angles(dim):
        inv = (1.0 / (np.float32(10000.0) ** (arange(0, dim, 2, dtype=np.float32) / np.float32(dim)))).astype(np.float32)
        ang = (arange(T, dtype=np.float32)[:, None] * inv[None, :]).astype(np.float32)
        return np.cos(ang).T.astype(np.float32), np.sin(ang).T.astype(np.float32)

    c, s = angles(64)
    cr, sr = angles(32)
    cosm = np.concatenate([cr, cr])
    sinm = np.concatenate([-sr, sr])
    tables = np.stack([np.tile(c, (4, 1)), np.concatenate([-s, s, -s, s]), np.concatenate([cosm, sinm, cosm, sinm])])

    sel = np.zeros((2, P), np.float32)
    sel[0, :64] = 1
    sel[1, 64:] = 1
    masks = np.zeros((2, 2 * 256 + P), np.float32)
    for first in range(2):
        m = masks[:, 256 * first:256 * first + 256]
        m[:, 65:128] = HIDDEN
        m[0, 192:256] = HIDDEN
        m[1, 0:64] = HIDDEN
        if first:
            m[0, 0:64] = HIDDEN
    masks[0, 512 + 64:512 + 128] = HIDDEN
    return {
        "x": np.ascontiguousarray(f["x"][0].T.reshape(KD, P, T).transpose(1, 0, 2)),
        "wall": wall, "smalls": np.ascontiguousarray(smalls), "fnorm": np.ascontiguousarray(col(f["final_norm"])),
        "sinks": sinks.reshape(DEPTH, 1, 2 * HEADS), "tables": np.ascontiguousarray(tables),
        "ident": np.eye(P, dtype=np.float32), "masks": np.concatenate([sel, masks], axis=1),
    }


def kernel(**inputs):
    import concourse.bacc as bacc
    from concourse.bass_utils import run_bass_kernel_spmd as run

    nc = bacc.Bacc("TRN2", target_bir_lowering=False, num_devices=1)
    arrays, args = {}, []
    for name, a in _layout(inputs).items():
        arrays[f"in_{name}"] = a
        args.append(nc.dram_tensor(f"in_{name}", a.shape, mybir.dt.from_np(a.dtype), kind="ExternalInput").ap())
    args.append(nc.dram_tensor("out_t", (KD, P, T), F32, kind="ExternalOutput").ap())
    encoder_kernel(nc, *args)
    r = run(nc, [arrays], core_ids=[0])
    got = r.results[0]["out_t"]
    return np.ascontiguousarray(np.asarray(got).reshape(D, T).T)[None]
```

```python
from contextlib import ExitStack

import concourse.bass as bass
from concourse import mybir
import numpy as np

F32 = mybir.dt.float32
F32R = mybir.dt.float32r
BF16 = mybir.dt.bfloat16
ALU = mybir.AluOpType
ACT = mybir.ActivationFunctionType
AX = mybir.AxisListType

P = 128
D = 1024
T = 1024
HALF = 512
DEPTH = 2
KD = D // P
NB = T // P
CHUNK = 64
FF = 2048
NF = FF // P
FG = 8
GROUPS = NF // FG
HEADS = 8
PAIRS = HEADS // 2
TOPK = 256
ROUNDS = TOPK // 8
CQ, CKV = 3, 2
EPS = 1e-6
MLA_SCALE = 96.0 ** -0.5
HEAD_SCALE = 64.0 ** -0.5
IDX_SCALE = 4.0 ** -0.5 * 64.0 ** -0.5
HIDDEN = -1e30
FUTURE = -2e38
TAKEN = -3e38

IQ, IK, MISC, SQ_, SK, SV, LQ, LKV, DK, DQ, GATE = 0, 2, 3, 4, 8, 9, 10, 13, 15, 16, 20
NPROJ = GATE + 3 * KD
MISC_ROPE, MISC_IW, MISC_V = 0, 32, 64

W_PROJ = 0
W_SWA = W_PROJ + NPROJ
W_MLAP = W_SWA + KD // 2
W_MLA = W_MLAP + 2 * PAIRS
W_DSA = W_MLA + KD // 2
W_OUT = W_DSA + KD // 2
W_FFN = W_OUT + KD
NW = W_FFN + GROUPS * (2 * FG + KD)

D_PROJ = 0
D_SWA = D_PROJ + NPROJ
D_MLAP = D_SWA + KD
D_MLA = D_MLAP + 4 * PAIRS
D_DSA = D_MLA + KD
D_OUT = D_DSA + KD
D_FFN = D_OUT + KD
ND = D_FFN + GROUPS * (2 * FG + KD)
assert NW % 2 == 0 and ND % 2 == 0

S_AN, S_FN, S_BG, S_QN, S_KVN, S_CW, S_CB = 0, 8, 16, 40, 43, 45, 93
NS = S_CB + NF

IDX_BLOCKS = range(TOPK // P, NB)
NIDX = len(IDX_BLOCKS)
SWA, MLA, DSA = 0, 1, 2
GATE_OF = (2, 0, 1)
PIECES = 2 * NB
TOGETHER = {SWA: ((0, 1, 2, 3), (4, 5, 6, 7)), MLA: ((7,), (6, 0), (5, 1), (4, 2), (3,))}
TOGETHER[DSA] = TOGETHER[MLA]
WINDOW = 256


def boff(b):
    return P * b * (b + 1) // 2


def width(br, blocks):
    return sum(WINDOW if br == SWA else (b + 1) * P for b in blocks)


def encoder_kernel(nc, x, wall, smalls, fnorm, sinks, tables, ident_h, masks_h, out):
    proj = nc.dram_tensor("proj_scratch", (NPROJ, P, T), F32).ap()
    xs = nc.dram_tensor("x_scratch", (P, KD, T), F32).ap()

    with ExitStack() as ctx:
        def sem(name):
            return ctx.enter_context(nc.semaphore(name))

        def small(name, shape, dt=F32):
            return ctx.enter_context(nc.sbuf_tensor(name, shape, dt))

        ident = small("ident", [P, P])
        ones = small("ones", [P, P])
        masks_all = small("masks_all", [2, P + 2 * 256 + P], BF16)
        selr, masks = masks_all[:, 0:P], masks_all[:, P:]
        sm = small("sm", [P, NS])
        fn = small("fn", [P, KD])
        sk = small("sk", [1, 2 * HEADS])
        eps = small("eps", [P, 1])
        nmax = small("nmax", [P, 16])
        psum_row = small("psum_row", [P, 16])
        pinv = small("pinv", [P, 16])
        root = small("root", [P, 2, 2 * NB])
        iw = small("iw", [P, NB, 4])
        m8 = small("m8", [P, NIDX, 8])

        base = (nc.sbuf_base + 63) // 64 * 64

        def put(name, shape, dt, off):
            assert base + off + 4 * int(np.prod(shape[1:])) <= nc.sbuf_usable_end, name
            return nc.alloc_sbuf_tensor_at(name, shape, dt, offset=base + off)

        K = 1024
        TB = 0
        RING = TB + 16448
        RX = RING + 24 * K
        RH = RX + 32 * K
        RG = RH + 64 * K
        RR = RG + 64 * K

        cosT = put("cosT", [P, T], F32, TB)
        sinT = put("sinT", [P, T], F32, TB + 4 * K)
        ropeM = put("ropeM", [P, T], F32, TB + 8 * K)
        mask32 = put("mask32", [2, P + 2 * 256 + P], F32, TB + 12 * K)
        km1 = put("km1", [P, T], F32, TB + 12 * K)
        tt = put("tt", [P, 2, T], F32, TB)
        diag = put("diag", [P, NB, P], F32, TB + 8 * K)
        gpad = put("gpad", [P, T + 2], F32, TB)
        conv = put("conv", [P, T], F32, TB + 4128)
        act = put("act", [P, T], F32, TB + 4128 + 4 * K)
        sqx = put("sqx", [P, 2, T], F32, TB)

        wraw = put("wraw", [P, 2, 1024], F32, RING)
        whi = put("whi", [P, 2, 1024], F32R, RING + 8 * K)
        wlo = put("wlo", [P, 2, 1024], F32R, RING + 16 * K)

        xt = put("xt", [P, KD, T], F32, RX)
        bias = put("bias", [P, boff(NB)], F32, RX)
        qb = put("qb", [P, T], F32, RX + 18 * K)
        kb = put("kb", [P, T], F32, RX + 22 * K)
        tmpo = put("tmpo", [P, T], F32, RX + 26 * K)

        hhi = put("hhi", [P, KD, T], F32R, RH)
        hlo = put("hlo", [P, KD, T], F32R, RH + 32 * K)
        mhi = put("mhi", [P, KD, T], F32R, RH)
        mlo = put("mlo", [P, KD, T], F32R, RH + 32 * K)
        chi = put("chi", [P, CQ, T], F32R, RH)
        craw = put("craw", [P, CQ, T], F32, RH + 12 * K)
        clo = put("clo", [P, CQ, T], F32R, RH + 12 * K)
        khi = put("khi", [P, CKV, T], F32R, RH + 24 * K)
        kraw = put("kraw", [P, CKV, T], F32, RH + 32 * K)
        klo = put("klo", [P, CKV, T], F32R, RH + 32 * K)
        qst = put("qst", [P, 2, T], F32R, RH + 8 * K)
        dkhi = put("dkhi", [P, T], F32R, RH + 16 * K)
        dklo = put("dklo", [P, T], F32R, RH + 20 * K)
        qs = put("qs", [P, 2, T], F32, RH)
        msc = put("msc", [P, 2, T], F32, RH + 24 * K)
        v = put("v", [P, NB, P], F32, RH + 40 * K)
        pr = put("pr", [P, 2, T], F32, RH + 48 * K)
        vprev = put("vprev", [P, NB, P], F32, RH + 24 * K)
        gs = put("gs", [P, 2, T], F32, RH + 48 * K)
        pt = put("pt", [P, 2, T], F32, RH + 56 * K)
        rope_t = put("rope_t", [P, T], F32, RH + 44 * K)
        vraw = put("vraw", [P, T], F32, RH + 56 * K)
        csq = put("csq", [P, T], F32, RH + 28 * K)
        csum = put("csum", [P, T], F32, RH + 8 * K)
        csum2 = put("csum2", [P, T], F32, RH + 24 * K)

        stage = put("stage", [P, 2, T], F32, RG)
        iq = put("iq", [P, 3, T], F32, RG + 8 * K)
        iqr = put("iqr", [P, 3, T], F32, RG + 20 * K)
        iqs = put("iqs", [P, 4, T], F32R, RG + 44 * K)
        ikhi = put("ikhi", [P, T], F32R, RG + 20 * K)
        iklo = put("iklo", [P, T], F32R, RG + 24 * K)
        rel = put("rel", [P, 2, T], F32, RG + 32 * K)
        qs_swa = put("qs_swa", [P, 2, T], F32, RG + 24 * K)
        vraw_swa = put("vraw_swa", [P, T], F32, RG + 20 * K)
        miscs = put("miscs", [P, T], F32, RG + 40 * K)
        acc = put("acc", [P, KD, T], F32, RG)
        ohi = put("ohi", [P, PAIRS, T], F32R, RG + 32 * K)
        olo = put("olo", [P, PAIRS, T], F32R, RG + 48 * K)
        ahi = put("ahi", [P, FG, T], F32R, RG)
        alo = put("alo", [P, FG, T], F32R, RG + 32 * K)

        xsum = put("xsum", [P, T], F32, RR)
        qm1 = put("qm1", [P, T], F32, RR)
        lat_diag = (qb, qm1)
        kr = tmpo

        dps = ctx.enter_context(nc.psum_tensor("dps", [P, 2, T], F32))
        tps = ctx.enter_context(nc.psum_tensor("tps", [P, T], F32))
        ops = ctx.enter_context(nc.psum_tensor("ops", [P, T], F32))
        ips = [tps, ops]

        const_in = sem("const_in")
        const_set = sem("const_set")
        x_first = [sem(f"x_first{i}") for i in range(4)]
        x_in = sem("x_in")
        small_in = sem("small_in")
        x_saved = sem("x_saved")
        table_in = sem("table_in")
        w_in = [sem("w_in0"), sem("w_in1")]
        w_high = sem("w_high")
        w_low = sem("w_low")
        w_used = sem("w_used")
        tile_done = sem("tile_done")
        tile_free = sem("tile_free")
        sum_zero = sem("sum_zero")
        squared = sem("squared")
        summed = sem("summed")
        stat_done = sem("stat_done")
        root_done = sem("root_done")
        rstd_done = sem("rstd_done")
        diag_done = sem("diag_done")
        spread = sem("spread")
        scaled = sem("scaled")
        norm_high = sem("norm_high")
        norm_low = sem("norm_low")
        stored = [sem("stored0"), sem("stored1")]
        idx_in = sem("idx_in")
        misc_in = sem("misc_in")
        rope_mul = sem("rope_mul")
        idx_rope = sem("idx_rope")
        v_turned = sem("v_turned")
        iw_done = sem("iw_done")
        idx_high = sem("idx_high")
        idx_low = sem("idx_low")
        idx_done = sem("idx_done")
        idx_relu = sem("idx_relu")
        idx_added = sem("idx_added")
        future_set = sem("future_set")
        top_found = sem("top_found")
        top_taken = sem("top_taken")
        bias_done = sem("bias_done")
        k_in = sem("k_in")
        v_in = sem("v_in")
        q_in = sem("q_in")
        k_roped = sem("k_roped")
        v_set = sem("v_set")
        v_done = sem("v_done")
        q_roped = sem("q_roped")
        k_high = sem("k_high")
        k_low = sem("k_low")
        q_high = sem("q_high")
        q_low = sem("q_low")
        logits = sem("logits")
        max_done = sem("max_done")
        exp_done = sem("exp_done")
        turned = sem("turned")
        turned_a = sem("turned_a")
        turned_b = sem("turned_b")
        row_recip = sem("row_recip")
        prob_scaled = sem("prob_scaled")
        out_half = sem("out_half")
        out_high = sem("out_high")
        out_low = sem("out_low")
        gate_in = [sem("gate_in0"), sem("gate_in1")]
        merged = sem("merged")
        sum_high = sem("sum_high")
        sum_low = sem("sum_low")
        lat_in = sem("lat_in")
        lat_first = sem("lat_first")
        lat_sq = sem("lat_sq")
        lat_sum = sem("lat_sum")
        lat_stat = sem("lat_stat")
        lat_root = sem("lat_root")
        lat_rstd = sem("lat_rstd")
        lat_diagonal = sem("lat_diagonal")
        lat_spread = sem("lat_spread")
        lat_scaled = sem("lat_scaled")
        lat_high = sem("lat_high")
        lat_low = sem("lat_low")
        mq_nope = sem("mq_nope")
        mq_mul = sem("mq_mul")
        mq_rope = sem("mq_rope")
        mk_nope = sem("mk_nope")
        kr_mul = sem("kr_mul")
        pad_set = sem("pad_set")
        ffn_gate = sem("ffn_gate")
        ffn_tap = sem("ffn_tap")
        ffn_conv = sem("ffn_conv")
        ffn_gelu = sem("ffn_gelu")
        ffn_high = sem("ffn_high")
        ffn_low = sem("ffn_low")
        out_scaled = sem("out_scaled")
        out_saved = [sem("out_saved0"), sem("out_saved1")]

        def counted(per_pair):
            total = PAIRS * sum(per_pair)

            def at(L, br, j=0):
                return L * total + PAIRS * sum(per_pair[:br]) + j * per_pair[br]
            return at

        unit_at = counted([2 * len(TOGETHER[br]) for br in (SWA, MLA, DSA)])
        wide_at = counted([2 * sum(width(br, u) > HALF for u in TOGETHER[br]) for br in (SWA, MLA, DSA)])
        max_at = counted([2 * len(TOGETHER[SWA]), PIECES, PIECES])
        piece_at = counted([PIECES] * 3)
        half_at = counted([2] * 3)

        def qs_of(br):
            return qs_swa if br == SWA else qs

        def units(br):
            n, piece, out = 0, 0, []
            for hd in range(2):
                for blocks in TOGETHER[br]:
                    col, placed = 0, []
                    for b in blocks:
                        placed.append((b, col))
                        col += WINDOW if br == SWA else (b + 1) * P
                    out.append((n, hd, placed, piece))
                    n, piece = n + 1, piece + len(blocks)
            return out

        def half_order(br):
            return (0, 1) if br == SWA else (1, 0)

        def sink_col(L, j, hd):
            h = j + 4 * hd
            return sk[0:1, bass.ds(2 * h, 2)]

        passed = sem("passed")

        def wait_apart(eng, s, value):
            eng.wait_ge(s, value)
            eng.sem_inc(passed, 1)

        block = ctx.enter_context(nc.Block())

        @block.gpsimd
        def _(pool):
            total = DEPTH * NW

            def split(n, u):
                pool.wait_ge(w_in[u], n * 8 + 16 - 8 * u)
                wait_apart(pool, w_used, n + 1)
                pool.tensor_copy(whi[:, u, :], wraw[:, u, :]).then_inc(w_high, 1)
                pool.wait_ge(w_high, n + 1)
                pool.tensor_tensor(wlo[:, u, :], wraw[:, u, :], whi[:, u, :].bitcast(F32),
                                   ALU.subtract).then_inc(w_low, 1)

            for u in range(2):
                pool.dma_start(wraw[:, u, :], wall[u]).then_inc(w_in[u], 16)
            with pool.Fori(0, total // 2 - 1) as i:
                for u in range(2):
                    split(2 * i + u, u)
                    pool.wait_ge(w_low, 2 * i + u + 1)
                    pool.dma_start(wraw[:, u, :], wall[2 * i + u + 2]).then_inc(w_in[u], 16)
            for u in range(2):
                split(total - 2 + u, u)

        @block.sync
        def _(sp):
            sp.sem_inc(stored[0], 16)
            sp.sem_inc(stored[1], 16)
            for i, s in enumerate(x_first):
                part = slice(i * KD // 4, (i + 1) * KD // 4)
                sp.dma_start(xt[:, part, :], x[:, part, :]).then_inc(s, 16)
            for dst, src in ((ident, ident_h), (mask32, masks_h), (fn, fnorm)):
                sp.dma_start(dst[:], src).then_inc(const_in, 16)

            def store(L, i, u):
                sp.wait_ge(tile_free, 2 + L * ND + i + 1)
                sp.dma_start(proj[i], stage[:, u, :]).then_inc(stored[u], 16)

            def rotated(dst, src, s):
                for r in range(4):
                    o = r ^ 1
                    sp.dma_start(dst[32 * r:32 * r + 32], src[32 * o:32 * o + 32]).then_inc(s, 16)

            def queries(L, br, j, tile):
                qs = qs_of(br)
                sp.dma_start(qs[:, 0, :], proj[tile + j]).then_inc(q_in, 16)
                rotated(qs[:, 1, :], proj[tile + j], q_in)

            def gates(L, br):
                wait_apart(sp, turned, unit_at(L, br, PAIRS))
                with sp.Fori(0, KD // 2) as b:
                    for u in range(2):
                        n = 2 * b + u
                        if br == SWA:
                            sp.wait_ge(tile_free, L * ND + D_SWA + n + 1)
                        else:
                            sp.wait_ge(merged, (2 * L + br - 1) * KD + n + 1)
                        sp.dma_start(gs[:, u, :], proj[GATE + KD * GATE_OF[br] + n]).then_inc(gate_in[u], 16)

            with sp.Fori(0, DEPTH) as L:
                sp.wait_ge(summed, KD + 3 * KD * L)
                sp.dma_start(sm[:], smalls[L]).then_inc(small_in, 16)
                sp.dma_start(sk[:], sinks[L]).then_inc(small_in, 16)
                sp.dma_start(xs, xt[:]).then_inc(x_saved, 16)
                sp.wait_ge(norm_low, 2 * KD * L + KD)
                for n, dst in enumerate((cosT, sinT, ropeM)):
                    sp.dma_start(dst[:], tables[n]).then_inc(table_in, 16)
                for i in range(4):
                    store(L, i, i % 2)
                sp.wait_ge(stored[0], 16 * (NPROJ // 2) * L + 48)
                sp.wait_ge(stored[1], 16 * (NPROJ // 2) * L + 48)
                sp.dma_start(iq[:], proj[0:3].rearrange("t p n -> p t n")).then_inc(idx_in, 16)
                for r in range(4):
                    o = r ^ 1
                    sp.dma_start(iqr[32 * r:32 * r + 32],
                                 proj[0:3, 32 * o:32 * o + 32].rearrange("t p n -> p t n")).then_inc(idx_in, 16)
                sp.dma_start(miscs[:], proj[MISC]).then_inc(misc_in, 16)
                with sp.Fori(2, 6) as b:
                    for u in range(2):
                        store(L, 2 * b + u, u)
                wait_apart(sp, stored[0], 16 * (NPROJ // 2) * L + 16 * 6 + 16)
                wait_apart(sp, stored[1], 16 * (NPROJ // 2) * L + 16 * 6 + 16)
                sp.wait_ge(x_saved, 16 * (L + 1))
                sp.dma_start(kb[:], proj[SK]).then_inc(k_in, 16)
                rotated(tmpo, proj[SK], k_in)
                sp.wait_ge(idx_relu, 4 * NIDX * (L + 1))
                sp.dma_start(vraw_swa[:], proj[SV]).then_inc(v_in, 16)
                queries(L, SWA, 0, SQ_)
                with sp.Fori(6, NPROJ // 2) as b:
                    for u in range(2):
                        store(L, 2 * b + u, u)
                wait_apart(sp, stored[0], 16 * (NPROJ // 2) * (L + 1) + 16)
                wait_apart(sp, stored[1], 16 * (NPROJ // 2) * (L + 1) + 16)
                sp.wait_ge(tile_done, L * ND + NPROJ)
                sp.dma_start(craw[:], proj[LQ:LQ + CQ].rearrange("t p n -> p t n")).then_inc(lat_in, 16)
                sp.dma_start(kraw[:], proj[LKV:LKV + CKV].rearrange("t p n -> p t n")).then_inc(lat_in, 16)
                sp.wait_ge(k_roped, 2 * L + 1)
                sp.dma_start(kr[0:32], proj[MISC, 0:32]).then_inc(lat_in, 16)
                sp.dma_start(kr[32:48], proj[MISC, 16:32]).then_inc(lat_in, 16)
                sp.dma_start(kr[48:64], proj[MISC, 0:16]).then_inc(lat_in, 16)
                with sp.Fori(1, PAIRS) as j:
                    sp.wait_ge(q_roped, 2 * PAIRS * L + j)
                    queries(L, SWA, j, SQ_)
                gates(L, SWA)
                sp.wait_ge(out_low, half_at(L, MLA, PAIRS) + 2)
                sp.dma_start(kb[:], proj[DK]).then_inc(k_in, 16)
                rotated(tmpo, proj[DK], k_in)
                sp.dma_start(vraw[:], proj[MISC]).then_inc(v_in, 16)
                queries(L, DSA, 0, DQ)
                gates(L, MLA)
                with sp.Fori(1, PAIRS) as j:
                    sp.wait_ge(q_roped, 2 * PAIRS * L + PAIRS + j)
                    queries(L, DSA, j, DQ)
                gates(L, DSA)
                sp.wait_ge(out_low, half_at(L, DSA, PAIRS) + 2)
                sp.dma_start(xt[:], xs).then_inc(x_in, 16)
            with sp.Fori(0, KD // 2) as b:
                for u in range(2):
                    k = 2 * b + u
                    sp.wait_ge(out_scaled, k + 1)
                    sp.dma_start(out[k], stage[:, u, :]).then_inc(out_saved[u], 16)
            sp.wait_ge(out_saved[0], 16 * (KD // 2))
            sp.wait_ge(out_saved[1], 16 * (KD // 2))
            sp.wait_ge(x_saved, 16 * DEPTH)

        @block.tensor
        def _(pe):
            pe.sem_inc(w_used, 1)

            def dense(w, u, wcol, kt, hi, lo, free, slot, ready=None, landed=True):
                if landed:
                    pe.wait_ge(w_low, w + 1)
                pe.wait_ge(tile_free, free)
                first = True
                for k in range(kt):
                    if ready is not None:
                        pe.wait_ge(ready[0], ready[1] + k + 1)
                    wh, wl = whi[:, u, wcol(k)], wlo[:, u, wcol(k)]
                    for a, b in ((wh, hi), (wh, lo), (wl, hi)):
                        for h in range(2):
                            mm = pe.matmul(dps[:, slot, h * HALF:(h + 1) * HALF], a,
                                           b[:, k, h * HALF:(h + 1) * HALF],
                                           start=(k == 0 and a is wh and b is hi),
                                           stop=(k == kt - 1 and a is wl))
                            if landed and first:
                                mm.then_inc(w_used, 1)
                            first = False
                mm.then_inc(tile_done, 1)

            def eighth(k):
                return slice(k * P, (k + 1) * P)

            def dense_pair(w, kt, hi, lo, free, ready):
                pe.wait_ge(tile_free, free + 1)
                late = kt - 2

                def step(u, k):
                    wh, wl = whi[:, u, eighth(k)], wlo[:, u, eighth(k)]
                    for a, b in ((wh, hi), (wh, lo), (wl, hi)):
                        for h in range(2):
                            mm = pe.matmul(dps[:, u, h * HALF:(h + 1) * HALF], a, b[:, k, h * HALF:(h + 1) * HALF],
                                           start=(k == 0 and a is wh and b is hi), stop=(k == kt - 1 and a is wl))
                            if u == 1 and k == late and h == 0 and a is wh and b is hi:
                                mm.then_inc(w_used, 1)
                    if k == kt - 1:
                        mm.then_inc(tile_done, 1)

                for k in range(late):
                    pe.wait_ge(ready[0], ready[1] + k + 1)
                    for u in range(2):
                        if k == 0:
                            pe.wait_ge(w_low, w + u + 1)
                        step(u, k)
                for u in range(2):
                    for k in range(late, kt):
                        if u == 0:
                            pe.wait_ge(ready[0], ready[1] + k + 1)
                        step(u, k)

            def statistics(count, src, ps, past_weights=False):
                for t in range(NB):
                    mm = pe.matmul(ps[:, 2 * t:2 * t + 2], src[:, t * P:(t + 1) * P], ones[:, 0:2], start=True, stop=True)
                    if past_weights and t == 0:
                        mm.then_inc(w_used, 1)
                mm.then_inc(count, 1)

            def spread_over_rows(count, src, ps):
                for h in range(2):
                    mm = pe.matmul(ps[:, h * HALF:(h + 1) * HALF], ones[:], src[:, h * HALF:(h + 1) * HALF],
                                   start=True, stop=True)
                mm.then_inc(count, 1)

            def norm(q, sums, past_weights):
                pe.wait_ge(summed, sums)
                statistics(stat_done, xsum, tps, past_weights)
                pe.wait_ge(diag_done, NB * (q + 1))
                spread_over_rows(spread, diag.rearrange("p t c -> p (t c)"), tps)

            def turn_values(src):
                for t in range(NB):
                    mm = pe.transpose(tps[:, t * P:(t + 1) * P], src[:, t * P:(t + 1) * P], ident[:])
                mm.then_inc(v_turned, 1)

            def qk(L, br, j, unit, before=None):
                n, hd, placed, piece = unit
                s = dps[:, n % 2, :]
                halves = (slice(0, 64), slice(64, P))
                q, k = ((qb, qm1)[hd][0:96, :], (kb, km1)[hd][0:96, :]) if br == MLA else (qb[halves[hd], :], kb[halves[hd], :])
                if before is not None:
                    jb, (_, _, placed_b, piece_b) = before
                    if br == DSA:
                        pe.wait_ge(max_done, max_at(L, br, jb) + piece_b + len(placed_b))
                    else:
                        pe.wait_ge(exp_done, piece_at(L, br, jb) + piece_b + len(placed_b))
                if br == DSA and n % (len(units(DSA)) // 2) == 0:
                    pe.wait_ge(q_low, 2 * (PAIRS * L + j) + hd + 1)
                for b, o in placed:
                    qcols = q[:, b * P:(b + 1) * P]
                    if br == SWA:
                        first = WINDOW if b == 0 else 0
                        pe.matmul(s[:, o:o + WINDOW], selr, masks[:, first:first + WINDOW], start=True,
                                  stop=False, skip_group_check=True)
                        pe.matmul(s[:, o:o + 2], ones[0:1, :], sink_col(L, j, hd), start=False, stop=False,
                                  skip_group_check=True)
                        before_ = 64 if b else 0
                        mm = pe.matmul(s[:, o + P - before_:o + WINDOW], qcols, k[:, b * P - before_:(b + 1) * P],
                                       start=False, stop=True, skip_group_check=True)
                    else:
                        end = o + (b + 1) * P
                        c = o
                        while c < end:
                            e = min((c // HALF + 1) * HALF, end)
                            if br == DSA:
                                pe.matmul(s[:, c:e], qst[:, hd, b * P:(b + 1) * P], dkhi[:, c - o:e - o],
                                          start=True, stop=False)
                                mm = pe.matmul(s[:, c:e], qst[halves[hd], hd, b * P:(b + 1) * P],
                                               dklo[halves[hd], c - o:e - o], start=False, stop=True)
                            else:
                                mm = pe.matmul(s[:, c:e], qcols, k[:, c - o:e - o], start=True, stop=True)
                            c = e
                        if br == MLA:
                            mm = pe.matmul(s[:, end - P:end], selr, masks[:, 512:512 + P], start=False,
                                           stop=True, skip_group_check=True)
                mm.then_inc(logits, 1)

            def mla_tile(L, j, i):
                w, d = L * NW + W_MLAP + 2 * j, L * ND + D_MLAP + 4 * j
                part = lambda k: slice(k * 256 + i % 2 * P, k * 256 + i % 2 * P + P)
                if i < 2:
                    dense(w, 0, part, CQ, chi, clo, d + i + 1, i, landed=(i == 0))
                else:
                    dense(w + 1, 1, part, CKV, khi, klo, d + i + 1, i % 2, landed=(i == 2))

            def mla_start(L, j):
                d = L * ND + D_MLAP + 4 * j
                first, second = units(MLA)[:2]
                pe.wait_ge(mq_rope, 8 * L + 2 * j + 2)
                pe.wait_ge(tile_free, d + 3 + 2)
                qk(L, MLA, j, first)
                pe.wait_ge(tile_free, d + 4 + 2)
                turn_values(tmpo)
                qk(L, MLA, j, second)

            def attention(L, br, j, last):
                work = units(br)
                n0, p0 = unit_at(L, br, j), piece_at(L, br, j)

                def evacuated(n):
                    pe.wait_ge(turned_a, n0 + n + 1)
                    if width(br, [b for b, _ in work[n][2]]) > HALF:
                        pe.wait_ge(turned_b, wide_at(L, br, j) + sum(width(br, [b for b, _ in w[2]]) > HALF
                                                                     for w in work[:n + 1]))

                def turn(unit):
                    n, hd, placed, piece = unit
                    if n:
                        evacuated(n - 1)
                    pe.wait_ge(prob_scaled, p0 + piece + len(placed))
                    for t in range(width(br, [b for b, _ in placed]) // P):
                        mm = pe.transpose(tps[:, t * P:(t + 1) * P], pr[:, n % 2, t * P:(t + 1) * P], ident[:])
                    mm.then_inc(turned, 1)

                def pv(unit):
                    n, hd, placed, piece = unit
                    evacuated(n)
                    for b, o in placed:
                        half = b // 4
                        if first_use[half] == (n, b):
                            pe.wait_ge(out_low, half_at(L, br, j) + 1 + half_order(br).index(half))
                        vcol = slice(0, 64) if br == DSA else slice(64 * hd, 64 * hd + 64)
                        out_ = ops[64 * hd:64 * hd + 64, b * P:(b + 1) * P]
                        if br == SWA:
                            pe.matmul(out_, vprev[:, b, vcol], pt[:, n % 2, o:o + P], start=True, stop=False)
                            mm = pe.matmul(out_, v[:, b, vcol], pt[:, n % 2, o + P:o + 2 * P], start=False, stop=True)
                        else:
                            for t in range(b + 1):
                                mm = pe.matmul(out_, v[:, t, vcol], pt[:, n % 2, o + t * P:o + (t + 1) * P],
                                               start=(t == 0), stop=(t == b))
                        if last_use[half] == (n, b):
                            mm.then_inc(out_half, 1)

                first_use, last_use = {}, {}
                for n, hd, placed, piece in work:
                    for b, o in placed:
                        first_use.setdefault(b // 4, (n, b))
                        last_use[b // 4] = (n, b)
                assert all(first_use[h][0] < len(work) // 2 for h in first_use)

                if br == MLA:
                    pe.wait_ge(v_done, 6 * L + 2 + j)
                for n, unit in enumerate(work):
                    ahead = n + 2 - len(work)
                    if ahead < 0:
                        qk(L, br, j, work[n + 2], (j, unit))
                    elif not last and br != MLA:
                        if ahead == 0 and br == SWA:
                            pe.wait_ge(q_roped, 2 * PAIRS * L + j + 2)
                        qk(L, br, j + 1, work[ahead], (j, unit))
                    turn(unit)
                    if ahead >= 0 and not last and br == MLA:
                        mla_tile(L, j + 1, ahead)
                    if n:
                        pv(work[n - 1])
                pv(work[-1])
                if not last and br == MLA:
                    mla_tile(L, j + 1, 2)
                    mla_tile(L, j + 1, 3)
                    mla_start(L, j + 1)

            def attentions(L, br):
                with pe.Fori(0, PAIRS - 1) as j:
                    attention(L, br, j, False)
                attention(L, br, PAIRS - 1, True)

            def merge_part(L, br, w0, d0, i):
                for e in range(2):
                    dense(L * NW + w0 + i, i % 2, lambda k, e=e: slice((e * PAIRS + k) * P, (e * PAIRS + k + 1) * P),
                          PAIRS, ohi, olo, L * ND + d0 + 2 * i + e + 1, e, landed=(e == 0))

            def merge(L, br, w0, d0):
                with pe.Fori(0, KD // 4) as i:
                    for u in range(2):
                        for e in range(2):
                            n = 2 * u + e
                            dense(L * NW + w0 + 2 * i + u, u, lambda k, e=e: slice((e * PAIRS + k) * P, (e * PAIRS + k + 1) * P),
                                  PAIRS, ohi, olo, L * ND + d0 + 4 * i + n + 1, n % 2, landed=(e == 0))

            pe.wait_ge(const_in, 48)
            pe.wait_ge(const_set, 3)
            with pe.Fori(0, DEPTH) as L:
                wb, db = L * NW, L * ND
                norm(2 * L, KD + 3 * KD * L, True)
                dense_pair(wb, KD, hhi, hlo, db + 1, (norm_low, 2 * KD * L))

                def project(lo_, hi_):
                    with pe.Fori(lo_ // 2, hi_ // 2) as i:
                        for u in range(2):
                            dense(wb + 2 * i + u, u, eighth, KD, hhi, hlo, db + 2 * i + u + 1, u)

                project(2, 8)
                pe.wait_ge(misc_in, 16 * (L + 1))
                turn_values(miscs)
                pe.wait_ge(iw_done, L + 1)
                pe.wait_ge(idx_low, 5 * (L + 1))
                s = 0
                for b in IDX_BLOCKS:
                    for h in range(4):
                        if s >= 2:
                            pe.wait_ge(idx_relu, 4 * NIDX * L + s - 1)
                        r = slice(64 * (h % 2), 64 * (h % 2) + 64)
                        nk = (b + 1) * P
                        for c in range(0, nk, HALF):
                            e = min(c + HALF, nk)
                            pe.matmul(ips[s % 2][:, c:e], iqs[:, h, b * P:(b + 1) * P], ikhi[:, c:e], start=True,
                                      stop=False)
                            mm = pe.matmul(ips[s % 2][:, c:e], iqs[r, h, b * P:(b + 1) * P], iklo[r, c:e],
                                           start=False, stop=True)
                        mm.then_inc(idx_done, 1)
                        s += 1
                wait_apart(pe, idx_relu, 4 * NIDX * (L + 1))
                project(8, NPROJ)

                pe.wait_ge(v_in, 32 * L + 16)
                turn_values(vraw_swa)
                pe.wait_ge(k_roped, 2 * L + 1)
                pe.wait_ge(q_roped, 2 * PAIRS * L + 1)
                for n, unit in enumerate(units(SWA)[:2]):
                    pe.wait_ge(tile_free, db + NPROJ + n + 1)
                    qk(L, SWA, 0, unit)
                wait_apart(pe, v_done, 6 * L + 1)
                attentions(L, SWA)
                wait_apart(pe, out_low, half_at(L, SWA, PAIRS) + 2)
                merge_part(L, SWA, W_SWA, D_SWA, 0)
                for c, src in enumerate((csum, csum2)):
                    pe.wait_ge(lat_sum, 3 * L + 2 + c)
                    statistics(lat_stat, src, (tps, ops)[c])
                merge_part(L, SWA, W_SWA, D_SWA, 1)
                for c, src in enumerate(lat_diag):
                    pe.wait_ge(lat_diagonal, 2 * NB * L + NB * (c + 1))
                    spread_over_rows(lat_spread, src, (tps, ops)[c])
                for i in range(2, KD // 2):
                    merge_part(L, SWA, W_SWA, D_SWA, i)
                wait_apart(pe, lat_low, 5 * (L + 1))
                for i in range(4):
                    mla_tile(L, 0, i)
                mla_start(L, 0)
                attentions(L, MLA)
                wait_apart(pe, out_low, half_at(L, MLA, PAIRS) + 2)
                for i in range(KD // 2):
                    merge_part(L, MLA, W_MLA, D_MLA, i)
                    if i == 1:
                        pe.wait_ge(v_in, 32 * L + 32)
                        turn_values(vraw)

                pe.wait_ge(k_low, L + 1)
                for n, unit in enumerate(units(DSA)[:2]):
                    pe.wait_ge(tile_free, db + D_DSA + n + 1)
                    qk(L, DSA, 0, unit)
                wait_apart(pe, v_done, 6 * L + 6)
                attentions(L, DSA)
                wait_apart(pe, out_low, half_at(L, DSA, PAIRS) + 2)
                merge(L, DSA, W_DSA, D_DSA)

                dense(wb + W_OUT, 0, eighth, KD, mhi, mlo, db + D_OUT + 1, 0, ready=(sum_low, KD * L))
                dense(wb + W_OUT + 1, 1, eighth, KD, mhi, mlo, db + D_OUT + 2, 1)
                with pe.Fori(1, KD // 2) as i:
                    for u in range(2):
                        dense(wb + W_OUT + 2 * i + u, u, eighth, KD, mhi, mlo, db + D_OUT + 2 * i + u + 1, u)

                norm(2 * L + 1, KD + 3 * KD * L + KD, True)
                for g in range(GROUPS):
                    wg, dg = wb + W_FFN + g * (2 * FG + KD), db + D_FFN + g * (2 * FG + KD)
                    if g == 0:
                        dense_pair(wg, KD, hhi, hlo, dg + 1, (norm_low, 2 * KD * L + KD))
                    with pe.Fori(1 if g == 0 else 0, FG) as f:
                        for u in range(2):
                            dense(wg + 2 * f + u, u, eighth, KD, hhi, hlo, dg + 2 * f + u + 1, u)
                    wg2, dg2 = wg + 2 * FG, dg + 2 * FG
                    dense(wg2, 0, eighth, FG, ahi, alo, dg2 + 1, 0, ready=(ffn_low, NF * L + FG * g + 1))
                    dense(wg2 + 1, 1, eighth, FG, ahi, alo, dg2 + 2, 1)
                    with pe.Fori(1, KD // 2) as i:
                        for u in range(2):
                            dense(wg2 + 2 * i + u, u, eighth, FG, ahi, alo, dg2 + 2 * i + u + 1, u)
            norm(2 * DEPTH, KD + 3 * KD * DEPTH, False)

        @block.scalar
        def _(act_):
            def norm_root(q):
                act_.wait_ge(stat_done, q + 1)
                act_.activation(root[:, 0, :], tps[:, 0:2 * NB], ACT.Sqrt, bias=eps[:, 0:1], scale=1.0 / D).then_inc(root_done, 1)

            def norm(L, q, g0):
                norm_root(q)
                act_.wait_ge(small_in, 32 * (L + 1))
                for k in range(KD):
                    act_.wait_ge(scaled, KD * q + k + 1)
                    act_.activation(hhi[:, k, :], tt[:, k % 2, :], ACT.Copy, scale=sm[:, g0 + k:g0 + k + 1]).then_inc(norm_high, 1)

            def squares(k, slot):
                act_.activation(sqx[:, slot, :], xt[:, k, :], ACT.Square).then_inc(squared, 1)

            def expo(L, br, j, unit):
                n, hd, placed, piece = unit
                m0 = max_at(L, br, j)
                for i, (b, o) in enumerate(placed):
                    nk = WINDOW if br == SWA else (b + 1) * P
                    c = 4 * (n % 4) + i
                    if br == DSA:
                        act_.wait_ge(max_done, m0 + piece + i + 1)
                    elif i == 0:
                        act_.wait_ge(max_done, m0 + (n + 1 if br == SWA else piece + len(placed)))
                    src, scale = (msc, -1.0) if br == DSA else (dps, 1.0)
                    act_.activation(pr[:, n % 2, o:o + nk], src[:, n % 2, o:o + nk], ACT.Exp,
                                    bias=nmax[:, c:c + 1], scale=scale,
                                    accum_out=psum_row[:, c:c + 1]).then_inc(exp_done, 1)

            def mla_query(L, j, h):
                q = (qb, qm1)[h]
                act_.wait_ge(tile_done, L * ND + D_MLAP + 4 * j + h + 1)
                act_.activation(q[0:64, :], dps[0:64, h, :], ACT.Copy, scale=MLA_SCALE).then_inc(mq_nope, 1)

            def mla_keys(L, j):
                d = L * ND + D_MLAP + 4 * j
                act_.wait_ge(tile_done, d + 3)
                act_.activation(kb[0:64, :], dps[0:64, 0, :], ACT.Copy).then_inc(mk_nope, 1)
                act_.wait_ge(mq_rope, 8 * L + 2 * j + 2)
                act_.activation(km1[0:64, :], dps[64:128, 0, :], ACT.Copy).then_inc(tile_free, 1)
                act_.wait_ge(tile_done, d + 4)
                act_.activation(tmpo[:], dps[:, 1, :], ACT.Copy).then_inc(tile_free, 1)

            def query_high(L, j, hd):
                rows = slice(64 * hd, 64 * hd + 64)
                act_.wait_ge(q_roped, 2 * PAIRS * L + PAIRS + j + 1)
                act_.activation(qst[rows, hd, :], qb[rows, :], ACT.Copy).then_inc(q_high, 1)

            def attention(L, br, j, last):
                work = units(br)
                n0 = unit_at(L, br, j)
                for n, unit in enumerate(work):
                    if n + 1 < len(work):
                        expo(L, br, j, work[n + 1])
                    elif not last and br != MLA:
                        expo(L, br, j + 1, work[0])
                    if not last and br == MLA and n == len(work) - 1:
                        mla_query(L, j + 1, 0)
                    act_.wait_ge(turned, n0 + n + 1)
                    w = min(width(br, [b for b, _ in unit[2]]), HALF)
                    act_.activation(pt[:, n % 2, 0:w], tps[:, 0:w], ACT.Copy).then_inc(turned_a, 1)
                    if not last and br == DSA and n in (4, 9):
                        query_high(L, j + 1, n // 5)
                if not last and br == MLA:
                    mla_query(L, j + 1, 1)
                for i, half in enumerate(half_order(br)):
                    act_.wait_ge(out_half, half_at(L, br, j) + i + 1)
                    c = slice(half * HALF, (half + 1) * HALF)
                    act_.activation(ohi[:, bass.ds(j, 1), c].rearrange("p a n -> p (a n)"), ops[:, c],
                                    ACT.Copy).then_inc(out_high, 1)
                if not last and br == MLA:
                    mla_keys(L, j + 1)
                    expo(L, br, j + 1, work[0])

            def attentions(L, br):
                expo(L, br, 0, units(br)[0])
                with act_.Fori(0, PAIRS - 1) as j:
                    attention(L, br, j, False)
                attention(L, br, PAIRS - 1, True)

            act_.wait_ge(const_set, 2)
            for k in range(KD):
                act_.wait_ge(x_first[4 * k // KD], 16)
                if k >= 2:
                    act_.wait_ge(summed, k - 1)
                squares(k, k % 2)
            with act_.Fori(0, DEPTH) as L:
                db = L * ND
                norm(L, 2 * L, S_AN)

                def features(lo_, hi_):
                    with act_.Fori(lo_ // 2, hi_ // 2) as i:
                        for u in range(2):
                            act_.wait_ge(tile_done, db + 2 * i + u + 1)
                            act_.wait_ge(stored[u], 16 * (NPROJ // 2) * L + 16 * i + 16)
                            act_.activation(stage[:, u, :], dps[:, u, :], ACT.Copy).then_inc(tile_free, 1)

                features(0, 6)
                act_.wait_ge(idx_rope, 3 * (L + 1))
                act_.activation(ikhi[:], iq[:, 2, :], ACT.Copy).then_inc(idx_high, 1)
                for h in range(4):
                    r = slice(64 * (h % 2), 64 * (h % 2) + 64)
                    act_.activation(iqs[r, h, :], iq[r, h // 2, :], ACT.Copy).then_inc(idx_high, 1)
                features(6, 8)
                for s in range(4 * NIDX):
                    nk = (IDX_BLOCKS[s // 4] + 1) * P
                    act_.wait_ge(idx_done, 4 * NIDX * L + s + 1)
                    if s >= 2:
                        act_.wait_ge(idx_added, 4 * NIDX * L + s - 1)
                    act_.activation(rel[:, s % 2, 0:nk], ips[s % 2][:, 0:nk], ACT.Relu).then_inc(idx_relu, 1)
                features(8, GATE)
                with act_.Fori(0, 3 * KD // 2) as i:
                    for u in range(2):
                        act_.wait_ge(tile_done, db + GATE + 2 * i + u + 1)
                        act_.wait_ge(stored[u], 16 * (NPROJ // 2) * L + 16 * (GATE // 2) + 16 * i + 16)
                        act_.activation(stage[:, u, :], dps[:, u, :], ACT.Sigmoid,
                                        bias=sm[:, bass.ds(S_BG + 2 * i + u, 1)]).then_inc(tile_free, 1)
                attentions(L, SWA)
                wait_apart(act_, lat_in, 80 * (L + 1))
                wait_apart(act_, out_half, half_at(L, SWA, PAIRS))
                for c, (raw, total, kt, k0) in enumerate(((craw, csum, CQ, 0), (kraw, csum2, CKV, 2))):
                    act_.activation(total[:], raw[:, 0, :], ACT.Square).then_inc(lat_first, 1)
                    for k in range(1, kt):
                        if c or k > 1:
                            act_.wait_ge(lat_sum, 3 * L + c + k - 1 + (1 if c else 0))
                        act_.activation(csq[:], raw[:, k, :], ACT.Square).then_inc(lat_sq, 1)
                for c, kt in enumerate((CQ, CKV)):
                    act_.wait_ge(lat_stat, 2 * L + c + 1)
                    act_.activation(root[:, c, :], (tps, ops)[c][:, 0:2 * NB], ACT.Sqrt, bias=eps[:, 0:1],
                                    scale=1.0 / (kt * P)).then_inc(lat_root, 1)
                for raw, hi, kt, g0, k0 in ((craw, chi, CQ, S_QN, 0), (kraw, khi, CKV, S_KVN, CQ)):
                    for k in range(kt):
                        act_.wait_ge(lat_scaled, 5 * L + k0 + k + 1)
                        act_.activation(hi[:, k, :], raw[:, k, :], ACT.Copy, scale=sm[:, g0 + k:g0 + k + 1]).then_inc(lat_high, 1)
                for h in range(2):
                    mla_query(L, 0, h)
                mla_keys(L, 0)
                attentions(L, MLA)
                wait_apart(act_, k_roped, 2 * L + 2)
                act_.activation(dkhi[:], kb[:], ACT.Copy).then_inc(k_high, 1)
                for hd in range(2):
                    query_high(L, 0, hd)
                attentions(L, DSA)
                for k in range(KD):
                    act_.wait_ge(merged, 2 + 2 * KD * L + KD + k + 1)
                    act_.activation(mhi[:, k, :], acc[:, k, :], ACT.Copy).then_inc(sum_high, 1)

                def residual(free0, sum0):
                    with act_.Fori(0, KD // 2) as i:
                        for u in range(2):
                            n = 2 * i + u
                            act_.wait_ge(tile_free, free0 + n + 1)
                            act_.wait_ge(summed, sum0 + n - 1)
                            act_.activation(sqx[:, u, :], xt[:, bass.ds(n, 1), :].rearrange("p a n -> p (a n)"),
                                            ACT.Square).then_inc(squared, 1)

                residual(db + D_OUT + 2, KD + 3 * KD * L)
                norm(L, 2 * L + 1, S_FN)
                with act_.Fori(0, GROUPS) as g:
                    dg = db + D_FFN + g * (2 * FG + KD)
                    wait_apart(act_, summed, KD + 3 * KD * L + KD + KD * g)
                    with act_.Fori(0, FG) as f:
                        n = NF * L + FG * g + f
                        act_.wait_ge(tile_done, dg + 2 * f + 1)
                        act_.wait_ge(ffn_low, n + 1)
                        act_.activation(gpad[:, 2:T + 2], dps[:, 0, :], ACT.Copy).then_inc(ffn_gate, 1)
                        act_.activation(conv[:], dps[:, 0, :], ACT.Identity,
                                        bias=sm[:, bass.ds(S_CB + FG * g + f, 1)],
                                        scale=sm[:, bass.ds(S_CW + 2 * NF + FG * g + f, 1)]).then_inc(tile_free, 1)
                        act_.wait_ge(ffn_conv, n + 1)
                        act_.activation(act[:], conv[:], ACT.Gelu).then_inc(ffn_gelu, 1)
                        act_.wait_ge(tile_free, 2 + dg + 2 * f + 2)
                        act_.activation(ahi[:, bass.ds(f, 1), :].rearrange("p a n -> p (a n)"), act[:],
                                        ACT.Copy).then_inc(ffn_high, 1)
                    residual(dg + 2 * FG + 2, KD + 3 * KD * L + KD + KD * g)
            norm_root(2 * DEPTH)
            act_.wait_ge(const_in, 48)
            for k in range(KD):
                act_.wait_ge(scaled, KD * 2 * DEPTH + k + 1)
                if k >= 2:
                    act_.wait_ge(out_saved[k % 2], 16 * (k // 2))
                act_.activation(stage[:, k % 2, :], tt[:, k % 2, :], ACT.Copy, scale=fn[:, k:k + 1]).then_inc(out_scaled, 1)

        @block.vector
        def _(dve):
            dve.sem_inc(tile_free, 2)
            dve.sem_inc(ffn_low, 1)
            dve.sem_inc(merged, 2)
            dve.sem_inc(out_low, 2)
            dve.memset(ones[:], 1.0).then_inc(const_set, 1)
            dve.memset(eps[:], EPS).then_inc(const_set, 1)

            def diagonal(c, dst, count, ready, done, n):
                dve.wait_ge(ready[0], ready[1])
                dve.reciprocal(root[:, c, :], root[:, c, :]).then_inc(done, 1)
                dve.wait_ge(done, n)
                for t in range(NB):
                    dve.tensor_scalar(dst[:, t * P:(t + 1) * P], ident[:], root[:, c, 2 * t:2 * t + 1], None,
                                      ALU.mult).then_inc(count, 1)

            def rstd(q):
                diagonal(0, diag.rearrange("p t c -> p (t c)"), diag_done, (root_done, q + 1), rstd_done, q + 1)
                dve.wait_ge(spread, q + 1)

            def norm(L, q, g0):
                rstd(q)

                def low(k):
                    dve.wait_ge(norm_high, KD * q + k + 1)
                    dve.scalar_tensor_tensor(hlo[:, k, :], tt[:, k % 2, :], sm[:, g0 + k:g0 + k + 1],
                                             hhi[:, k, :].bitcast(F32), ALU.mult, ALU.subtract).then_inc(norm_low, 1)

                dve.wait_ge(small_in, 32 * (L + 1))
                for k in range(KD):
                    if k >= 2:
                        dve.wait_ge(norm_low, KD * q + k - 1)
                    dve.tensor_tensor(tt[:, k % 2, :], xt[:, k, :], tps[:], ALU.mult).then_inc(scaled, 1)
                    if k >= 1:
                        low(k - 1)
                dve.wait_ge(scaled, KD * (q + 1))
                low(KD - 1)

            def add_square(n, slot):
                dve.wait_ge(squared, n + 1)
                if not (isinstance(n, int) and n == 0):
                    dve.wait_ge(summed, n)
                dve.tensor_tensor(xsum[:], xsum[:], sqx[:, slot, :], ALU.add).then_inc(summed, 1)

            def top(L, br, j, unit):
                n, hd, placed, piece = unit
                n0 = unit_at(L, br, j)
                c = 4 * (n % 4)
                if br == SWA:
                    dve.wait_ge(logits, n0 + n + 1)
                    dve.tensor_reduce(nmax[:, c:c + 4], dps[:, n % 2, :].rearrange("p (b k) -> p b k", k=WINDOW),
                                      AX.X, ALU.max, negate=True).then_inc(max_done, 1)
                    return
                if br == DSA:
                    wait_apart(dve, logits, n0 + n + 1)
                else:
                    dve.wait_ge(logits, n0 + n + 1)
                for i, (b, o) in enumerate(placed):
                    nk = (b + 1) * P
                    if br == DSA:
                        dve.tensor_tensor_reduce(out=msc[:, n % 2, o:o + nk], in0=dps[:, n % 2, o:o + nk],
                                                 in1=bias[:, boff(b):boff(b) + nk], scale=-1.0, scalar=3e38,
                                                 op0=ALU.add, op1=ALU.min,
                                                 accum_out=nmax[:, c + i:c + i + 1]).then_inc(max_done, 1)
                    else:
                        dve.tensor_reduce(nmax[:, c + i:c + i + 1], dps[:, n % 2, o:o + nk], AX.X, ALU.max,
                                          negate=True).then_inc(max_done, 1)

            def mla_query(L, j, h):
                q, d, n = (qb, qm1)[h], L * ND + D_MLAP + 4 * j, 8 * L + 2 * j + h
                dve.wait_ge(tile_done, d + h + 1)
                dve.wait_ge(mq_nope, n + 1)
                dve.scalar_tensor_tensor(q[64:96, :], dps[64:96, h, :], MLA_SCALE, ropeM[64:96, :], ALU.mult,
                                         ALU.mult).then_inc(mq_mul, 1)
                dve.wait_ge(mq_mul, n + 1)
                dve.scalar_tensor_tensor(rope_t[64:96, :], dps[96:128, h, :], MLA_SCALE, ropeM[96:128, :],
                                         ALU.mult, ALU.mult).then_inc(tile_free, 1)
                dve.wait_ge(tile_free, 2 + d + h + 1)
                dve.tensor_tensor(q[64:96, :], q[64:96, :], rope_t[64:96, :], ALU.add).then_inc(mq_rope, 1)
                dve.wait_ge(mq_rope, n + 1)

            def divide(L, br, j, unit):
                n, hd, placed, piece = unit
                c = 4 * (n % 4)
                dve.wait_ge(exp_done, piece_at(L, br, j) + piece + len(placed))
                dve.reciprocal(pinv[:, c:c + len(placed)], psum_row[:, c:c + len(placed)]).then_inc(row_recip, 1)
                dve.wait_ge(row_recip, unit_at(L, br, j) + n + 1)
                for i, (b, o) in enumerate(placed):
                    nk = WINDOW if br == SWA else (b + 1) * P
                    dve.tensor_scalar(pr[:, n % 2, o:o + nk], pr[:, n % 2, o:o + nk], pinv[:, c + i:c + i + 1],
                                      None, ALU.mult).then_inc(prob_scaled, 1)

            def attention(L, br, j, last):
                work = units(br)
                n0 = unit_at(L, br, j)
                number = 2 * PAIRS * L + (PAIRS if br == DSA else 0) + j + 1

                def evacuate(unit):
                    n, hd, placed, piece = unit
                    w = width(br, [b for b, _ in placed])
                    if w > HALF:
                        dve.wait_ge(turned, n0 + n + 1)
                        dve.tensor_copy(pt[:, n % 2, HALF:w], tps[:, HALF:w]).then_inc(turned_b, 1)

                def low(i):
                    half = half_order(br)[i]
                    dve.wait_ge(out_high, half_at(L, br, j) + i + 1)
                    c = slice(half * HALF, (half + 1) * HALF)
                    hi = ohi[:, bass.ds(j, 1), c].rearrange("p a n -> p (a n)").bitcast(F32)
                    dve.tensor_tensor(olo[:, bass.ds(j, 1), c].rearrange("p a n -> p (a n)"), ops[:, c], hi,
                                      ALU.subtract).then_inc(out_low, 1)

                end = len(work)
                for n, unit in enumerate(work):
                    if n:
                        divide(L, br, j, unit)
                    if n + 2 < end:
                        top(L, br, j, work[n + 2])
                    elif not last and br != MLA:
                        top(L, br, j + 1, work[n + 2 - end])
                    if not last and br == MLA and n == end - 1:
                        mla_query(L, j + 1, 0)
                    evacuate(unit)
                    if not last and br == SWA and n in (0, 1):
                        rotate_half(L, br, j + 1, number, n)
                    if not last and br == SWA and n == 1:
                        add_rotated(br)
                    if not last and br == DSA:
                        if n in (1, 2):
                            rotate_half(L, br, j + 1, number, n - 1)
                        elif n == 3:
                            add_rotated(br)
                        elif n == 5:
                            query_low(L, j + 1, 0)
                if not last and br == MLA:
                    mla_query(L, j + 1, 1)
                low(0)
                if not last and br != MLA:
                    divide(L, br, j + 1, work[0])
                low(1)
                if not last and br == DSA:
                    query_low(L, j + 1, 1)
                if not last and br == MLA:
                    top(L, br, j + 1, work[0])
                    place_values(0, P, 7 * L + 3 + j + 1)
                    top(L, br, j + 1, work[1])
                    divide(L, br, j + 1, work[0])

            def attentions(L, br):
                with dve.Fori(0, PAIRS - 1) as j:
                    attention(L, br, j, False)
                attention(L, br, PAIRS - 1, True)

            def rotate_half(L, br, j, n, part):
                qs = qs_of(br)
                t = 1 - part
                if part == 0:
                    dve.wait_ge(q_in, 80 * (n + 1))
                dve.scalar_tensor_tensor(qs[:, t, :], qs[:, t, :], HEAD_SCALE, (cosT, sinT)[t][:], ALU.mult,
                                         ALU.mult).then_inc(rope_mul, 1)
                if part == 1:
                    dve.wait_ge(rope_mul, rope_at(L, br) + 2 * j + 2)

            def query_low(L, j, hd):
                rows, others = slice(64 * hd, 64 * hd + 64), slice(64 - 64 * hd, 128 - 64 * hd)
                dve.wait_ge(q_high, 2 * (PAIRS * L + j) + hd + 1)
                dve.tensor_tensor(qst[others, hd, :], qb[rows, :], qst[rows, hd, :].bitcast(F32),
                                  ALU.subtract).then_inc(q_low, 1)

            def add_rotated(br):
                qs = qs_of(br)
                dve.tensor_tensor(qb[:], qs[:, 0, :], qs[:, 1, :], ALU.add).then_inc(q_roped, 1)

            def rope_at(L, br):
                return L * 26 + 6 + (0 if br == SWA else 10) + 2

            def rope_keys(L, br, n):
                dve.wait_ge(k_in, 80 * (n + 1))
                dve.tensor_tensor(tmpo[:], tmpo[:], sinT[:], ALU.mult).then_inc(rope_mul, 1)
                dve.tensor_tensor(kb[:], kb[:], cosT[:], ALU.mult).then_inc(rope_mul, 1)
                dve.wait_ge(rope_mul, rope_at(L, br))
                dve.tensor_tensor(kb[:], kb[:], tmpo[:], ALU.add).then_inc(k_roped, 1)

            def place_values(col, cols, turned_):
                dve.wait_ge(v_turned, turned_)
                ps8 = tps[:].rearrange("p (t c) -> p t c", c=P)
                dve.tensor_copy(v[:, :, 0:cols], ps8[:, :, col:col + cols]).then_inc(v_done, 1)

            def merge_swa(L, n):
                u = n % 2
                dve.wait_ge(gate_in[u], 16 * (KD // 2) * (3 * L + SWA) + 16 * (n // 2) + 16)
                dve.wait_ge(tile_done, L * ND + D_SWA + n + 1)
                dve.tensor_tensor(acc[:, n, :], dps[:, u, :], gs[:, u, :], ALU.mult).then_inc(tile_free, 1)

            def merge_tile(L, br, d0, n):
                u = n % 2
                dve.wait_ge(gate_in[u], 16 * (KD // 2) * (3 * L + br) + 16 * (n // 2) + 16)
                dve.wait_ge(tile_done, L * ND + d0 + n + 1)
                dve.tensor_tensor(gs[:, u, :], dps[:, u, :], gs[:, u, :], ALU.mult).then_inc(tile_free, 1)
                dve.wait_ge(tile_free, 2 + L * ND + d0 + n + 1)
                dve.tensor_tensor(acc[:, n, :], acc[:, n, :], gs[:, u, :], ALU.add).then_inc(merged, 1)

            dve.memset(xsum[:], 0.0).then_inc(sum_zero, 1)
            dve.wait_ge(sum_zero, 1)
            for k in range(KD):
                add_square(k, k % 2)
            dve.wait_ge(const_in, 48)
            dve.tensor_copy(masks_all[:], mask32[:]).then_inc(const_set, 1)
            dve.wait_ge(const_set, 3)
            with dve.Fori(0, DEPTH) as L:
                db = L * ND
                norm(L, 2 * L, S_AN)
                dve.wait_ge(table_in, 48 * (L + 1))
                dve.wait_ge(idx_in, 80 * (L + 1))
                for t in range(3):
                    dve.tensor_tensor(iqr[:, t, :], iqr[:, t, :], sinT[:], ALU.mult).then_inc(rope_mul, 1)
                    dve.tensor_tensor(iq[:, t, :], iq[:, t, :], cosT[:], ALU.mult).then_inc(rope_mul, 1)
                    dve.wait_ge(rope_mul, L * 26 + 2 * t + 2)
                    dve.tensor_tensor(iq[:, t, :], iq[:, t, :], iqr[:, t, :], ALU.add).then_inc(idx_rope, 1)
                dve.wait_ge(idx_high, 5 * L + 1)
                dve.tensor_tensor(iklo[:], iq[:, 2, :], ikhi[:].bitcast(F32), ALU.subtract).then_inc(idx_low, 1)
                for h in range(4):
                    r, others = slice(64 * (h % 2), 64 * (h % 2) + 64), slice(64 - 64 * (h % 2), P - 64 * (h % 2))
                    dve.wait_ge(idx_high, 5 * L + 2 + h)
                    dve.tensor_tensor(iqs[others, h, :], iq[r, h // 2, :], iqs[r, h, :].bitcast(F32),
                                      ALU.subtract).then_inc(idx_low, 1)
                dve.wait_ge(v_turned, 7 * L + 1)
                dve.tensor_scalar(iw[:], tps[:].rearrange("p (t c) -> p t c", c=P)[:, :, MISC_IW:MISC_IW + 4],
                                  IDX_SCALE, None, ALU.mult).then_inc(iw_done, 1)
                dve.wait_ge(iw_done, L + 1)
                dve.wait_ge(x_saved, 16 * (L + 1))
                s = 0
                for n, b in enumerate(IDX_BLOCKS):
                    nk = (b + 1) * P
                    c = bias[:, boff(b):boff(b) + nk]
                    for h in range(4):
                        dve.wait_ge(idx_relu, 4 * NIDX * L + s + 1)
                        if h == 0:
                            dve.tensor_scalar(c, rel[:, s % 2, 0:nk], iw[:, b, h:h + 1], None,
                                              ALU.mult).then_inc(idx_added, 1)
                        else:
                            dve.wait_ge(idx_added, 4 * NIDX * L + s)
                            dve.scalar_tensor_tensor(c, rel[:, s % 2, 0:nk], iw[:, b, h:h + 1], c, ALU.mult,
                                                     ALU.add).then_inc(idx_added, 1)
                        s += 1
                    dve.wait_ge(idx_added, 4 * NIDX * L + s)
                    dve.memset(bias[0:64, boff(b) + nk - CHUNK:boff(b) + nk], FUTURE).then_inc(future_set, 1)
                wait_apart(dve, future_set, NIDX * (L + 1))
                with dve.Fori(0, ROUNDS) as r:
                    for n, b in enumerate(IDX_BLOCKS):
                        dve.max(m8[:, n, :], bias[:, boff(b):boff(b + 1)]).then_inc(top_found, 1)
                    wait_apart(dve, top_found, (ROUNDS * L + r) * NIDX + NIDX)
                    for n, b in enumerate(IDX_BLOCKS):
                        dve.match_replace(bias[:, boff(b):boff(b + 1)], m8[:, n, :], bias[:, boff(b):boff(b + 1)],
                                          TAKEN).then_inc(top_taken, 1)
                    dve.wait_ge(top_taken, (ROUNDS * L + r) * NIDX + NIDX)
                first = boff(IDX_BLOCKS[0])
                dve.tensor_scalar(bias[:, first:boff(NB)], bias[:, first:boff(NB)], TAKEN, HIDDEN, ALU.not_equal,
                                  ALU.mult).then_inc(bias_done, 1)
                dve.memset(bias[:, 0:first], 0.0).then_inc(bias_done, 1)
                dve.wait_ge(bias_done, 4 * L + 2)
                for b in range(IDX_BLOCKS[0]):
                    dve.memset(bias[0:64, boff(b + 1) - CHUNK:boff(b + 1)], HIDDEN).then_inc(bias_done, 1)
                dve.wait_ge(bias_done, 4 * L + 4)

                rope_keys(L, SWA, 2 * L)
                for part in range(2):
                    rotate_half(L, SWA, 0, 2 * PAIRS * L, part)
                add_rotated(SWA)
                ps8 = tps[:].rearrange("p (t c) -> p t c", c=P)
                dve.wait_ge(tile_done, db + NPROJ)
                dve.memset(vprev[0:64], 0.0).then_inc(v_set, 1)
                dve.memset(vprev[64:128, 0, :], 0.0).then_inc(v_set, 1)
                dve.wait_ge(v_turned, 7 * L + 1 + 1)
                dve.tensor_copy(vprev[64:128, 1:NB, :], ps8[64:128, 0:NB - 1, :]).then_inc(v_set, 1)
                dve.wait_ge(v_set, 3 * L + 3)
                place_values(0, P, 7 * L + 2)
                for unit in units(SWA)[:2]:
                    top(L, SWA, 0, unit)
                divide(L, SWA, 0, units(SWA)[0])
                attentions(L, SWA)
                latents = ((craw, csum, chi, clo, CQ, S_QN, 0, 0), (kraw, csum2, khi, klo, CKV, S_KVN, CQ, 2))
                for c, (raw, total, hi, lo, kt, g0, k0, s0) in enumerate(latents):
                    dve.wait_ge(lat_first, 2 * L + c + 1)
                    for k in range(1, kt):
                        dve.wait_ge(lat_sq, 3 * L + s0 + k)
                        if c or k > 1:
                            dve.wait_ge(lat_sum, 3 * L + s0 + k - 1)
                        dve.tensor_tensor(total[:], total[:], csq[:], ALU.add).then_inc(lat_sum, 1)
                merge_swa(L, 0)
                merge_swa(L, 1)
                for c in range(2):
                    diagonal(c, lat_diag[c], lat_diagonal, (lat_root, 2 * L + c + 1), lat_rstd, 2 * L + c + 1)
                merge_swa(L, 2)
                merge_swa(L, 3)

                def lat_scale(c, k):
                    raw, total, hi, lo, kt, g0, k0, s0 = latents[c]
                    dve.wait_ge(lat_spread, 2 * L + c + 1)
                    dve.tensor_tensor(raw[:, k, :], raw[:, k, :], (tps, ops)[c][:], ALU.mult).then_inc(lat_scaled, 1)

                def lat_halve(c, k):
                    raw, total, hi, lo, kt, g0, k0, s0 = latents[c]
                    dve.wait_ge(lat_high, 5 * L + k0 + k + 1)
                    dve.scalar_tensor_tensor(lo[:, k, :], raw[:, k, :], sm[:, g0 + k:g0 + k + 1],
                                             hi[:, k, :].bitcast(F32), ALU.mult, ALU.subtract).then_inc(lat_low, 1)

                lat_scale(0, 0)
                lat_scale(0, 1)
                lat_halve(0, 0)
                merge_swa(L, 4)
                lat_scale(0, 2)
                lat_halve(0, 1)
                lat_scale(1, 0)
                merge_swa(L, 5)
                lat_halve(0, 2)
                lat_scale(1, 1)
                lat_halve(1, 0)
                merge_swa(L, 6)
                lat_halve(1, 1)
                dve.wait_ge(lat_in, 80 * (L + 1))
                dve.tensor_tensor(rope_t[0:32, :], kr[32:64, :], ropeM[32:64, :], ALU.mult).then_inc(kr_mul, 1)
                dve.tensor_tensor(kr[0:32, :], kr[0:32, :], ropeM[0:32, :], ALU.mult).then_inc(kr_mul, 1)
                merge_swa(L, 7)
                dve.wait_ge(kr_mul, 4 * L + 2)
                dve.tensor_tensor(kb[64:96, :], kr[0:32, :], rope_t[0:32, :], ALU.add).then_inc(kr_mul, 1)
                dve.tensor_tensor(km1[64:96, :], kr[0:32, :], rope_t[0:32, :], ALU.add).then_inc(kr_mul, 1)
                wait_apart(dve, kr_mul, 4 * L + 4)
                for h in range(2):
                    mla_query(L, 0, h)
                top(L, MLA, 0, units(MLA)[0])
                place_values(0, P, 7 * L + 3)
                top(L, MLA, 0, units(MLA)[1])
                divide(L, MLA, 0, units(MLA)[0])
                attentions(L, MLA)
                for n in range(4):
                    merge_tile(L, MLA, D_MLA, n)
                rope_keys(L, DSA, 2 * L + 1)
                merge_tile(L, MLA, D_MLA, 4)
                place_values(MISC_V, 64, 7 * L + 7)
                for part in range(2):
                    rotate_half(L, DSA, 0, 2 * PAIRS * L + PAIRS, part)
                merge_tile(L, MLA, D_MLA, 5)
                add_rotated(DSA)
                dve.wait_ge(k_high, L + 1)
                dve.tensor_tensor(dklo[:], kb[:], dkhi[:].bitcast(F32), ALU.subtract).then_inc(k_low, 1)
                merge_tile(L, MLA, D_MLA, 6)
                for hd in range(2):
                    query_low(L, 0, hd)
                merge_tile(L, MLA, D_MLA, 7)

                for unit in units(DSA)[:2]:
                    top(L, DSA, 0, unit)
                divide(L, DSA, 0, units(DSA)[0])
                attentions(L, DSA)
                def merged_low(k):
                    dve.wait_ge(sum_high, KD * L + k + 1)
                    dve.tensor_tensor(mlo[:, k, :], acc[:, k, :], mhi[:, k, :].bitcast(F32),
                                      ALU.subtract).then_inc(sum_low, 1)

                for n in range(KD):
                    merge_tile(L, DSA, D_DSA, n)
                    if 1 <= n <= 4:
                        merged_low(n - 1)
                dve.wait_ge(merged, 2 + 2 * KD * (L + 1))
                for k in range(4, KD):
                    merged_low(k)

                def residual(d0, n0, z):
                    dve.wait_ge(summed, n0)
                    dve.memset(xsum[:], 0.0).then_inc(sum_zero, 1)
                    wait_apart(dve, sum_zero, z)
                    with dve.Fori(0, KD // 2) as i:
                        for u in range(2):
                            n = 2 * i + u
                            xn = xt[:, bass.ds(n, 1), :].rearrange("p a n -> p (a n)")
                            dve.wait_ge(tile_done, d0 + n + 1)
                            dve.tensor_tensor(xn, xn, dps[:, u, :], ALU.add).then_inc(tile_free, 1)
                            add_square(n0 + n, u)

                dve.wait_ge(x_in, 16 * (L + 1))
                residual(db + D_OUT, KD + 3 * KD * L, 3 * L + 2)
                norm(L, 2 * L + 1, S_FN)
                wait_apart(dve, norm_low, 2 * KD * (L + 1))
                with dve.Fori(0, GROUPS) as g:
                    dg = db + D_FFN + g * (2 * FG + KD)
                    dve.wait_ge(summed, KD + 3 * KD * L + KD + KD * g)
                    dve.memset(gpad[:, 0:2], 0.0).then_inc(pad_set, 1)
                    wait_apart(dve, pad_set, GROUPS * L + g + 1)
                    with dve.Fori(0, FG) as f:
                        n = NF * L + FG * g + f
                        w = S_CW + FG * g + f
                        dve.wait_ge(ffn_gate, n + 1)
                        dve.wait_ge(tile_free, 2 + dg + 2 * f + 1)
                        dve.scalar_tensor_tensor(conv[:], gpad[:, 1:T + 1], sm[:, bass.ds(w + NF, 1)], conv[:], ALU.mult,
                                                 ALU.add).then_inc(ffn_tap, 1)
                        dve.wait_ge(ffn_tap, n + 1)
                        dve.scalar_tensor_tensor(conv[:], gpad[:, 0:T], sm[:, bass.ds(w, 1)], conv[:], ALU.mult,
                                                 ALU.add).then_inc(ffn_conv, 1)
                        dve.wait_ge(ffn_gelu, n + 1)
                        dve.wait_ge(tile_done, dg + 2 * f + 2)
                        dve.tensor_tensor(act[:], act[:], dps[:, 1, :], ALU.mult).then_inc(tile_free, 1)
                        dve.wait_ge(ffn_high, n + 1)
                        dve.tensor_tensor(alo[:, bass.ds(f, 1), :].rearrange("p a n -> p (a n)"), act[:],
                                          ahi[:, bass.ds(f, 1), :].rearrange("p a n -> p (a n)").bitcast(F32),
                                          ALU.subtract).then_inc(ffn_low, 1)
                    residual(dg + 2 * FG, KD + 3 * KD * L + KD + KD * g, 3 * L + 3 + g)
            rstd(2 * DEPTH)
            for k in range(KD):
                if k >= 2:
                    dve.wait_ge(out_scaled, k - 1)
                dve.tensor_tensor(tt[:, k % 2, :], xt[:, k, :], tps[:], ALU.mult).then_inc(scaled, 1)


def _layout(inp):
    f = {k: np.ascontiguousarray(np.asarray(v, dtype=np.float32)) for k, v in inp.items()}
    arange = np.arange
    seg, at = {}, 0
    for name, w in zip(("cq", "ckv", "kr", "dq", "dk", "dv", "iq", "ik", "iw", "sq", "sk", "sv", "g"),
                       (384, 256, 32, 512, 64, 64, 256, 64, 4, 512, 128, 128, 3072)):
        seg[name] = arange(at, at + w)
        at += w
    pad = lambda n: np.full(n, -1)
    twin = lambda c: [np.concatenate([c[j * 64:(j + 1) * 64], c[(j + 4) * 64:(j + 5) * 64]]) for j in range(4)]
    cols = [seg["iq"], seg["ik"], seg["ik"], seg["kr"], seg["iw"], pad(28), seg["dv"], *twin(seg["sq"]), seg["sk"],
            seg["sv"], seg["cq"], seg["ckv"], seg["dk"], seg["dk"], *twin(seg["dq"]), seg["g"]]
    cols = np.concatenate(cols)
    assert cols.size == NPROJ * P
    swap = np.concatenate([arange(80, 96), arange(64, 80)])

    def tiles(w, kt, width):
        n = w.shape[1] // width
        return w.reshape(kt, P, n, width).transpose(2, 1, 0, 3).reshape(n, P, kt * width)

    def padded(t):
        return np.concatenate([t, np.zeros(t.shape[:2] + (1024 - t.shape[2],), np.float32)], axis=2)

    perm = np.concatenate([np.concatenate([arange(j * 64, (j + 1) * 64), arange((j + 4) * 64, (j + 5) * 64)])
                           for j in range(4)])
    wall = []
    for l in range(DEPTH):
        w = np.concatenate([f["w_in"][l], np.zeros((D, 1), np.float32)], axis=1)[:, cols]
        wall.append(tiles(w, KD, P))

        def branch(wb, order):
            t = tiles(wb[order], PAIRS, P)
            return t.reshape(KD // 2, 2, P, PAIRS * P).transpose(0, 2, 1, 3).reshape(KD // 2, P, 1024)

        uq, ukv = f["mla_w_uq"][l], f["mla_w_ukv"][l]
        qcols = np.concatenate([np.concatenate([h * 96 + arange(96), h * 96 + swap]) for h in range(HEADS)])
        tq = tiles(uq[:, qcols], CQ, 2 * P)
        kvcols = np.concatenate([np.concatenate([h * 128 + arange(64) for h in (2 * j, 2 * j + 1)] +
                                                [h * 128 + 64 + arange(64) for h in (2 * j, 2 * j + 1)])
                                 for j in range(PAIRS)])
        tkv = tiles(ukv[:, kvcols], CKV, 2 * P)
        wall.append(branch(f["w_branch_swa"][l], perm))
        wall.append(np.stack([padded(tq), padded(tkv)], axis=1).reshape(2 * PAIRS, P, 1024))
        wall.append(branch(f["w_branch_mla"][l], arange(512)))
        wall.append(branch(f["w_branch_dsa"][l], perm))
        wall.append(tiles(f["w_out"][l], KD, P))
        tg, tu = tiles(f["w_gate"][l], KD, P), tiles(f["w_up"][l], KD, P)
        for g in range(GROUPS):
            s = slice(g * FG, (g + 1) * FG)
            wall.append(np.stack([tg[s], tu[s]], axis=1).reshape(2 * FG, P, 1024))
            wall.append(tiles(f["w_down"][l][g * FG * P:(g + 1) * FG * P], FG, P))
    wall = np.ascontiguousarray(np.concatenate(wall))
    assert wall.shape == (DEPTH * NW, P, 1024)

    col = lambda a: a.reshape(-1, P).T
    smalls = np.stack([np.concatenate([col(f["attn_norm"][l]), col(f["ffn_norm"][l]), col(f["b_gate"][l]),
                                       col(f["mla_q_norm"][l]), col(f["mla_kv_norm"][l]),
                                       *(col(f["conv_w"][l, c]) for c in range(3)), col(f["conv_b"][l])], axis=1)
                       for l in range(DEPTH)])
    assert smalls.shape == (DEPTH, P, NS)
    sinks = np.zeros((DEPTH, 1, HEADS, 2), np.float32)
    sinks[:, 0, :, 0] = f["swa_sinks"][:DEPTH]

    def angles(dim):
        inv = (1.0 / (np.float32(10000.0) ** (arange(0, dim, 2, dtype=np.float32) / np.float32(dim)))).astype(np.float32)
        ang = (arange(T, dtype=np.float32)[:, None] * inv[None, :]).astype(np.float32)
        return np.cos(ang).T.astype(np.float32), np.sin(ang).T.astype(np.float32)

    c, s = angles(64)
    cr, sr = angles(32)
    cosm = np.concatenate([cr, cr])
    sinm = np.concatenate([-sr, sr])
    tables = np.stack([np.tile(c, (4, 1)), np.concatenate([-s, s, -s, s]), np.concatenate([cosm, sinm, cosm, sinm])])

    sel = np.zeros((2, P), np.float32)
    sel[0, :64] = 1
    sel[1, 64:] = 1
    masks = np.zeros((2, 2 * 256 + P), np.float32)
    for first in range(2):
        m = masks[:, 256 * first:256 * first + 256]
        m[:, 1:64] = HIDDEN
        m[0, 192:256] = HIDDEN
        m[1, 64:128] = HIDDEN
        if first:
            m[0, 64:128] = HIDDEN
    masks[0, 512 + 64:512 + 128] = HIDDEN
    return {
        "x": np.ascontiguousarray(f["x"][0].T.reshape(KD, P, T).transpose(1, 0, 2)),
        "wall": wall, "smalls": np.ascontiguousarray(smalls), "fnorm": np.ascontiguousarray(col(f["final_norm"])),
        "sinks": sinks.reshape(DEPTH, 1, 2 * HEADS), "tables": np.ascontiguousarray(tables),
        "ident": np.eye(P, dtype=np.float32), "masks": np.concatenate([sel, masks], axis=1),
    }


def kernel(**inputs):
    import concourse.bacc as bacc
    from concourse.bass_utils import run_bass_kernel_spmd as run

    nc = bacc.Bacc("TRN2", target_bir_lowering=False, num_devices=1)
    arrays, args = {}, []
    for name, a in _layout(inputs).items():
        arrays[f"in_{name}"] = a
        args.append(nc.dram_tensor(f"in_{name}", a.shape, mybir.dt.from_np(a.dtype), kind="ExternalInput").ap())
    args.append(nc.dram_tensor("out_t", (KD, P, T), F32, kind="ExternalOutput").ap())
    encoder_kernel(nc, *args)
    r = run(nc, [arrays], core_ids=[0])
    got = r.results[0]["out_t"]
    return np.ascontiguousarray(np.asarray(got).reshape(D, T).T)[None]
```
